# Optimizing a Trainium2 kernel written in Bass

```python
import jax, jax.numpy as jnp
from jax import lax
import numpy as np
import jax
import jax.numpy as jnp

D_MODEL = 1024
BATCH = 1
SEQ = 1024
DEPTH = 2

HEAD_DIM = 64
ROPE_THETA = 500000.0
ROT_DIM = HEAD_DIM // 4
GRID_W = 64
EPS = 1e-6
NEG_INF = -1e30
QBLK = 128

A_HEADS = 3 * D_MODEL // (4 * HEAD_DIM)
A_WIDTH = A_HEADS * HEAD_DIM
A_PATTERNS = ((128, 1), (512, 4), (2048, 16))
B_GROUP_DIM = 64
B_GROUPS = D_MODEL // (4 * B_GROUP_DIM)
B_WIDTH = B_GROUPS * B_GROUP_DIM
B_CHUNK = 128
EVEN_IN = 3 * A_WIDTH + 2 * B_WIDTH
C_HEADS = D_MODEL // (2 * HEAD_DIM)
C_Q_RANK = D_MODEL // 4
C_KV_RANK = D_MODEL // 8
C_NOPE = HEAD_DIM
C_ROPE = HEAD_DIM // 2
C_V = HEAD_DIM
D_HEADS = D_MODEL // (2 * HEAD_DIM)
D_KV_HEADS = 2
D_GROUP = D_HEADS // D_KV_HEADS
D_THETA = 10000.0
ODD_IN = C_Q_RANK + C_KV_RANK + C_ROPE + (D_HEADS + 2 * D_KV_HEADS) * HEAD_DIM
N_EXPERTS = 16
EC_FACTOR = 2
EXPERT_FF = 512


def rmsnorm(x, g):
    xf = x.astype(jnp.float32)
    y = xf * lax.rsqrt(jnp.mean(xf * xf, axis=-1, keepdims=True) + EPS)
    return (y * g.astype(jnp.float32)).astype(x.dtype)

def rope(x, pos, theta):
    r = x.shape[-1]
    half = r // 2
    inv = jnp.power(jnp.float32(theta), -jnp.arange(half, dtype=jnp.float32) * (2.0 / r))
    ang = pos.astype(jnp.float32)[:, None] * inv[None, :]
    shape = (pos.shape[0],) + (1,) * (x.ndim - 3) + (half,)
    cos = jnp.cos(ang).reshape(shape)
    sin = jnp.sin(ang).reshape(shape)
    xf = x.astype(jnp.float32)
    x1, x2 = xf[..., :half], xf[..., half:]
    return jnp.concatenate([x1 * cos - x2 * sin, x1 * sin + x2 * cos], axis=-1).astype(x.dtype)

def partial_rope(x, pos):
    return jnp.concatenate([rope(x[..., :ROT_DIM], pos, ROPE_THETA), x[..., ROT_DIM:]], axis=-1)

def axial_rope(x, row, col):
    half = x.shape[-1] // 2
    return jnp.concatenate([rope(x[..., :half], row, D_THETA), rope(x[..., half:], col, D_THETA)], axis=-1)

def dilated_band_attention(q, k, v, window, dilation):
    b, s, h, dh = q.shape
    r = window // (2 * dilation)
    blk = r
    L = s // dilation
    nb = -(-L // blk)
    lp = nb * blk

    def residue(t):
        return t.reshape(b, L, dilation, h, dh).transpose(0, 2, 1, 3, 4)

    qr = jnp.pad(residue(q), ((0, 0), (0, 0), (0, lp - L), (0, 0), (0, 0)))
    qr = qr.reshape(b, dilation, nb, blk, h, dh)

    def band(t):
        tp = jnp.pad(residue(t), ((0, 0), (0, 0), (blk, lp - L + blk), (0, 0), (0, 0)))
        tp = tp.reshape(b, dilation, nb + 2, blk, h, dh)
        return jnp.concatenate([tp[:, :, 0:nb], tp[:, :, 1:nb + 1], tp[:, :, 2:nb + 2]], axis=3)

    kb, vb = band(k), band(v)
    scores = jnp.einsum('bdnqhc,bdnkhc->bdnhqk', qr, kb).astype(jnp.float32) * (dh ** -0.5)
    qi = jnp.arange(blk)[:, None]
    ki = jnp.arange(3 * blk)[None, :]
    in_band = jnp.abs(ki - blk - qi) <= r
    kpos = jnp.arange(nb)[:, None] * blk - blk + jnp.arange(3 * blk)[None, :]
    valid = in_band[None] & ((kpos >= 0) & (kpos < L))[:, None, :]
    scores = jnp.where(valid[None, None, :, None], scores, NEG_INF)
    lse = jax.nn.logsumexp(scores, axis=-1)
    p = jnp.exp(scores - lse[..., None])
    out = jnp.einsum('bdnhqk,bdnkhc->bdnqhc', p.astype(v.dtype), vb)
    out = out.reshape(b, dilation, lp, h, dh)[:, :, :L].transpose(0, 2, 1, 3, 4).reshape(b, s, h, dh)
    lse = lse.transpose(0, 1, 2, 4, 3).reshape(b, dilation, lp, h)[:, :, :L]
    lse = lse.transpose(0, 2, 1, 3).reshape(b, s, h)
    return out, lse

def dilated_mixture(q, k, v):
    results = [dilated_band_attention(q, k, v, w, d) for (w, d) in A_PATTERNS]
    outs = jnp.stack([o for (o, _) in results], axis=0)
    lses = jnp.stack([l for (_, l) in results], axis=0)
    wts = jax.nn.softmax(lses, axis=0)
    return jnp.einsum('pbsh,pbshc->bshc', wts.astype(q.dtype), outs)

def spatial_gating(z, v_norm, w_s, b_s):
    b, s, _ = z.shape
    z = jax.nn.gelu(z)
    u, vv = jnp.split(z, 2, axis=-1)
    u = u.reshape(b, s, B_GROUPS, B_GROUP_DIM)
    vv = rmsnorm(vv.reshape(b, s, B_GROUPS, B_GROUP_DIM), v_norm)
    vv = vv.reshape(b, s // B_CHUNK, B_CHUNK, B_GROUPS, B_GROUP_DIM)
    mixed = jnp.einsum('gpq,bnqgc->bnpgc', w_s, vv) + b_s.T[None, None, :, :, None]
    return (u * mixed.reshape(b, s, B_GROUPS, B_GROUP_DIM)).reshape(b, s, B_WIDTH)

def block_attention(q, k, v):
    b, s, kvh, g, dk = q.shape
    nq = s // QBLK
    scale = dk ** -0.5
    qb = q.reshape(b, nq, QBLK, kvh, g, dk).transpose(1, 0, 2, 3, 4, 5)

    def one(qblk):
        sc = jnp.einsum('bqkgc,bskc->bkgqs', qblk, k).astype(jnp.float32) * scale
        p = jax.nn.softmax(sc, axis=-1)
        return jnp.einsum('bkgqs,bskc->bqkgc', p.astype(v.dtype), v)

    out = lax.map(one, qb)
    return out.transpose(1, 0, 2, 3, 4, 5).reshape(b, s, kvh * g * v.shape[-1])

def mixer_even(h, pos, w_in, gmlp_norm, w_s, b_s, w_out):
    b, s, _ = h.shape
    proj = h @ w_in
    q, k, v, z = jnp.split(proj, [A_WIDTH, 2 * A_WIDTH, 3 * A_WIDTH], axis=-1)
    q = partial_rope(q.reshape(b, s, A_HEADS, HEAD_DIM), pos)
    k = partial_rope(k.reshape(b, s, A_HEADS, HEAD_DIM), pos)
    v = v.reshape(b, s, A_HEADS, HEAD_DIM)
    a_out = dilated_mixture(q, k, v).reshape(b, s, A_WIDTH)
    g_out = spatial_gating(z, gmlp_norm, w_s, b_s)
    return jnp.concatenate([a_out, g_out], axis=-1) @ w_out

def mixer_odd(h, pos, row, col, w_in, cq_norm, w_cq_up, ckv_norm, w_ckv_up, dq_norm, dk_norm, w_out):
    b, s, _ = h.shape
    proj = h @ w_in
    o1 = C_Q_RANK
    o2 = o1 + C_KV_RANK
    o3 = o2 + C_ROPE
    o4 = o3 + D_HEADS * HEAD_DIM
    o5 = o4 + D_KV_HEADS * HEAD_DIM
    cq, ckv, ck_rope, dq, dk, dv = jnp.split(proj, [o1, o2, o3, o4, o5], axis=-1)
    cq = (rmsnorm(cq, cq_norm) @ w_cq_up).reshape(b, s, C_HEADS, C_NOPE + C_ROPE)
    q_nope, q_rope = cq[..., :C_NOPE], rope(cq[..., C_NOPE:], pos, ROPE_THETA)
    kv = (rmsnorm(ckv, ckv_norm) @ w_ckv_up).reshape(b, s, C_HEADS, C_NOPE + C_V)
    k_nope, v_c = kv[..., :C_NOPE], kv[..., C_NOPE:]
    k_rope = rope(ck_rope, pos, ROPE_THETA)
    q_c = jnp.concatenate([q_nope, q_rope], axis=-1)[:, :, :, None]
    k_c = jnp.concatenate([k_nope, jnp.broadcast_to(k_rope[:, :, None], (b, s, C_HEADS, C_ROPE))], axis=-1)
    c_out = block_attention(q_c, k_c, v_c)
    dq = axial_rope(rmsnorm(dq.reshape(b, s, D_KV_HEADS, D_GROUP, HEAD_DIM), dq_norm), row, col)
    dk = axial_rope(rmsnorm(dk.reshape(b, s, D_KV_HEADS, HEAD_DIM), dk_norm), row, col)
    dv = dv.reshape(b, s, D_KV_HEADS, HEAD_DIM)
    d_out = block_attention(dq, dk, dv)
    return jnp.concatenate([c_out, d_out], axis=-1) @ w_out

def ec_moe(h, w_router, w_gate, w_up, w_down):
    b, s, d = h.shape
    cap = EC_FACTOR * s // N_EXPERTS
    logits = jnp.einsum('bsd,de->bse', h, w_router).astype(jnp.float32)
    aff = jax.nn.softmax(logits, axis=-1)
    gates, idx = lax.top_k(aff.transpose(0, 2, 1), cap)
    xs = jax.vmap(lambda hb, ib: hb[ib])(h, idx)
    g = jnp.einsum('becd,edf->becf', xs, w_gate)
    u = jnp.einsum('becd,edf->becf', xs, w_up)
    y = jnp.einsum('becf,efd->becd', jax.nn.silu(g) * u, w_down)
    y = y * gates[..., None].astype(y.dtype)
    return jax.vmap(lambda ib, yb: jnp.zeros((s, d), yb.dtype).at[ib.reshape(-1)].add(yb.reshape(-1, d)))(idx, y)

def first_inputs(seed: int = 0) -> dict:
    key = jax.random.key(seed)
    ks = jax.random.split(key, 21)
    n_even = (DEPTH + 1) // 2
    n_odd = DEPTH // 2

    def normal(k, shape, scale):
        return jax.random.normal(k, shape, jnp.float32) * scale

    def gain(k, shape):
        return 1.0 + 0.02 * jax.random.normal(k, shape, jnp.float32)

    return {
        "x": normal(ks[0], (BATCH, SEQ, D_MODEL), 1.0),
        "norm_mix": gain(ks[1], (DEPTH, D_MODEL)),
        "norm_ffn": gain(ks[2], (DEPTH, D_MODEL)),
        "even_w_in": normal(ks[3], (n_even, D_MODEL, EVEN_IN), D_MODEL ** -0.5),
        "even_gmlp_norm": gain(ks[4], (n_even, B_GROUPS, B_GROUP_DIM)),
        "even_w_spatial": normal(ks[5], (n_even, B_GROUPS, B_CHUNK, B_CHUNK), B_CHUNK ** -0.5),
        "even_b_spatial": normal(ks[6], (n_even, B_GROUPS, B_CHUNK), 0.02),
        "even_w_out": normal(ks[7], (n_even, A_WIDTH + B_WIDTH, D_MODEL), (A_WIDTH + B_WIDTH) ** -0.5),
        "odd_w_in": normal(ks[8], (n_odd, D_MODEL, ODD_IN), D_MODEL ** -0.5),
        "odd_cq_norm": gain(ks[9], (n_odd, C_Q_RANK)),
        "odd_w_cq_up": normal(ks[10], (n_odd, C_Q_RANK, C_HEADS * (C_NOPE + C_ROPE)), C_Q_RANK ** -0.5),
        "odd_ckv_norm": gain(ks[11], (n_odd, C_KV_RANK)),
        "odd_w_ckv_up": normal(ks[12], (n_odd, C_KV_RANK, C_HEADS * (C_NOPE + C_V)), C_KV_RANK ** -0.5),
        "odd_dq_norm": gain(ks[13], (n_odd, HEAD_DIM)),
        "odd_dk_norm": gain(ks[14], (n_odd, HEAD_DIM)),
        "odd_w_out": normal(ks[15], (n_odd, C_HEADS * C_V + D_HEADS * HEAD_DIM, D_MODEL), (C_HEADS * C_V + D_HEADS * HEAD_DIM) ** -0.5),
        "moe_w_router": normal(ks[16], (DEPTH, D_MODEL, N_EXPERTS), D_MODEL ** -0.5),
        "moe_w_gate": normal(ks[17], (DEPTH, N_EXPERTS, D_MODEL, EXPERT_FF), D_MODEL ** -0.5),
        "moe_w_up": normal(ks[18], (DEPTH, N_EXPERTS, D_MODEL, EXPERT_FF), D_MODEL ** -0.5),
        "moe_w_down": normal(ks[19], (DEPTH, N_EXPERTS, EXPERT_FF, D_MODEL), EXPERT_FF ** -0.5),
        "final_norm": gain(ks[20], (D_MODEL,)),
    }

def first_block(x, norm_mix, norm_ffn, even_w_in, even_gmlp_norm, even_w_spatial, even_b_spatial, even_w_out,
              odd_w_in, odd_cq_norm, odd_w_cq_up, odd_ckv_norm, odd_w_ckv_up, odd_dq_norm, odd_dk_norm, odd_w_out,
              moe_w_router, moe_w_gate, moe_w_up, moe_w_down, final_norm):
    b, s, _ = x.shape
    pos = jnp.arange(s, dtype=jnp.int32)
    rows = s // GRID_W
    row = jnp.repeat(jnp.arange(rows, dtype=jnp.int32), GRID_W)
    col = jnp.tile(jnp.arange(GRID_W, dtype=jnp.int32), rows)
    for i in range(DEPTH):
        j = i // 2
        h = rmsnorm(x, norm_mix[i])
        if i % 2 == 0:
            mix = mixer_even(h, pos, even_w_in[j], even_gmlp_norm[j], even_w_spatial[j], even_b_spatial[j], even_w_out[j])
        else:
            mix = mixer_odd(h, pos, row, col, odd_w_in[j], odd_cq_norm[j], odd_w_cq_up[j], odd_ckv_norm[j],
                            odd_w_ckv_up[j], odd_dq_norm[j], odd_dk_norm[j], odd_w_out[j])
        x = x + mix
        x = x + ec_moe(rmsnorm(x, norm_ffn[i]), moe_w_router[i], moe_w_gate[i], moe_w_up[i], moe_w_down[i])
    return rmsnorm(x, final_norm)


DEPTH_2 = 1

CTX_LEN = 256
ATTN_WIDTH = D_MODEL // 2
N_Q_HEADS = ATTN_WIDTH // HEAD_DIM
N_KV_HEADS = N_Q_HEADS // 4
Q_PER_KV = N_Q_HEADS // N_KV_HEADS
KV_WIDTH = N_KV_HEADS * HEAD_DIM
WINDOW = 128
BLOCK = 128
ROPE_BASE = 10000.0
RWKV_WIDTH = D_MODEL // 2
RWKV_HEAD_DIM = 64
RWKV_HEADS = RWKV_WIDTH // RWKV_HEAD_DIM
DECAY_LORA = 32
ICLR_LORA = 32
GATE_LORA = 96
RWKV_IN_WIDTH = 3 * RWKV_WIDTH + DECAY_LORA + ICLR_LORA + GATE_LORA
SHORT_CONV = 3
N_BRANCHES = 2
IN_WIDTH = ATTN_WIDTH + 2 * KV_WIDTH + RWKV_IN_WIDTH + N_BRANCHES * D_MODEL
D_FF = 4 * D_MODEL
N_MOD = 6
NORM_EPS = 1e-6
LNX_EPS = 1e-5 * RWKV_HEAD_DIM
IN_SPLITS = [ATTN_WIDTH, ATTN_WIDTH + KV_WIDTH, ATTN_WIDTH + 2 * KV_WIDTH,
             ATTN_WIDTH + 2 * KV_WIDTH + RWKV_IN_WIDTH]
RW_SPLITS = [RWKV_WIDTH, 2 * RWKV_WIDTH, 3 * RWKV_WIDTH,
             3 * RWKV_WIDTH + DECAY_LORA, 3 * RWKV_WIDTH + DECAY_LORA + ICLR_LORA]


def rmsnorm_2(x, g):
    xf = x.astype(jnp.float32)
    y = xf * lax.rsqrt(jnp.mean(xf * xf, axis=-1, keepdims=True) + NORM_EPS)
    return (y * g.astype(jnp.float32)).astype(x.dtype)

def modulate(h, shift, scale):
    return h * (1 + scale) + shift

def axial_rope_tables(rows):
    n_freq = HEAD_DIM // 4
    inv_freq = jnp.power(ROPE_BASE, -jnp.arange(n_freq, dtype=jnp.float32) / n_freq)
    row = jnp.repeat(jnp.arange(rows, dtype=jnp.float32), GRID_W)
    col = jnp.tile(jnp.arange(GRID_W, dtype=jnp.float32), rows)
    ang = jnp.concatenate([row[:, None] * inv_freq, col[:, None] * inv_freq], axis=-1)
    return jnp.cos(ang), jnp.sin(ang)

def apply_rope(x, cos, sin):
    half = x.shape[-1] // 2
    x1, x2 = x[..., :half], x[..., half:]
    c = cos[:, None, :].astype(x.dtype)
    s = sin[:, None, :].astype(x.dtype)
    return jnp.concatenate([x1 * c - x2 * s, x1 * s + x2 * c], axis=-1)

def sink_column(sink, lead_shape):
    s = sink.astype(jnp.float32).reshape(N_KV_HEADS, Q_PER_KV)
    return jnp.broadcast_to(s[:, :, None, None], lead_shape + (1,))

def latent_window_attention(q, k, v, kc, vc, sink):
    B, L, _, dh = q.shape
    Lc = kc.shape[1]
    nb = L // BLOCK
    scale = dh ** -0.5
    qb = q.reshape(B, nb, BLOCK, N_KV_HEADS, Q_PER_KV, dh)
    pad = ((0, 0), (BLOCK, BLOCK), (0, 0), (0, 0))

    def band(t):
        tb = jnp.pad(t, pad).reshape(B, nb + 2, BLOCK, N_KV_HEADS, dh)
        return jnp.concatenate([tb[:, :-2], tb[:, 1:-1], tb[:, 2:]], axis=2)

    kb, vb = band(k), band(v)
    s_loc = jnp.einsum('bnqgrd,bnkgd->bngrqk', qb, kb).astype(jnp.float32) * scale
    s_ctx = jnp.einsum('bnqgrd,bcgd->bngrqc', qb, kc).astype(jnp.float32) * scale
    blk = jnp.arange(nb)[:, None, None]
    qi = jnp.arange(BLOCK)[None, :, None]
    kj = jnp.arange(3 * BLOCK)[None, None, :]
    i_pos = blk * BLOCK + qi
    j_pos = blk * BLOCK - BLOCK + kj
    valid = (jnp.abs(i_pos - j_pos) <= WINDOW) & (j_pos >= 0) & (j_pos < L)
    s_loc = jnp.where(valid[None, :, None, None], s_loc, -jnp.inf)
    s_sink = jnp.broadcast_to(sink.astype(jnp.float32).reshape(N_KV_HEADS, Q_PER_KV)[None, None, :, :, None, None],
                              s_loc.shape[:-1] + (1,))
    p = jax.nn.softmax(jnp.concatenate([s_loc, s_ctx, s_sink], axis=-1), axis=-1)
    p_loc = p[..., :3 * BLOCK].astype(v.dtype)
    p_ctx = p[..., 3 * BLOCK:3 * BLOCK + Lc].astype(v.dtype)
    o = (jnp.einsum('bngrqk,bnkgd->bnqgrd', p_loc, vb)
         + jnp.einsum('bngrqc,bcgd->bnqgrd', p_ctx, vc))
    return o.reshape(B, L, N_Q_HEADS * dh)

def context_attention(qc, kc, vc, sink):
    B, Lc, _, dh = qc.shape
    qg = qc.reshape(B, Lc, N_KV_HEADS, Q_PER_KV, dh)
    s = jnp.einsum('bqgrd,bkgd->bgrqk', qg, kc).astype(jnp.float32) * dh ** -0.5
    s_sink = sink_column(sink, s.shape[1:-1])[None]
    s_sink = jnp.broadcast_to(s_sink, s.shape[:-1] + (1,))
    p = jax.nn.softmax(jnp.concatenate([s, s_sink], axis=-1), axis=-1)
    o = jnp.einsum('bgrqk,bkgd->bqgrd', p[..., :Lc].astype(vc.dtype), vc)
    return o.reshape(B, Lc, N_Q_HEADS * dh)

def short_conv(u, w):
    L = u.shape[1]
    half = SHORT_CONV // 2
    up = jnp.pad(u, ((0, 0), (half, half), (0, 0)))
    return sum(up[:, t:t + L] * w[t] for t in range(SHORT_CONV))

def rwkv_prepare(u, decay_w0, decay_w2, iclr_a0, iclr_a2, k_k, k_a):
    B, L, _ = u.shape
    r, k, v, hw, ha, hg = jnp.split(u, RW_SPLITS, axis=-1)

    def heads(t):
        return t.astype(jnp.float32).reshape(B, L, RWKV_HEADS, RWKV_HEAD_DIM)

    kk = heads(k * k_k)
    kk = kk * lax.rsqrt(jnp.maximum(jnp.sum(kk * kk, axis=-1, keepdims=True), 1e-24))
    dirs = []
    for d in range(2):
        w_log = -jax.nn.softplus(-(decay_w0[d] + jnp.tanh(hw) @ decay_w2[d])) - 0.5
        a = jax.nn.sigmoid(iclr_a0[d] + ha @ iclr_a2[d])
        decay = jnp.exp(-jnp.exp(heads(w_log)))
        k_d = heads(k * (1 + (a - 1) * k_a))
        dirs.append((decay, kk * heads(a), k_d))
    return heads(r), heads(v), hg, kk, dirs

def wkv7_scan(S0, r, decay, kk, b, k, v, reverse, emit):
    xs = tuple(jnp.moveaxis(t, 1, 0) for t in (r, decay, kk, b, k, v))

    def step(S, inp):
        r_t, w_t, kk_t, b_t, k_t, v_t = inp
        sa = jnp.einsum('bhvk,bhk->bhv', S, -kk_t)
        S = S * w_t[:, :, None, :] + sa[..., None] * b_t[:, :, None, :] + v_t[..., None] * k_t[:, :, None, :]
        y = jnp.einsum('bhvk,bhk->bhv', S, r_t) if emit else None
        return S, y

    S, ys = lax.scan(step, S0, xs, reverse=reverse)
    return S, (jnp.moveaxis(ys, 0, 1) if emit else None)

def rwkv_output(y, r, v, hg, dirs, gate_g2, r_k, lnx_w, lnx_b):
    B, L = y.shape[:2]
    mu = jnp.mean(y, axis=-1, keepdims=True)
    var = jnp.mean(jnp.square(y - mu), axis=-1, keepdims=True)
    yn = (y - mu) * lax.rsqrt(var + LNX_EPS)
    k_sum = dirs[0][2] + dirs[1][2]
    bonus = jnp.sum(r * k_sum * r_k.astype(jnp.float32), axis=-1, keepdims=True) * v
    out = (yn.reshape(B, L, RWKV_WIDTH) * lnx_w + lnx_b + bonus.reshape(B, L, RWKV_WIDTH)).astype(hg.dtype)
    g = jax.nn.sigmoid(hg) @ gate_g2
    return out * g

def merge_branches(ya, yr, gate_logits, w_branch_attn, w_branch_rwkv, w_out):
    ga, gr = jnp.split(jax.nn.sigmoid(gate_logits), N_BRANCHES, axis=-1)
    return (ga * (ya @ w_branch_attn) + gr * (yr @ w_branch_rwkv)) @ w_out

def sq_relu_mlp(h, w_up, w_down):
    return jnp.square(jax.nn.relu(h @ w_up)) @ w_down

def trunk_layer(x, xc, c, c_ctx, cos, sin, w_ada, b_ada, norm1_g, w_in, sink, conv_w,
                decay_w0, decay_w2, iclr_a0, iclr_a2, gate_g2, k_k, k_a, r_k, lnx_w, lnx_b,
                w_branch_attn, w_branch_rwkv, w_out, norm2_g, w_mlp_up, w_mlp_down, update_ctx):
    B, L, D = x.shape
    Lc = xc.shape[1]
    mod = (jax.nn.silu(c) @ w_ada + b_ada).reshape(B, 1, N_MOD, D)
    shift1, scale1, gate1, shift2, scale2, gate2 = [mod[:, :, i] for i in range(N_MOD)]
    modc = (jax.nn.silu(c_ctx) @ w_ada + b_ada).reshape(N_MOD, D)

    h = modulate(rmsnorm_2(x, norm1_g), shift1, scale1)
    hc = modulate(rmsnorm_2(xc, norm1_g), modc[0], modc[1])
    q, k, v, rw, gl = jnp.split(h @ w_in, IN_SPLITS, axis=-1)
    qc, kc, vc, rwc, glc = jnp.split(hc @ w_in, IN_SPLITS, axis=-1)

    q = apply_rope(q.reshape(B, L, N_Q_HEADS, HEAD_DIM), cos, sin)
    k = apply_rope(k.reshape(B, L, N_KV_HEADS, HEAD_DIM), cos, sin)
    v = v.reshape(B, L, N_KV_HEADS, HEAD_DIM)
    kc = kc.reshape(B, Lc, N_KV_HEADS, HEAD_DIM)
    vc = vc.reshape(B, Lc, N_KV_HEADS, HEAD_DIM)
    ya = latent_window_attention(q, k, v, kc, vc, sink)

    r_l, v_l, hg_l, kk_l, dirs_l = rwkv_prepare(short_conv(rw, conv_w), decay_w0, decay_w2,
                                               iclr_a0, iclr_a2, k_k, k_a)
    r_c, v_c, hg_c, kk_c, dirs_c = rwkv_prepare(short_conv(rwc, conv_w), decay_w0, decay_w2,
                                               iclr_a0, iclr_a2, k_k, k_a)
    S0 = jnp.zeros((B, RWKV_HEADS, RWKV_HEAD_DIM, RWKV_HEAD_DIM), jnp.float32)
    y_lat = []
    y_ctx = []
    for d, rev in enumerate((False, True)):
        dec_c, b_c, k_c = dirs_c[d]
        S_ctx, yc_d = wkv7_scan(S0, r_c, dec_c, kk_c, b_c, k_c, v_c, rev, update_ctx)
        dec_l, b_l, k_l = dirs_l[d]
        _, y_d = wkv7_scan(S_ctx, r_l, dec_l, kk_l, b_l, k_l, v_l, rev, True)
        y_lat.append(y_d)
        y_ctx.append(yc_d)
    yr = rwkv_output(y_lat[0] + y_lat[1], r_l, v_l, hg_l, dirs_l, gate_g2, r_k, lnx_w, lnx_b)

    x = x + gate1 * merge_branches(ya, yr, gl, w_branch_attn, w_branch_rwkv, w_out)
    x = x + gate2 * sq_relu_mlp(modulate(rmsnorm_2(x, norm2_g), shift2, scale2), w_mlp_up, w_mlp_down)

    if update_ctx:
        yac = context_attention(qc.reshape(B, Lc, N_Q_HEADS, HEAD_DIM), kc, vc, sink)
        yrc = rwkv_output(y_ctx[0] + y_ctx[1], r_c, v_c, hg_c, dirs_c, gate_g2, r_k, lnx_w, lnx_b)
        xc = xc + modc[2] * merge_branches(yac, yrc, glc, w_branch_attn, w_branch_rwkv, w_out)
        xc = xc + modc[5] * sq_relu_mlp(modulate(rmsnorm_2(xc, norm2_g), modc[3], modc[4]), w_mlp_up, w_mlp_down)
    return x, xc

def second_inputs(seed: int = 0) -> dict:
    key = jax.random.key(seed)
    ks = iter(jax.random.split(key, 32))

    def nrm(shape, s):
        return jax.random.normal(next(ks), shape, jnp.float32) * s

    D = D_MODEL
    L = DEPTH_2
    conv_base = jnp.asarray([0.25, 1.0, 0.25], jnp.float32)[None, :, None]
    return {
        "x": nrm((BATCH, SEQ, D), 1.0),
        "c": nrm((BATCH, D), 1.0),
        "ctx": nrm((BATCH, CTX_LEN, D), 1.0),
        "c_ctx": nrm((D,), 1.0),
        "w_ada": nrm((L, D, N_MOD * D), 0.5 * D ** -0.5),
        "b_ada": nrm((L, N_MOD * D), 0.02),
        "norm1_g": 1.0 + nrm((L, D), 0.05),
        "w_in": nrm((L, D, IN_WIDTH), D ** -0.5),
        "sink": nrm((L, N_Q_HEADS), 0.5),
        "conv_w": conv_base + nrm((L, SHORT_CONV, RWKV_IN_WIDTH), 0.05),
        "decay_w0": nrm((L, 2, RWKV_WIDTH), 0.5),
        "decay_w2": nrm((L, 2, DECAY_LORA, RWKV_WIDTH), DECAY_LORA ** -0.5),
        "iclr_a0": nrm((L, 2, RWKV_WIDTH), 0.5),
        "iclr_a2": nrm((L, 2, ICLR_LORA, RWKV_WIDTH), ICLR_LORA ** -0.5),
        "gate_g2": nrm((L, GATE_LORA, RWKV_WIDTH), GATE_LORA ** -0.5),
        "k_k": 1.0 + nrm((L, RWKV_WIDTH), 0.1),
        "k_a": 1.0 + nrm((L, RWKV_WIDTH), 0.1),
        "r_k": nrm((L, RWKV_HEADS, RWKV_HEAD_DIM), 0.1),
        "lnx_w": 1.0 + nrm((L, RWKV_WIDTH), 0.05),
        "lnx_b": nrm((L, RWKV_WIDTH), 0.02),
        "w_branch_attn": nrm((L, ATTN_WIDTH, D), ATTN_WIDTH ** -0.5),
        "w_branch_rwkv": nrm((L, RWKV_WIDTH, D), RWKV_WIDTH ** -0.5),
        "w_out": nrm((L, D, D), D ** -0.5),
        "norm2_g": 1.0 + nrm((L, D), 0.05),
        "w_mlp_up": nrm((L, D, D_FF), D ** -0.5),
        "w_mlp_down": nrm((L, D_FF, D), D_FF ** -0.5),
        "norm_f_g": 1.0 + nrm((D,), 0.05),
    }

def second_block(x, c, ctx, c_ctx, w_ada, b_ada, norm1_g, w_in, sink, conv_w, decay_w0, decay_w2,
              iclr_a0, iclr_a2, gate_g2, k_k, k_a, r_k, lnx_w, lnx_b, w_branch_attn, w_branch_rwkv,
              w_out, norm2_g, w_mlp_up, w_mlp_down, norm_f_g):
    rows = x.shape[1] // GRID_W
    cos, sin = axial_rope_tables(rows)
    xc = ctx
    for l in range(DEPTH_2):
        x, xc = trunk_layer(x, xc, c, c_ctx, cos, sin, w_ada[l], b_ada[l], norm1_g[l], w_in[l], sink[l],
                            conv_w[l], decay_w0[l], decay_w2[l], iclr_a0[l], iclr_a2[l], gate_g2[l],
                            k_k[l], k_a[l], r_k[l], lnx_w[l], lnx_b[l], w_branch_attn[l], w_branch_rwkv[l],
                            w_out[l], norm2_g[l], w_mlp_up[l], w_mlp_down[l], update_ctx=(l < DEPTH_2 - 1))
    return rmsnorm_2(x, norm_f_g)


def setup_inputs(seed=0):
    out = dict(first_inputs(seed))
    for name, value in second_inputs(seed + 1).items():
        if name != "x":
            out[name + "_2"] = value
    return out


def reference(
    x, norm_mix, norm_ffn, even_w_in, even_gmlp_norm, even_w_spatial, even_b_spatial,
    even_w_out, odd_w_in, odd_cq_norm, odd_w_cq_up, odd_ckv_norm, odd_w_ckv_up, odd_dq_norm,
    odd_dk_norm, odd_w_out, moe_w_router, moe_w_gate, moe_w_up, moe_w_down, final_norm, c_2,
    ctx_2, c_ctx_2, w_ada_2, b_ada_2, norm1_g_2, w_in_2, sink_2, conv_w_2, decay_w0_2,
    decay_w2_2, iclr_a0_2, iclr_a2_2, gate_g2_2, k_k_2, k_a_2, r_k_2, lnx_w_2, lnx_b_2,
    w_branch_attn_2, w_branch_rwkv_2, w_out_2, norm2_g_2, w_mlp_up_2, w_mlp_down_2, norm_f_g_2,
):
    x = first_block(
        x, norm_mix, norm_ffn, even_w_in, even_gmlp_norm, even_w_spatial, even_b_spatial,
        even_w_out, odd_w_in, odd_cq_norm, odd_w_cq_up, odd_ckv_norm, odd_w_ckv_up, odd_dq_norm,
        odd_dk_norm, odd_w_out, moe_w_router, moe_w_gate, moe_w_up, moe_w_down, final_norm,
    )
    return second_block(
        x, c_2, ctx_2, c_ctx_2, w_ada_2, b_ada_2, norm1_g_2, w_in_2, sink_2, conv_w_2,
        decay_w0_2, decay_w2_2, iclr_a0_2, iclr_a2_2, gate_g2_2, k_k_2, k_a_2, r_k_2, lnx_w_2,
        lnx_b_2, w_branch_attn_2, w_branch_rwkv_2, w_out_2, norm2_g_2, w_mlp_up_2, w_mlp_down_2,
        norm_f_g_2,
    )


_drawn_inputs = setup_inputs


def setup_inputs(seed=0):
    import zlib

    import numpy as np

    out = dict(_drawn_inputs(seed))
    spreads = {}
    factors = {'norm_mix': 3.118,
     'even_gmlp_norm': 4.011,
     'even_b_spatial': 4.119,
     'odd_cq_norm': 8.0,
     'odd_ckv_norm': 8.0,
     'odd_dq_norm': 8.0,
     'odd_dk_norm': 8.0,
     'final_norm': 2.789,
     'ctx_2': 4.941,
     'norm1_g_2': 3.662,
     'sink_2': 8.0,
     'decay_w0_2': 3.373,
     'decay_w2_2': 3.79,
     'k_k_2': 64.0,
     'lnx_w_2': 64.0,
     'lnx_b_2': 200.0,
     'norm2_g_2': 8.0}
    for name, (base, spread) in spreads.items():
        noise = np.random.default_rng([zlib.crc32(name.encode()), seed]).standard_normal(out[name].shape)
        drawn = base * np.exp(spread * noise) if base else spread * noise
        out[name] = jnp.asarray(drawn.astype(out[name].dtype))
    for name, factor in factors.items():
        out[name] = (out[name] * factor).astype(out[name].dtype)
    return out
```

```python
from contextlib import ExitStack, contextmanager

import numpy as np

import concourse.bass as bass
from concourse import mybir

F32 = mybir.dt.float32
U32 = mybir.dt.uint32
ALU = mybir.AluOpType
ACT = mybir.ActivationFunctionType
AX = mybir.AxisListType

P = 128
D = 1024
S = 1024
TILES = S // P
KT = D // P
EPS = 1e-6
NEG = -1e30
HD = 64
BANK = 512
KB = 1024
ARENA = 16896

A_WIDTH, B_WIDTH, A_HEADS = 768, 256, 12
N_EXPERTS, CAP, FF = 16, 128, 512
CTX = 256
LNX_EPS = 1e-5 * 64
RW_CH = 4
T_ALL = CTX + S
CHUNK = 64


class Step:

    def __init__(self, eng, sem):
        self.eng, self.sem, self.n = eng, sem, 0

    def __call__(self, *instructions):
        for i in instructions:
            i.then_inc(self.sem, 1)
            self.n += 1
        self.eng.wait_ge(self.sem, self.n)


STAGES = [0]


@contextmanager
def stage(nc, *names):
    STAGES[0] += 1
    sems = [nc.alloc_semaphore(f"{n}_s{STAGES[0]}") for n in names]
    with nc.Block(no_gpsimd_drain=True) as block:
        yield (block, *sems)
    nc.clear_and_free_semaphores(sems)
    nc.all_engine_barrier()


class Chip:

    def __init__(self, nc, dram):
        self.nc, self.dram, self.n = nc, dram, 0
        self.psum = nc.alloc_psum_tensor("psum", [P, 8, BANK], F32)
        self.dump = None

    def at(self, name, kb, shape, dt=F32):
        self.n += 1
        nbytes = int(np.prod(shape[1:])) * 4
        assert ARENA + kb * KB + nbytes <= 229344, (name, kb, shape)
        return self.nc.alloc_sbuf_tensor_at(f"{name}_{self.n}", shape, dt, offset=ARENA + int(kb * KB))


def bcast(ap, shape):
    return ap.to_broadcast(shape)



def load(c, pairs, small=False):
    with stage(c.nc, "tables_loaded") as (block, loaded):
        @block.sync
        def _(sp):
            for dst, src in pairs:
                sp.dma_start(dst, src, allow_slow_non_contiguous=small).then_inc(loaded, 16)
            sp.wait_ge(loaded, 16 * len(pairs))


def norm_rows(c, src, dst, tiles, gain, scr):
    nc = c.nc
    gain_b = c.at("gain_b", scr, [P, D])
    sq = c.at("squares", scr + 4, [P, 2, D])
    st = c.at("stats", scr + 12, [P, 3, tiles])
    with stage(nc, "gain_loaded", "squares_summed", "roots_taken", "rows_scaled", "dve_step") as (
            block, gain_loaded, summed, roots, scaled, dve_step):
        @block.sync
        def _(sp):
            sp.dma_start(gain_b[:], gain.partition_broadcast(P)).then_inc(gain_loaded, 16)
            sp.wait_ge(gain_loaded, 16)

        @block.scalar
        def _(act):
            for t in range(tiles):
                if t >= 2:
                    act.wait_ge(summed, t - 1)
                act.activation(sq[:, t % 2], src[:, t], ACT.Square, accum_out=st[:, 0, t:t + 1]).then_inc(summed, 1)
            act.wait_ge(summed, tiles)
            act.activation(st[:, 1], st[:, 0], ACT.Sqrt, scale=1.0 / D, bias=c.eps[:, 0:1]).then_inc(roots, 1)

        @block.vector
        def _(dve):
            step = Step(dve, dve_step)
            dve.wait_ge(roots, 1)
            step(dve.reciprocal(st[:, 2], st[:, 1]))
            dve.wait_ge(gain_loaded, 16)
            for t in range(tiles):
                dve.scalar_tensor_tensor(dst[:, t], src[:, t], st[:, 2, t:t + 1], gain_b[:],
                                         ALU.mult, ALU.mult).then_inc(scaled, 1)
            dve.wait_ge(scaled, tiles)


def transposes(c, groups):
    nc, ps = c.nc, c.psum
    n = len(groups)
    with stage(nc, "block_transposed", "act_copied", "dve_copied") as (block, done, act_copied, dve_copied):
        @block.tensor
        def _(pe):
            for i, (srcs, dst, _, _) in enumerate(groups):
                if i >= 8:
                    pe.wait_ge(act_copied if i % 2 else dve_copied, (i - 8) // 2 + 1)
                w = dst.shape[0]
                for j, s in enumerate(srcs):
                    last = pe.transpose(ps[0:w, i % 8, j * P:(j + 1) * P], s, c.ident[:])
                last.then_inc(done, 1)

        def copy(i, eng):
            srcs, dst, scale, shift = groups[i]
            w = dst.shape[0]
            src = ps[0:w, i % 8, 0:P * len(srcs)]
            eng.wait_ge(done, i + 1)
            if len(dst.shape) == 3:
                src = src.rearrange("p (a b) -> p a b", b=dst.shape[2])
            return src, dst, scale, shift

        @block.scalar
        def _(act):
            for i in range(1, n, 2):
                src, dst, scale, shift = copy(i, act)
                if scale is None:
                    act.activation(dst, src, ACT.Copy).then_inc(act_copied, 1)
                else:
                    act.activation(dst, src, ACT.Identity, bias=shift, scale=scale).then_inc(act_copied, 1)

        @block.vector
        def _(dve):
            for i in range(0, n, 2):
                src, dst, scale, shift = copy(i, dve)
                if scale is None:
                    dve.tensor_copy(dst, src).then_inc(dve_copied, 1)
                else:
                    dve.tensor_scalar(dst, src, scale, shift, ALU.mult, ALU.add).then_inc(dve_copied, 1)


def rows_to_cols(c, rows, cols, tiles, chunks, col0=0, scale=None, shift=None):
    groups = []
    for half in range(0, tiles, 4):
        m = min(4, tiles - half)
        for k in range(chunks):
            groups.append(([rows[:, t, col0 + k * P:col0 + (k + 1) * P] for t in range(half, half + m)],
                           cols[:, k, half * P:(half + m) * P],
                           None if scale is None else scale[:, k:k + 1],
                           None if shift is None else shift[:, k:k + 1]))
    transposes(c, groups)


def linear(c, kt, units, weights, ring, evacuate):
    nc, ps = c.nc, c.psum
    on_act, act_evacuate, dve_evacuate = evacuate
    before = {u: sum(1 for v in range(u) if on_act(v) == on_act(u)) for u in range(len(units))}
    last_use = {w: max(u for u, x in enumerate(units) if x[0] == w) for w in range(len(weights))}
    slots = len(ring)
    names = [f"weights_loaded_{i}" for i in range(slots)]
    with stage(nc, "unit_summed", "act_evacuated", "dve_evacuated", *names) as (
            block, summed, act_evac, dve_evac, *loaded):
        @block.sync
        def _(sp):
            for w, pairs in enumerate(weights):
                if w >= slots:
                    sp.wait_ge(summed, last_use[w - slots] + 1)
                dst, src = pairs(ring[w % slots])
                sp.dma_start(dst, src).then_inc(loaded[w % slots], 16)

        @block.tensor
        def _(pe):
            for u, (w, operands, shape) in enumerate(units):
                if weights:
                    pe.wait_ge(loaded[w % slots], 16 * (w // slots + 1))
                if u >= 8:
                    pe.wait_ge(act_evac if on_act(u - 8) else dve_evac, before[u - 8] + 1)
                out = ps[0:shape[0], u % 8, 0:shape[1]]
                for k in range(kt):
                    lhsT, rhs = operands(ring[w % slots], k)
                    last = pe.matmul(out, lhsT, rhs, start=(k == 0), stop=(k == kt - 1))
                last.then_inc(summed, 1)

        @block.scalar
        def _(act):
            for u, (_, _, shape) in enumerate(units):
                if on_act(u):
                    act.wait_ge(summed, u + 1)
                    act_evacuate(u, act, ps[0:shape[0], u % 8, 0:shape[1]]).then_inc(act_evac, 1)

        @block.vector
        def _(dve):
            for u, (_, _, shape) in enumerate(units):
                if not on_act(u):
                    dve.wait_ge(summed, u + 1)
                    dve_evacuate(u, dve, ps[0:shape[0], u % 8, 0:shape[1]]).then_inc(dve_evac, 1)


def linear_rows(c, cols, kt, w_dram, spans, ring_kb, slots, tiles, on_act, act_evac, dve_evac):
    ring = [c.at("weights", ring_kb + 2 * kt * i, [P, kt, BANK]) for i in range(slots)]
    w_rows = w_dram.rearrange("(k p) n -> p k n", p=P)
    weights, units = [], []
    for i, (a, b) in enumerate(spans):
        weights.append(lambda slot, a=a, b=b: (slot[:, :, 0:b - a], w_rows[:, :, a:b]))
        for t in range(tiles):
            units.append((i, lambda slot, k, t=t, a=a, b=b: (cols[:, k, t * P:(t + 1) * P], slot[:, k, 0:b - a]),
                          (P, b - a)))
    linear(c, kt, units, weights, ring, (
        lambda u: on_act(u // tiles),
        lambda u, act, psum: act_evac(u // tiles, u % tiles, act, psum),
        lambda u, dve, psum: dve_evac(u // tiles, u % tiles, dve, psum)))


def rope(step, dve, x1, x2, cos, sin, tmp):
    a, b, e, f = tmp
    step(dve.tensor_tensor(a, x1, cos, ALU.mult), dve.tensor_tensor(b, x2, sin, ALU.mult),
         dve.tensor_tensor(e, x1, sin, ALU.mult), dve.tensor_tensor(f, x2, cos, ALU.mult))
    step(dve.tensor_tensor(x1, a, b, ALU.subtract), dve.tensor_tensor(x2, e, f, ALU.add))


def attention(c, works, scale, tiles_kb, widths, sink=None):
    nc, ps = c.nc, c.psum
    n = len(works)
    biased = works[0][3] is not None
    at = lambda name, off, shape: c.at(name, tiles_kb + off, shape)
    s_b = at("scores", 0, [P, 2, 1024])
    p_b = at("probs", 8, [P, 2, 1024])
    pt_b = at("probs_turned", 16, [P, 2, 8, P])
    st = at("softmax_stats", 24, [P, 2, 8])
    with stage(nc, "scores_ready", "max_ready", "probs_ready", "probs_turned", "act_turned", "dve_turned",
               "weighted", "out_written", "dve_step", "sink_exp") as (
            block, scores_ready, max_ready, probs_ready, turned, act_turned, dve_turned, weighted,
            out_written, dve_step, sink_exp):
        S_ = lambda i: ps[:, 2 * (i % 2):2 * (i % 2) + 2, :].rearrange("p a b -> p (a b)")
        PT = lambda h: ps[:, 4 + h, :]
        O_ = lambda i: ps[:, 6 + i % 2, 0:HD]

        @block.tensor
        def _(pe):
            def scores(i):
                q, pieces, _, _, _, _ = works[i]
                if i >= 2:
                    pe.wait_ge(max_ready, i - 1)
                    pe.wait_ge(probs_ready, i - 1)
                for col, k in pieces:
                    last = pe.matmul(S_(i)[:, col:col + k.shape[-1]], q, k, start=True, stop=True)
                last.then_inc(scores_ready, 1)

            def turn(i):
                m = len(works[i][2])
                pe.wait_ge(probs_ready, i + 1)
                if i >= 1:
                    pe.wait_ge(act_turned, i)
                    pe.wait_ge(dve_turned, i)
                for j in range(m):
                    last = pe.transpose(PT(j // 4)[:, (j % 4) * P:(j % 4 + 1) * P],
                                        p_b[:, i % 2, j * P:(j + 1) * P], c.ident[:])
                last.then_inc(turned, 1)

            def weigh(i):
                v = works[i][2]
                pe.wait_ge(act_turned, i + 1)
                pe.wait_ge(dve_turned, i + 1)
                if i >= 2:
                    pe.wait_ge(out_written, i - 1)
                for j, vt in enumerate(v):
                    last = pe.matmul(O_(i), pt_b[:, i % 2, j, :], vt, start=(j == 0), stop=(j == len(v) - 1))
                last.then_inc(weighted, 1)

            scores(0)
            for i in range(n):
                if i + 1 < n:
                    scores(i + 1)
                if i >= 1:
                    weigh(i - 1)
                turn(i)
            weigh(n - 1)

        @block.scalar
        def _(act):
            def probs(i):
                w = widths(i)
                act.wait_ge(max_ready, i + 1)
                if i >= 2:
                    act.wait_ge(turned, i - 1)
                    act.wait_ge(out_written, i - 1)
                src = s_b[:, i % 2, 0:w] if biased else S_(i)[:, 0:w]
                if sink is not None:
                    act.activation(st[:, i % 2, 4:5], sink[1][:, works[i][5]:works[i][5] + 1], ACT.Exp,
                                   bias=st[:, i % 2, 1:2]).then_inc(sink_exp, 1)
                act.activation(p_b[:, i % 2, 0:w], src, ACT.Exp, bias=st[:, i % 2, 1:2], scale=scale,
                               accum_out=st[:, i % 2, 2:3]).then_inc(probs_ready, 1)

            probs(0)
            for i in range(n):
                if i + 1 < n:
                    probs(i + 1)
                act.wait_ge(turned, i + 1)
                if i >= 2:
                    act.wait_ge(weighted, i - 1)
                m = min(4, len(works[i][2]))
                act.activation(pt_b[:, i % 2, 0:m, :].rearrange("p a b -> p (a b)"), PT(0)[:, 0:m * P],
                               ACT.Copy).then_inc(act_turned, 1)

        @block.vector
        def _(dve):
            step = Step(dve, dve_step)

            def maxima(i):
                w = widths(i)
                dve.wait_ge(scores_ready, i + 1)
                if i >= 2:
                    dve.wait_ge(probs_ready, i - 1)
                if biased:
                    step(dve.tensor_tensor_reduce(s_b[:, i % 2, 0:w], S_(i)[:, 0:w], works[i][3], 1.0, NEG,
                                                  ALU.add, ALU.max, st[:, i % 2, 0:1]))
                else:
                    step(dve.tensor_reduce(st[:, i % 2, 0:1], S_(i)[:, 0:w], AX.X, ALU.max))
                if sink is not None:
                    k = works[i][5]
                    step(dve.tensor_tensor(st[:, i % 2, 0:1], st[:, i % 2, 0:1], sink[0][:, k:k + 1], ALU.max))
                dve.tensor_scalar(st[:, i % 2, 1:2], st[:, i % 2, 0:1], -scale, None, ALU.mult)\
                   .then_inc(max_ready, 1)

            def write(i):
                b = st[:, i % 2]
                dve.wait_ge(probs_ready, i + 1)
                if sink is not None:
                    dve.wait_ge(sink_exp, i + 1)
                    step(dve.tensor_tensor(b[:, 2:3], b[:, 2:3], b[:, 4:5], ALU.add))
                step(dve.reciprocal(b[:, 3:4], b[:, 2:3]))
                dve.wait_ge(weighted, i + 1)
                dve.tensor_scalar(works[i][4], O_(i), b[:, 3:4], None, ALU.mult).then_inc(out_written, 1)

            maxima(0)
            for i in range(n):
                if i + 1 < n:
                    maxima(i + 1)
                if i >= 1:
                    write(i - 1)
                dve.wait_ge(turned, i + 1)
                if i >= 2:
                    dve.wait_ge(weighted, i - 1)
                m = len(works[i][2])
                if m > 4:
                    dve.tensor_copy(pt_b[:, i % 2, 4:m, :].rearrange("p a b -> p (a b)"),
                                    PT(1)[:, 0:(m - 4) * P]).then_inc(dve_turned, 1)
                else:
                    dve.nop().then_inc(dve_turned, 1)
            write(n - 1)



def even_mixer(c, x, w):
    nc, dram = c.nc, c.dram
    hn = c.at("h_rows", 38 + 96, [P, TILES, D])
    hT = c.at("h_cols", 38, [P, KT, S])
    norm_rows(c, x, hn, TILES, dram["norm_mix"][0], 180)
    rows_to_cols(c, hn, hT, TILES, KT)
    qk = c.at("qk_rows", 118, [P, TILES, 2 * A_WIDTH])
    vz = c.at("vz_rows", 166, [P, TILES, A_WIDTH + 2 * B_WIDTH])
    v = lambda t, a, b: vz[:, t, a:b]
    spans = [(0, 512), (512, 1024), (1024, 1536), (1536, 2048), (2048, 2304), (2304, 2816)]

    def place(s, t):
        a, b = spans[s]
        return qk[:, t, a:b] if b <= 2 * A_WIDTH else vz[:, t, a - 2 * A_WIDTH:b - 2 * A_WIDTH]

    linear_rows(c, hT, KT, w, spans, 70, 3, TILES, lambda s: s == 5,
                lambda s, t, act, p: act.activation(place(s, t), p, ACT.Gelu_apprx_tanh),
                lambda s, t, dve, p: dve.tensor_copy(place(s, t), p))

    tmp = [c.at("rope_tmp", 70 + 6 * i, [P, TILES, 24, 8]) for i in range(4)]
    heads = qk[:].rearrange("p t (h e) -> p t h e", e=HD)
    with stage(nc, "dve_step") as (block, dve_step):
        @block.vector
        def _(dve):
            step = Step(dve, dve_step)
            cos = c.rope_cos[:, :, 0:8].unsqueeze(2).to_broadcast([P, TILES, 24, 8])
            sin = c.rope_sin[:, :, 0:8].unsqueeze(2).to_broadcast([P, TILES, 24, 8])
            rope(step, dve, heads[:, :, :, 0:8], heads[:, :, :, 8:16], cos, sin, [t[:] for t in tmp])
    qkT = c.at("qk_cols", 38, [P, 12, S])
    rows_to_cols(c, qk, qkT, TILES, 12)

    bias = c.at("window_bias", 86, [P, 1920])
    load(c, [(bias[:], dram["const_even_bias"])])
    ag = c.at("mix_rows", 118, [P, TILES, D])
    works = []
    for h in range(A_HEADS):
        r = slice(64 * (h % 2), 64 * (h % 2) + 64)
        for t in range(TILES):
            works.append((qkT[r, h // 2, t * P:(t + 1) * P],
                          [(0, qkT[r, 6 + h // 2, 0:512]), (512, qkT[r, 6 + h // 2, 512:1024])],
                          [vz[:, j, h * HD:(h + 1) * HD] for j in range(TILES)],
                          bias[:, 896 - 128 * t:896 - 128 * t + 1024], ag[:, t, h * HD:(h + 1) * HD], None))
    attention(c, works, HD ** -0.5, 94 - 0.5, lambda i: 1024)

    G = 4
    ws = c.at("w_spatial", 38, [P, G, P])
    wsT = c.at("w_spatial_turned", 40, [P, G, P])
    bs = c.at("b_spatial", 42, [P, G])
    gn = c.at("gmlp_gain", 42.5, [P, B_WIDTH])
    load(c, [(ws[:], dram["even_w_spatial"][0].rearrange("g p q -> p g q")),
             (bs[:], dram["even_b_spatial"][0].rearrange("g p -> p g")),
             (gn[:], dram["even_gmlp_norm"][0].rearrange("g c -> (g c)").partition_broadcast(P))], small=True)
    transposes(c, [([ws[:, g] for g in range(G)], wsT[:].rearrange("p g q -> p (g q)"), None, None)])
    vv = vz[:, :, A_WIDTH + B_WIDTH:A_WIDTH + 2 * B_WIDTH].rearrange("p t (g e) -> p t g e", e=64)
    u = vz[:, :, A_WIDTH:A_WIDTH + B_WIDTH]
    group_norm_rows(c, vv, gn[:].rearrange("p (g e) -> p g e", e=64).unsqueeze(1).to_broadcast([P, TILES, G, 64]),
                    TILES, G, 64, 44)
    ps = c.psum
    with stage(nc, "mixed", "gated") as (block, mixed, gated):
        @block.tensor
        def _(pe):
            for g in range(G):
                pe.matmul(ps[:, g, :].rearrange("p (t e) -> p t e", e=64), wsT[:, g], vv[:, :, g, :],
                          start=True, stop=True).then_inc(mixed, 1)

        @block.vector
        def _(dve):
            for g in range(G):
                dve.wait_ge(mixed, g + 1)
                dve.scalar_tensor_tensor(ag[:, :, A_WIDTH + g * 64:A_WIDTH + (g + 1) * 64],
                                         ps[:, g, :].rearrange("p (t e) -> p t e", e=64), bs[:, g:g + 1],
                                         u[:, :, g * 64:(g + 1) * 64], ALU.add, ALU.mult).then_inc(gated, 1)
    if c.dump:
        c.dump("g_out", ag)
    out_and_residual(c, x, ag, dram["even_w_out"][0], 38, 70)


def group_norm_rows(c, x, gain, tiles, groups, width, kb):
    sq = c.at("squares", kb, [P, tiles, groups, width])
    st = c.at("stats", kb + tiles * groups * width * 4 / KB, [P, 3, tiles, groups])
    with stage(c.nc, "sums_ready", "roots_ready", "dve_step") as (block, sums, roots, dve_step):
        @block.vector
        def _(dve):
            step = Step(dve, dve_step)
            step(dve.tensor_tensor(sq[:], x, x, ALU.mult))
            dve.tensor_reduce(st[:, 0], sq[:], AX.X, ALU.add).then_inc(sums, 1)
            dve.wait_ge(roots, 1)
            step(dve.reciprocal(st[:, 2], st[:, 1]))
            step(dve.tensor_tensor(x, x, st[:, 2].unsqueeze(3).to_broadcast([P, tiles, groups, width]), ALU.mult))
            step(dve.tensor_tensor(x, x, gain, ALU.mult))

        @block.scalar
        def _(act):
            act.wait_ge(sums, 1)
            act.activation(st[:, 1], st[:, 0], ACT.Sqrt, scale=1.0 / width, bias=c.eps[:, 0:1]).then_inc(roots, 1)


def out_and_residual(c, x, rows, w_dram, cols_kb, ring_kb):
    T = c.at("mix_cols", cols_kb, [P, KT, S])
    rows_to_cols(c, rows, T, TILES, KT)
    spans = [(0, 512), (512, 1024)]
    linear_rows(c, T, KT, w_dram, spans, ring_kb, 2, TILES, lambda s: False, None,
                lambda s, t, dve, p: dve.tensor_tensor(x[:, t, s * 512:(s + 1) * 512], p,
                                                       x[:, t, s * 512:(s + 1) * 512], ALU.add))



def experts(c, x, layer):
    nc, dram, ps = c.nc, c.dram, c.psum
    hn = c.at("h_rows", 38, [P, TILES, D])
    hT = c.at("h_cols", 70, [P, KT, S])
    norm_rows(c, x, hn, TILES, dram["norm_ffn"][layer], 102)
    rows_to_cols(c, hn, hT, TILES, KT)
    wr = c.at("w_router", 102, [P, KT, N_EXPERTS])
    lg = c.at("logits", 103, [P, TILES, N_EXPERTS])
    aff = c.at("affinity", 104, [N_EXPERTS, S])
    best = c.at("best_values", 108, [N_EXPERTS, CAP])
    besti = c.at("best_tokens", 109, [N_EXPERTS, CAP], U32)
    bestf = c.at("best_tokens_f", 110, [N_EXPERTS, CAP])
    sm = c.at("softmax_stats", 111, [P, 2, TILES])
    gates = c.at("gates", 4.5, [P, N_EXPERTS])
    tokens = c.at("tokens", 4.625, [P, N_EXPERTS], U32)
    h_dram, x_dram = dram["h_scratch"], dram["x_scratch"]
    with stage(nc, "stored", "router_loaded", "logits_ready", "max_off", "exp_ready", "aff_ready", "turned",
               "best_ready", "best_turned", "dve_step") as (
            block, stored, router_loaded, logits_ready, max_off, exp_ready, aff_ready, turned, best_ready,
            best_turned, dve_step):
        @block.sync
        def _(sp):
            sp.dma_start(wr[:], dram["moe_w_router"][layer].rearrange("(k p) e -> p k e", p=P))\
              .then_inc(router_loaded, 16)
            sp.dma_start(h_dram.rearrange("(t p) d -> p t d", p=P), hn[:]).then_inc(stored, 16)
            sp.dma_start(x_dram.rearrange("(t p) d -> p t d", p=P), x[:]).then_inc(stored, 16)
            sp.wait_ge(stored, 32)

        @block.tensor
        def _(pe):
            pe.wait_ge(router_loaded, 16)
            for t in range(TILES):
                for k in range(KT):
                    last = pe.matmul(ps[:, 0, t * 16:(t + 1) * 16], hT[:, k, t * P:(t + 1) * P], wr[:, k],
                                     start=(k == 0), stop=(k == KT - 1))
            last.then_inc(logits_ready, 1)
            pe.wait_ge(aff_ready, 1)
            for t in range(TILES):
                last = pe.transpose(ps[0:16, 1 + t // 4, (t % 4) * P:(t % 4 + 1) * P], lg[:, t], c.ident[:])
            last.then_inc(turned, 1)
            pe.wait_ge(best_ready, 1)
            pe.transpose(ps[:, 3, 0:16], best[:], c.ident[0:16, 0:16])
            pe.transpose(ps[:, 3, 16:32], bestf[:], c.ident[0:16, 0:16]).then_inc(best_turned, 1)

        @block.scalar
        def _(act):
            act.wait_ge(max_off, 1)
            act.activation(lg[:], lg[:], ACT.Exp).then_inc(exp_ready, 1)

        @block.vector
        def _(dve):
            step = Step(dve, dve_step)
            flat = ps[:, 0, 0:128].rearrange("p (t e) -> p t e", e=16)
            wide = lambda a: a.unsqueeze(2).to_broadcast([P, TILES, 16])
            dve.wait_ge(logits_ready, 1)
            step(dve.tensor_reduce(sm[:, 0], flat, AX.X, ALU.max))
            dve.tensor_tensor(lg[:], flat, wide(sm[:, 0]), ALU.subtract).then_inc(max_off, 1)
            dve.wait_ge(exp_ready, 1)
            step(dve.tensor_reduce(sm[:, 0], lg[:], AX.X, ALU.add))
            step(dve.reciprocal(sm[:, 1], sm[:, 0]))
            dve.tensor_tensor(lg[:], lg[:], wide(sm[:, 1]), ALU.mult).then_inc(aff_ready, 1)
            dve.wait_ge(turned, 1)
            step(dve.tensor_copy(aff[:], ps[0:16, 1:3, :].rearrange("p a b -> p (a b)")))
            for r in range(CAP // 8):
                b = best[:, r * 8:(r + 1) * 8]
                step(dve.max(b, aff[:]))
                step(dve.max_index(besti[:, r * 8:(r + 1) * 8], b, aff[:]))
                step(dve.match_replace(aff[:], b, aff[:], -1.0))
            dve.tensor_copy(bestf[:], besti[:]).then_inc(best_ready, 1)
            dve.wait_ge(best_turned, 1)
            step(dve.tensor_copy(gates[:], ps[:, 3, 0:16]), dve.tensor_copy(tokens[:], ps[:, 3, 16:32]))
    if c.dump:
        c.dump("gates", gates)

    NE = N_EXPERTS
    wg = c.at("w_gate", 38, [P, 2, KT, FF])
    wu = c.at("w_up", 70, [P, 2, KT, FF])
    wd = c.at("w_down", 102, [P, 2, 4, D])
    xs = c.at("picked", 134, [P, 2, D])
    xT = c.at("picked_cols", 142, [P, 2, KT, P])
    sg = c.at("silu_gate", 150, [P, 2, FF])
    ac = c.at("activated", 154, [P, 2, FF])
    aT = c.at("activated_cols", 158, [P, 2, 4, P])
    y = c.at("expert_out", 162, [P, 2, D])
    with stage(nc, "gate_up_loaded_0", "gate_up_loaded_1", "down_loaded_0", "down_loaded_1", "picked_0", "picked_1",
               "picked_turned", "picked_copied", "gate_up_done", "silu_done", "activated", "act_turned",
               "act_copied", "down_done", "scaled_dve", "scattered", "scaled_act") as (
            block, gu0, gu1, dn0, dn1, pk0, pk1, turned, copied, gate_up, silu, activated, aturned, acopied, down,
            scaled, scattered, scaled_act):
        gu, dn, pk = (gu0, gu1), (dn0, dn1), (pk0, pk1)

        @block.sync
        def _(sp):
            for e in range(NE):
                b = e % 2
                if e >= 2:
                    sp.wait_ge(gate_up, e - 1)
                sp.dma_start(wg[:, b], dram["moe_w_gate"][layer, e].rearrange("(k p) f -> p k f", p=P)).then_inc(gu[b], 16)
                sp.dma_start(wu[:, b], dram["moe_w_up"][layer, e].rearrange("(k p) f -> p k f", p=P)).then_inc(gu[b], 16)
                if e >= 2:
                    sp.wait_ge(down, e - 1)
                sp.dma_start(wd[:, b], dram["moe_w_down"][layer, e].rearrange("(k p) f -> p k f", p=P)).then_inc(dn[b], 16)

        @block.gpsimd
        def _(pool):
            def pick(e):
                if e >= 2:
                    pool.wait_ge(turned, e - 1)
                pool.indirect_dma_start(xs[:, e % 2], None, h_dram,
                                        bass.IndirectOffsetOnAxis(tokens[:, e:e + 1], 0)).then_inc(pk[e % 2], 16)

            pick(0)
            for e in range(NE):
                if e + 1 < NE:
                    pick(e + 1)
                pool.wait_ge(scaled, e + 1)
                pool.wait_ge(scaled_act, e + 1)
                if e >= 1:
                    pool.wait_ge(scattered, 16 * e)
                pool.indirect_dma_start(x_dram, bass.IndirectOffsetOnAxis(tokens[:, e:e + 1], 0), y[:, e % 2], None,
                                        compute_op=ALU.add).then_inc(scattered, 16)
            pool.wait_ge(scattered, 16 * NE)

        @block.tensor
        def _(pe):
            def turn(e):
                pe.wait_ge(pk[e % 2], 16 * (e // 2 + 1))
                if e >= 1:
                    pe.wait_ge(copied, 2 * e)
                for k in range(KT):
                    last = pe.transpose(ps[:, k // 4, (k % 4) * P:(k % 4 + 1) * P], xs[:, e % 2, k * P:(k + 1) * P],
                                        c.ident[:])
                last.then_inc(turned, 1)

            turn(0)
            for e in range(NE):
                b = e % 2
                pe.wait_ge(copied, 2 * e + 2)
                pe.wait_ge(gu[b], 32 * (e // 2 + 1))
                if e >= 1:
                    pe.wait_ge(activated, e)
                for bank, wt in ((2, wg), (3, wu)):
                    for k in range(KT):
                        last = pe.matmul(ps[:, bank, :], xT[:, b, k], wt[:, b, k], start=(k == 0), stop=(k == KT - 1))
                last.then_inc(gate_up, 1)
                if e + 1 < NE:
                    turn(e + 1)
                pe.wait_ge(activated, e + 1)
                if e >= 1:
                    pe.wait_ge(acopied, e)
                for k in range(4):
                    last = pe.transpose(ps[:, 4, k * P:(k + 1) * P], ac[:, b, k * P:(k + 1) * P], c.ident[:])
                last.then_inc(aturned, 1)
                pe.wait_ge(acopied, e + 1)
                pe.wait_ge(dn[b], 16 * (e // 2 + 1))
                if e >= 1:
                    pe.wait_ge(scaled, e)
                    pe.wait_ge(scaled_act, e)
                for half in range(2):
                    for k in range(4):
                        last = pe.matmul(ps[:, 5 + half, :], aT[:, b, k], wd[:, b, k, half * 512:(half + 1) * 512],
                                         start=(k == 0), stop=(k == 3))
                last.then_inc(down, 1)

        @block.scalar
        def _(act):
            for e in range(NE):
                b = e % 2
                act.wait_ge(gate_up, e + 1)
                if e >= 2:
                    act.wait_ge(activated, e - 1)
                act.activation(sg[:, b], ps[:, 2, :], ACT.Silu).then_inc(silu, 1)
                act.wait_ge(down, e + 1)
                if e >= 2:
                    act.wait_ge(scattered, 16 * (e - 1))
                act.activation(y[:, b, 512:1024], ps[:, 6, :], ACT.Copy, scale=gates[:, e:e + 1])\
                   .then_inc(scaled_act, 1)

        @block.vector
        def _(dve):
            def copy_rows(e):
                dve.wait_ge(turned, e + 1)
                if e >= 2:
                    dve.wait_ge(gate_up, e - 1)
                for h in range(2):
                    dve.tensor_copy(xT[:, e % 2, 4 * h:4 * h + 4].rearrange("p a b -> p (a b)"), ps[:, h, :])\
                       .then_inc(copied, 1)

            copy_rows(0)
            for e in range(NE):
                b = e % 2
                dve.wait_ge(silu, e + 1)
                if e >= 2:
                    dve.wait_ge(aturned, e - 1)
                dve.tensor_tensor(ac[:, b], sg[:, b], ps[:, 3, :], ALU.mult).then_inc(activated, 1)
                if e + 1 < NE:
                    copy_rows(e + 1)
                dve.wait_ge(aturned, e + 1)
                if e >= 2:
                    dve.wait_ge(down, e - 1)
                dve.tensor_copy(aT[:, b].rearrange("p a b -> p (a b)"), ps[:, 4, :]).then_inc(acopied, 1)
                dve.wait_ge(down, e + 1)
                if e >= 2:
                    dve.wait_ge(scattered, 16 * (e - 1))
                dve.tensor_scalar(y[:, b, 0:512], ps[:, 5, :], gates[:, e:e + 1], None, ALU.mult).then_inc(scaled, 1)
    load(c, [(x[:], x_dram.rearrange("(t p) d -> p t d", p=P))])



def odd_mixer(c, x):
    dram = c.dram
    hn = c.at("h_rows", 134, [P, TILES, D])
    hT = c.at("h_cols", 38, [P, KT, S])
    norm_rows(c, x, hn, TILES, dram["norm_mix"][1], 180)
    rows_to_cols(c, hn, hT, TILES, KT)
    low = c.at("latent_rows", 118, [P, TILES, 416])
    dqk = c.at("d_rows", 131, [P, TILES, 768])
    dv = c.at("dv_rows", 155, [P, TILES, 128])
    spans = [(0, 416), (416, 928), (928, 1184)]

    def copy_out(s, t, act, p):
        if s == 0:
            return act.activation(low[:, t], p, ACT.Copy)
        if s == 1:
            return act.activation(dqk[:, t, 0:512], p, ACT.Copy)
        act.activation(dqk[:, t, 512:640], p[:, 0:128], ACT.Copy)
        return act.activation(dv[:, t], p[:, 128:256], ACT.Copy)

    linear_rows(c, hT, KT, dram["odd_w_in"][0], spans, 70, 3, TILES, lambda s: True, copy_out, None)

    gains = c.at("norm_gains", 38, [P, 512])
    load(c, [(gains[:, 0:256], dram["odd_cq_norm"][0].partition_broadcast(P)),
             (gains[:, 256:384], dram["odd_ckv_norm"][0].partition_broadcast(P)),
             (gains[:, 384:448], dram["odd_dq_norm"][0].partition_broadcast(P)),
             (gains[:, 448:512], dram["odd_dk_norm"][0].partition_broadcast(P))])
    wide = lambda a, g, w: a.unsqueeze(1).unsqueeze(1).to_broadcast([P, TILES, g, w])
    group_norm_rows(c, low[:, :, 0:256].unsqueeze(2), wide(gains[:, 0:256], 1, 256), TILES, 1, 256, 40)
    group_norm_rows(c, low[:, :, 256:384].unsqueeze(2), wide(gains[:, 256:384], 1, 128), TILES, 1, 128, 40)
    heads = dqk[:].rearrange("p t (h e) -> p t h e", e=HD)
    group_norm_rows(c, heads[:, :, 0:8], wide(gains[:, 384:448], 8, 64), TILES, 8, 64, 40)
    group_norm_rows(c, heads[:, :, 8:10], wide(gains[:, 448:512], 2, 64), TILES, 2, 64, 40)
    tmp = [c.at("rope_tmp", 40 + 5 * i, [P, TILES, 10, 16]) for i in range(4)]
    table = lambda t, a, b, g: t[:, :, a:b].unsqueeze(2).to_broadcast([P, TILES, g, b - a])
    with stage(c.nc, "dve_step") as (block, dve_step):
        @block.vector
        def _(dve):
            step = Step(dve, dve_step)
            for off, a in ((0, 24), (32, 40)):
                rope(step, dve, heads[:, :, 0:10, off:off + 16], heads[:, :, 0:10, off + 16:off + 32],
                     table(c.rope_cos, a, a + 16, 10), table(c.rope_sin, a, a + 16, 10), [t[:] for t in tmp])
            kr = low[:, :, 384:416].unsqueeze(2)
            rope(step, dve, kr[:, :, :, 0:16], kr[:, :, :, 16:32], table(c.rope_cos, 8, 24, 1),
                 table(c.rope_sin, 8, 24, 1), [t[:, :, 0:1] for t in tmp])
            step(dve.tensor_copy(dqk[:, :, 640:704], dqk[:, :, 576:640]),
                 dve.tensor_copy(dqk[:, :, 704:768], dqk[:, :, 512:576]))

    mix = c.at("mix_rows", 175, [P, TILES, D])
    dT = c.at("d_cols", 38, [P, 6, S])
    rows_to_cols(c, dqk, dT, TILES, 6)
    works = []
    for h in range(8):
        r, kv = slice(64 * (h % 2), 64 * (h % 2) + 64), h // 4
        kc = 4 if h % 2 == kv else 5
        for t in range(TILES):
            works.append((dT[r, h // 2, t * P:(t + 1) * P], [(0, dT[r, kc, 0:512]), (512, dT[r, kc, 512:1024])],
                          [dv[:, j, kv * 64:(kv + 1) * 64] for j in range(TILES)], None,
                          mix[:, t, 512 + h * 64:512 + (h + 1) * 64], None))
    attention(c, works, HD ** -0.5, 62, lambda i: 1024)

    lowT = c.at("latent_cols", 38, [P, 3, S])
    rows_to_cols(c, low, lowT, TILES, 3)
    wq = c.at("w_cq_up", 50, [P, 2, 768])
    wkv = c.at("w_ckv_up", 56, [P, 1024])
    q = c.at("c_q_rows", 60, [P, TILES, 768])
    load(c, [(wq[:], dram["odd_w_cq_up"][0].rearrange("(k p) n -> p k n", p=P)), (wkv[:], dram["odd_w_ckv_up"][0])])
    linear(c, 2, [(0, lambda slot, k, t=t, h=h: (lowT[:, k, t * P:(t + 1) * P], wq[:, k, h * 384:(h + 1) * 384]), (P, 384))
                  for h in range(2) for t in range(TILES)], [], [None],
           (lambda u: True,
            lambda u, act, p: act.activation(q[:, u % 8, (u // 8) * 384:(u // 8 + 1) * 384], p, ACT.Copy), None))
    qr = q[:].rearrange("p t (h e) -> p t h e", e=96)
    tmp = [c.at("rope_tmp", 84 + 4 * i, [P, TILES, 8, 16]) for i in range(4)]
    with stage(c.nc, "dve_step") as (block, dve_step):
        @block.vector
        def _(dve):
            step = Step(dve, dve_step)
            rope(step, dve, qr[:, :, :, 64:80], qr[:, :, :, 80:96], table(c.rope_cos, 8, 24, 8),
                 table(c.rope_sin, 8, 24, 8), [t[:] for t in tmp])
    qT = c.at("c_q_cols", 143, [96, 8, S])
    transposes(c, [([q[:, t, h * 96:(h + 1) * 96] for t in range(a, a + 4)], qT[:, h, a * P:(a + 4) * P], None, None)
                   for a in (0, 4) for h in range(8)])
    vc = c.at("c_v_rows", 60, [P, TILES, 512])
    kc = c.at("c_k_rows", 76, [P, TILES, 768])
    kcr = kc[:].rearrange("p t (h e) -> p t h e", e=96)
    vcr = vc[:].rearrange("p t (h e) -> p t h e", e=64)

    def split_kv(u, dve, p):
        t, h = u % 8, u // 8
        p4 = p.rearrange("p (h e) -> p h e", e=128)
        dve.tensor_copy(kcr[:, t, 4 * h:4 * h + 4, 0:64], p4[:, :, 0:64])
        dve.tensor_copy(kcr[:, t, 4 * h:4 * h + 4, 64:96], low[:, t, 384:416].unsqueeze(1).to_broadcast([P, 4, 32]))
        return dve.tensor_copy(vcr[:, t, 4 * h:4 * h + 4, :], p4[:, :, 64:128])

    linear(c, 1, [(0, lambda slot, k, t=t, h=h: (lowT[:, 2, t * P:(t + 1) * P], wkv[:, h * 512:(h + 1) * 512]), (P, 512))
                  for h in range(2) for t in range(TILES)], [], [None], (lambda u: False, None, split_kv))
    kT = c.at("c_k_cols", 101, [96, 8, S])
    transposes(c, [([kc[:, t, h * 96:(h + 1) * 96] for t in range(a, a + 4)], kT[:, h, a * P:(a + 4) * P], None, None)
                   for a in (0, 4) for h in range(8)])
    works = [(qT[:, h, t * P:(t + 1) * P], [(0, kT[:, h, 0:512]), (512, kT[:, h, 512:1024])],
              [vc[:, j, h * 64:(h + 1) * 64] for j in range(TILES)], None, mix[:, t, h * 64:(h + 1) * 64], None)
             for h in range(8) for t in range(TILES)]
    attention(c, works, 96.0 ** -0.5, 76, lambda i: 1024)
    if c.dump:
        c.dump("odd_mix", mix)
    out_and_residual(c, x, mix, dram["odd_w_out"][0], 38, 70)



def second_block(c, x):
    nc, dram, ps = c.nc, c.dram, c.psum
    va, vb = c.at("vector_rows", 38, [P, P]), c.at("conv_rows", 38.5, [P, P])
    vT = c.at("vector_cols", 4.75, [P, 92])
    conv = c.at("conv_cols", 5.25, [P, 42])
    mod = c.at("modulation", 5.5, [P, 96])
    flat = lambda a: a.rearrange("(r p) -> r p", p=P)
    rows = [(0, flat(dram["b_ada_2"][0])), (48, flat(dram["c_2"][0])), (56, flat(dram["c_ctx_2"])),
            (64, dram["decay_w0_2"][0].rearrange("a (r p) -> (a r) p", p=P)),
            (72, dram["iclr_a0_2"][0].rearrange("a (r p) -> (a r) p", p=P)),
            (80, flat(dram["k_k_2"][0])), (84, flat(dram["k_a_2"][0])),
            (88, dram["r_k_2"][0].rearrange("(r a) e -> r (a e)", a=2))]
    with stage(nc, "cleared", "loaded", "turned", "copied") as (block, cleared, loaded, turned, copied):
        @block.gpsimd
        def _(pool):
            pool.memset(va[:], 0.0).then_inc(cleared, 1)
            pool.memset(vb[:], 0.0).then_inc(cleared, 1)

        @block.sync
        def _(sp):
            sp.wait_ge(cleared, 2)
            for r, src in rows:
                sp.dma_start(va[r:r + src.shape[0], :], src).then_inc(loaded, 16)
            for tap in range(3):
                cw = dram["conv_w_2"][0, tap]
                sp.dma_start(vb[14 * tap:14 * tap + 12, :], flat(cw[0:1536])).then_inc(loaded, 16)
                sp.dma_start(vb[14 * tap + 12:14 * tap + 13, 0:64], cw[1536:1600].unsqueeze(0)).then_inc(loaded, 16)
                sp.dma_start(vb[14 * tap + 13:14 * tap + 14, 0:96], cw[1600:1696].unsqueeze(0)).then_inc(loaded, 16)

        @block.tensor
        def _(pe):
            pe.wait_ge(loaded, 16 * (len(rows) + 9))
            pe.transpose(ps[:, 0, 0:P], va[:], c.ident[:])
            pe.transpose(ps[:, 1, 0:P], vb[:], c.ident[:]).then_inc(turned, 1)

        @block.vector
        def _(dve):
            dve.wait_ge(turned, 1)
            dve.tensor_copy(conv[:], ps[:, 1, 0:42])
            dve.tensor_copy(vT[:, 0:48], ps[:, 0, 0:48])
            dve.tensor_copy(vT[:, 64:92], ps[:, 0, 64:92]).then_inc(copied, 1)
            dve.wait_ge(copied, 1)

        @block.scalar
        def _(act):
            act.wait_ge(copied, 1)
            act.activation(vT[:, 48:64], ps[:, 0, 48:64], ACT.Silu).then_inc(copied, 1)
            act.wait_ge(copied, 2)

    cond = vT[:, 48:64].rearrange("p (a k) -> p k a", k=KT)
    w_ada = dram["w_ada_2"][0].rearrange("(k p) n -> p k n", p=P)
    ring = [c.at("weights", 38 + 16 * i, [P, KT, BANK]) for i in range(4)]
    linear(c, KT, [(u // 4, lambda slot, k, u=u: (slot[:, k, (u % 4) * P:(u % 4 + 1) * P], cond[:, k]), (P, 2))
                   for u in range(48)],
           [lambda slot, w=w: (slot[:], w_ada[:, :, w * BANK:(w + 1) * BANK]) for w in range(12)], ring,
           (lambda u: False, None,
            lambda u, dve, p: dve.tensor_scalar(mod[:, 2 * u:2 * u + 2], p, vT[:, u:u + 1], None, ALU.add)))
    mod3 = mod[:].rearrange("p (i k a) -> p i k a", i=6, k=KT)
    mods = c.at("modulation_scales", 5.875, [P, 3, KT])
    with stage(nc, "dve_step") as (block, dve_step):
        @block.vector
        def _(dve):
            step = Step(dve, dve_step)
            step(dve.tensor_scalar(mods[:, 0], mod3[:, 1, :, 0], 1.0, None, ALU.add),
                 dve.tensor_scalar(mods[:, 1], mod3[:, 1, :, 1], 1.0, None, ALU.add),
                 dve.tensor_scalar(mods[:, 2], mod3[:, 4, :, 0], 1.0, None, ALU.add))

    hn = c.at("h_rows", 134, [P, TILES, D])
    hT = c.at("h_cols", 38, [P, KT, S])
    norm_rows(c, x, hn, TILES, dram["norm1_g_2"][0], 180)
    rows_to_cols(c, hn, hT, TILES, KT, 0, mods[:, 0], mod3[:, 0, :, 0])
    xc, hcn = c.at("ctx_rows", 134, [P, 2, D]), c.at("h_ctx_rows", 142, [P, 2, D])
    hcT = c.at("h_ctx_cols", 70, [P, KT, CTX])
    load(c, [(xc[:], dram["ctx_2"][0].rearrange("(t p) d -> p t d", p=P))])
    norm_rows(c, xc, hcn, 2, dram["norm1_g_2"][0], 180)
    rows_to_cols(c, hcn, hcT, 2, KT, 0, mods[:, 1], mod3[:, 0, :, 1])
    if c.dump:
        c.dump("h2", hT)

    w_in = dram["w_in_2"][0]
    qk = c.at("qk_rows", 126, [P, TILES, 768])
    v = c.at("v_rows", 150, [P, 2 + TILES, 128])
    kx = c.at("ctx_k_rows", 155, [P, 2, 256])
    spans = [(0, 512), (512, 768)]

    def copy_out(s, t, act, p):
        if s == 0:
            return act.activation(qk[:, t, 0:512], p, ACT.Copy)
        act.activation(qk[:, t, 512:640], p[:, 0:128], ACT.Copy)
        return act.activation(v[:, 2 + t], p[:, 128:256], ACT.Copy)

    def copy_ctx(s, t, act, p):
        act.activation(kx[:, t, 0:128], p[:, 0:128], ACT.Copy)
        act.activation(kx[:, t, 128:192], p[:, 64:128], ACT.Copy)
        act.activation(kx[:, t, 192:256], p[:, 0:64], ACT.Copy)
        return act.activation(v[:, t], p[:, 128:256], ACT.Copy)

    linear_rows(c, hT, KT, w_in, spans, 78, 3, TILES, lambda s: True, copy_out, None)
    linear_rows(c, hcT, KT, w_in, [(512, 768)], 78, 3, 2, lambda s: True, copy_ctx, None)
    heads = qk[:].rearrange("p t (h e) -> p t h e", e=HD)
    tmp = [c.at("rope_tmp", 78 + 10 * i, [P, TILES, 10, 32]) for i in range(4)]
    table = lambda t: t[:, :, 24:56].unsqueeze(2).to_broadcast([P, TILES, 10, 32])
    with stage(nc, "stored", "dve_step") as (block, stored, dve_step):
        @block.sync
        def _(sp):
            sp.dma_start(dram["h_scratch"].rearrange("(k p) s -> p k s", p=P), hT[:]).then_inc(stored, 16)
            sp.dma_start(dram["x_scratch"].rearrange("(t p) d -> p t d", p=P), x[:]).then_inc(stored, 16)
            sp.wait_ge(stored, 32)

        @block.vector
        def _(dve):
            step = Step(dve, dve_step)
            rope(step, dve, heads[:, :, 0:10, 0:32], heads[:, :, 0:10, 32:64], table(c.rope_cos),
                 table(c.rope_sin), [t[:] for t in tmp])
            step(dve.tensor_copy(qk[:, :, 640:704], qk[:, :, 576:640]),
                 dve.tensor_copy(qk[:, :, 704:768], qk[:, :, 512:576]))
    qkT = c.at("qk_cols", 157, [P, 6, T_ALL])
    rows_to_cols(c, qk, qkT[:, :, CTX:], TILES, 6)
    rows_to_cols(c, kx, qkT[:, 4:6, 0:CTX], 2, 2)
    bias = c.at("window_bias", 103, [P, 2, 640])
    sinks = c.at("sinks", 108, [P, 2, 8])
    ya = c.at("ya_rows", 108.5, [P, TILES, 512])
    load(c, [(bias[:], dram["const_window_bias"]), (sinks[:, 1], dram["sink_2"][0].partition_broadcast(P))])
    with stage(nc, "dve_step") as (block, dve_step):
        @block.vector
        def _(dve):
            Step(dve, dve_step)(dve.tensor_scalar(sinks[:, 0], sinks[:, 1], float(HD) ** 0.5, None, ALU.mult))
    works = []
    for h in range(8):
        r, kv = slice(64 * (h % 2), 64 * (h % 2) + 64), h // 4
        kc = 4 if h % 2 == kv else 5
        for t in range(TILES):
            a, b = max(t - 1, 0), min(t + 2, TILES)
            n = (b - a) * P
            first = min(n, 256)
            pieces = [(0, qkT[r, kc, 0:CTX]), (CTX, qkT[r, kc, CTX + a * P:CTX + a * P + first])]
            if n > first:
                pieces.append((512, qkT[r, kc, CTX + a * P + first:CTX + b * P]))
            works.append((qkT[r, h // 2, CTX + t * P:CTX + (t + 1) * P], pieces,
                          [v[:, j, kv * 64:(kv + 1) * 64] for j in [0, 1] + list(range(2 + a, 2 + b))],
                          bias[:, 0 if t else 1, 0:CTX + n], ya[:, t, h * 64:(h + 1) * 64], h))
    attention(c, works, HD ** -0.5, 78, lambda i: works[i][3].shape[1], (sinks[:, 0], sinks[:, 1]))
    if c.dump:
        c.dump("ya", ya)
    yaT = c.at("ya_cols", 191, [P, 4, S])
    rows_to_cols(c, ya, yaT, TILES, 4)

    yr = rwkv(c, hT, hcT, w_in, conv, vT)
    if c.dump:
        c.dump("yr", yr)
    yrT = c.at("yr_cols", 169, [P, 4, S])
    rows_to_cols(c, yr, yrT, TILES, 4)
    load(c, [(hT[:], dram["h_scratch"].rearrange("(k p) s -> p k s", p=P)),
             (x[:], dram["x_scratch"].rearrange("(t p) d -> p t d", p=P))])

    W = 256
    NW = D // W
    wgt = c.at("gate_weights", 70, [P, 2, 2, KT, W])
    wbr = c.at("branch_weights", 102, [P, 2, 2, 4, W])
    m = c.at("merged_rows", 118, [P, TILES, D])
    sg = c.at("gates", 150, [P, 2, 2, W])
    pr = c.at("gated", 154, [P, 2, 2, W])
    gates_a = w_in[:, 2464:3488].rearrange("(k p) n -> p k n", p=P)
    gates_r = w_in[:, 3488:4512].rearrange("(k p) n -> p k n", p=P)
    wa = dram["w_branch_attn_2"][0].rearrange("(k p) n -> p k n", p=P)
    wr = dram["w_branch_rwkv_2"][0].rearrange("(k p) n -> p k n", p=P)
    with stage(nc, "weights_loaded_0", "weights_loaded_1", "products_ready", "sigmoids_ready", "branches_gated",
               "merged") as (block, l0, l1, products, sigmoids, gated, merged):
        loaded = (l0, l1)

        @block.sync
        def _(sp):
            for n in range(NW):
                if n >= 2:
                    sp.wait_ge(products, (n - 1) * TILES)
                cols = slice(n * W, (n + 1) * W)
                for dst, src in ((wgt[:, n % 2, 0], gates_a), (wgt[:, n % 2, 1], gates_r),
                                 (wbr[:, n % 2, 0], wa), (wbr[:, n % 2, 1], wr)):
                    sp.dma_start(dst, src[:, :, cols]).then_inc(loaded[n % 2], 16)

        @block.tensor
        def _(pe):
            for i in range(NW * TILES):
                n, t = divmod(i, TILES)
                pe.wait_ge(loaded[n % 2], 64 * (n // 2 + 1))
                if i >= 2:
                    pe.wait_ge(sigmoids, 2 * (i - 1))
                    pe.wait_ge(gated, i - 1)
                b, tok = 4 * (i % 2), slice(t * P, (t + 1) * P)
                for j in range(2):
                    for k in range(KT):
                        pe.matmul(ps[:, b + j, 0:W], hT[:, k, tok], wgt[:, n % 2, j, k], start=(k == 0),
                                  stop=(k == KT - 1))
                for j, y in enumerate((yaT, yrT)):
                    for k in range(4):
                        last = pe.matmul(ps[:, b + 2 + j, 0:W], y[:, k, tok], wbr[:, n % 2, j, k], start=(k == 0),
                                         stop=(k == 3))
                last.then_inc(products, 1)

        @block.scalar
        def _(act):
            for i in range(NW * TILES):
                act.wait_ge(products, i + 1)
                if i >= 2:
                    act.wait_ge(gated, i - 1)
                for j in range(2):
                    act.activation(sg[:, i % 2, j], ps[:, 4 * (i % 2) + j, 0:W], ACT.Sigmoid).then_inc(sigmoids, 1)

        @block.vector
        def _(dve):
            for i in range(NW * TILES):
                n, t = divmod(i, TILES)
                dve.wait_ge(sigmoids, 2 * i + 2)
                if i >= 2:
                    dve.wait_ge(merged, i - 1)
                dve.tensor_tensor(pr[:, i % 2], sg[:, i % 2], ps[:, 4 * (i % 2) + 2:4 * (i % 2) + 4, 0:W],
                                  ALU.mult).then_inc(gated, 1)
                dve.wait_ge(gated, i + 1)
                dve.tensor_tensor(m[:, t, n * W:(n + 1) * W], pr[:, i % 2, 0], pr[:, i % 2, 1], ALU.add)\
                   .then_inc(merged, 1)
            dve.wait_ge(merged, NW * TILES)

    mT = c.at("merged_cols", 38, [P, KT, S])
    rows_to_cols(c, m, mT, TILES, KT)
    g1, g2 = c.at("gate1_rows", 102, [P, D]), c.at("gate2_rows", 106, [P, D])
    spread = c.at("gate_spread", 110, [P, 2, KT, P])
    for j, (g, i) in enumerate(((g1, 2), (g2, 5))):
        with stage(nc, "spread_out") as (block, spread_out):
            @block.vector
            def _(dve):
                dve.tensor_copy(spread[:, j], mod3[:, i, :, 0].unsqueeze(2).to_broadcast([P, KT, P]))\
                   .then_inc(spread_out, 1)
                dve.wait_ge(spread_out, 1)
        transposes(c, [([spread[:, j, k] for k in range(a, a + 4)], g[:, a * P:(a + 4) * P], None, None)
                       for a in (0, 4)])
    gt = c.at("gated_out", 118, [P, 2, BANK])
    with ExitStack():
        counter = c.nc.alloc_semaphore("gated_out_ready")

        def add_gated(s, t, dve, p):
            u = s * TILES + t
            cols = slice(s * 512, (s + 1) * 512)
            dve.tensor_tensor(gt[:, u % 2], p, g1[:, cols], ALU.mult).then_inc(counter, 1)
            dve.wait_ge(counter, u + 1)
            return dve.tensor_tensor(x[:, t, cols], x[:, t, cols], gt[:, u % 2], ALU.add)

        linear_rows(c, mT, KT, dram["w_out_2"][0], [(0, 512), (512, 1024)], 70, 2, TILES, lambda s: False, None,
                    add_gated)
        c.nc.clear_and_free_semaphores([counter])
        c.nc.all_engine_barrier()
    if c.dump:
        c.dump("x_merge", x)

    g2k = c.at("gate2_rows_kept", 200, [P, D])
    with stage(nc, "moved") as (block, moved):
        @block.vector
        def _(dve):
            dve.tensor_copy(g2k[:], g2[:]).then_inc(moved, 1)
            dve.wait_ge(moved, 1)
    norm_rows(c, x, hn, TILES, dram["norm2_g_2"][0], 180)
    rows_to_cols(c, hn, hT, TILES, KT, 0, mods[:, 2], mod3[:, 3, :, 0])
    wu = c.at("w_up", 70, [P, 2, KT, 512])
    wd = c.at("w_down", 102, [P, 2, 4, D])
    aT = c.at("hidden_cols", 134, [P, 2, 4, S])
    acc = c.at("mlp_rows", 166, [P, TILES, D])
    rl = c.at("relu", 198, [P, 1, 512])
    mlp(c, x, hT, wu, wd, aT, acc, rl, g2k)


def mlp(c, x, hT, wu, wd, aT, acc, rl, gate):
    nc, dram, ps = c.nc, c.dram, c.psum
    steps = 4 * D // 512
    w_up = dram["w_mlp_up_2"][0].rearrange("(k p) n -> p k n", p=P)
    w_down = dram["w_mlp_down_2"][0].rearrange("(s k p) n -> s p k n", p=P, k=4)
    with stage(nc, "up_loaded_0", "up_loaded_1", "down_loaded_0", "down_loaded_1", "up_done", "relu_done",
               "squared", "down_done", "added", "dve_step") as (
            block, u0, u1, d0, d1, up_done, relu_done, squared, down_done, added, dve_step):
        up_loaded, down_loaded = (u0, u1), (d0, d1)

        @block.sync
        def _(sp):
            for s in range(steps):
                if s >= 2:
                    sp.wait_ge(up_done, 8 * (s - 1))
                sp.dma_start(wu[:, s % 2], w_up[:, :, s * 512:(s + 1) * 512]).then_inc(up_loaded[s % 2], 16)
                if s >= 2:
                    sp.wait_ge(down_done, 16 * (s - 1))
                sp.dma_start(wd[:, s % 2], w_down[s]).then_inc(down_loaded[s % 2], 16)

        @block.tensor
        def _(pe):
            def up(s):
                pe.wait_ge(up_loaded[s % 2], 16 * (s // 2 + 1))
                for i in range(8):
                    u = 8 * s + i
                    if u >= 4:
                        pe.wait_ge(relu_done, u - 3)
                    f, half = i // 2, i % 2
                    for k in range(KT):
                        last = pe.matmul(ps[:, i % 4, :], wu[:, s % 2, k, f * P:(f + 1) * P],
                                         hT[:, k, half * 512:(half + 1) * 512], start=(k == 0), stop=(k == KT - 1))
                    last.then_inc(up_done, 1)

            def down(s):
                pe.wait_ge(squared, 8 * (s + 1))
                pe.wait_ge(down_loaded[s % 2], 16 * (s // 2 + 1))
                for i in range(16):
                    u = 16 * s + i
                    if u >= 4:
                        pe.wait_ge(added, u - 3)
                    t, half = i // 2, i % 2
                    for k in range(4):
                        last = pe.matmul(ps[:, 4 + i % 4, :], aT[:, s % 2, k, t * P:(t + 1) * P],
                                         wd[:, s % 2, k, half * 512:(half + 1) * 512], start=(k == 0), stop=(k == 3))
                    last.then_inc(down_done, 1)

            up(0)
            for s in range(steps):
                if s + 1 < steps:
                    up(s + 1)
                down(s)

        @block.scalar
        def _(act):
            for s in range(steps):
                for i in range(8):
                    u = 8 * s + i
                    act.wait_ge(up_done, u + 1)
                    if u >= 1:
                        act.wait_ge(squared, u)
                    act.activation(rl[:, 0], ps[:, i % 4, :], ACT.Relu).then_inc(relu_done, 1)
                    act.wait_ge(relu_done, u + 1)
                    if s >= 2:
                        act.wait_ge(down_done, 16 * (s - 1))
                    act.activation(aT[:, s % 2, i // 2, (i % 2) * 512:(i % 2 + 1) * 512], rl[:, 0],
                                   ACT.Square).then_inc(squared, 1)

        @block.vector
        def _(dve):
            for s in range(steps):
                for i in range(16):
                    u = 16 * s + i
                    t, cols = i // 2, slice((i % 2) * 512, (i % 2 + 1) * 512)
                    dve.wait_ge(down_done, u + 1)
                    if s == 0:
                        dve.tensor_copy(acc[:, t, cols], ps[:, 4 + i % 4, :]).then_inc(added, 1)
                    else:
                        dve.wait_ge(added, u - 15)
                        dve.tensor_tensor(acc[:, t, cols], acc[:, t, cols], ps[:, 4 + i % 4, :], ALU.add)\
                           .then_inc(added, 1)
            dve.wait_ge(added, 16 * steps)
            step = Step(dve, dve_step)
            step(dve.tensor_tensor(acc[:], acc[:], gate[:].unsqueeze(1).to_broadcast([P, TILES, D]), ALU.mult))
            step(dve.tensor_tensor(x[:], x[:], acc[:], ALU.add))



def rwkv(c, hT, hcT, w_in, conv, vT):
    nc, dram, ps = c.nc, c.dram, c.psum
    widths = [P] * 12 + [64, 96]
    starts = [768 + P * j for j in range(12)] + [768 + 1536, 768 + 1600]
    U0, U1 = 1, CTX + 2
    ub = c.at("conv_in", 110, [P, 2, T_ALL + 3])
    rw = c.at("rwkv_cols", 120.5, [P, 14, T_ALL])
    ring = [c.at("weights", 78 + 16 * i, [P, KT, BANK]) for i in range(2)]
    rw_w = w_in[:, 768:2464].rearrange("(k p) n -> p k n", p=P)
    cuts = [(0, 512), (512, 1024), (1024, 1536), (1536, 1696)]
    parts = [(0, CTX, U0), (0, 512, U1), (512, 1024, U1 + 512)]
    with stage(nc, "weights_loaded_0", "weights_loaded_1", "edges_cleared", "summed", "copied", "convolved",
               "dve_step") as (block, l0, l1, edges, summed, copied, convolved, dve_step):
        loaded = (l0, l1)

        @block.sync
        def _(sp):
            for w, (a, b) in enumerate(cuts):
                if w >= 2:
                    sp.wait_ge(summed, 3 * 4 * (w - 1))
                sp.dma_start(ring[w % 2][:, :, 0:b - a], rw_w[:, :, a:b]).then_inc(loaded[w % 2], 16)

        @block.gpsimd
        def _(pool):
            for col in (0, CTX + 1, T_ALL + 2):
                pool.memset(ub[:, :, col:col + 1], 0.0).then_inc(edges, 1)

        @block.tensor
        def _(pe):
            for j in range(14):
                w = j // 4
                pe.wait_ge(loaded[w % 2], 16 * (w // 2 + 1))
                o = starts[j] - 768 - 512 * w
                for i, (a, b, _) in enumerate(parts):
                    u = 3 * j + i
                    if u >= 6:
                        pe.wait_ge(copied, u - 5)
                    for k in range(KT):
                        rhs = hcT[:, k, a:b] if i == 0 else hT[:, k, a:b]
                        last = pe.matmul(ps[0:widths[j], u % 6, 0:b - a], ring[w % 2][:, k, o:o + widths[j]], rhs,
                                         start=(k == 0), stop=(k == KT - 1))
                    last.then_inc(summed, 1)

        @block.scalar
        def _(act):
            for j in range(14):
                if j >= 2:
                    act.wait_ge(convolved, j - 1)
                for i, (a, b, o) in enumerate(parts):
                    u = 3 * j + i
                    act.wait_ge(summed, u + 1)
                    act.activation(ub[0:widths[j], j % 2, o:o + b - a], ps[0:widths[j], u % 6, 0:b - a], ACT.Copy)\
                       .then_inc(copied, 1)

        @block.vector
        def _(dve):
            step = Step(dve, dve_step)
            dve.wait_ge(edges, 3)
            for j in range(14):
                dve.wait_ge(copied, 3 * j + 3)
                n = widths[j]
                tap = lambda i: conv[0:n, 14 * i + j:14 * i + j + 1]
                for s, (o, n_tok, d) in enumerate(((U0, CTX, 0), (U1, S, CTX))):
                    u, out = ub[0:n, j % 2], rw[0:n, j, d:d + n_tok]
                    step(dve.tensor_scalar(out, u[:, o - 1:o - 1 + n_tok], tap(0), None, ALU.mult))
                    step(dve.scalar_tensor_tensor(out, u[:, o:o + n_tok], tap(1), out, ALU.mult, ALU.add))
                    step(dve.scalar_tensor_tensor(out, u[:, o + 1:o + 1 + n_tok], tap(2), out, ALU.mult, ALU.add))
                dve.nop().then_inc(convolved, 1)
    if c.dump:
        c.dump("rw", rw[:, 0:12])

    NT = T_ALL // P
    vrow = c.at("v_rows", 38, [P, NT, 512])
    rows = []
    for a in range(0, NT, 4):
        n = min(4, NT - a)
        for j in range(4):
            for t in range(a, a + n):
                rows.append(([rw[:, 8 + j, t * P:(t + 1) * P]], vrow[:, t, j * P:(j + 1) * P], None, None))
    transposes(c, rows)

    kk = rw[:, 8:12, :]
    r_, k_ = rw[:, 0:4, :], rw[:, 4:8, :]
    sq = c.at("kk_squares", 58, [P, 4, T_ALL])
    blocks = c.at("head_blocks", 98, [P, P])
    load(c, [(blocks[:], dram["const_head_blocks"])])
    with stage(nc, "squared", "summed", "rooted", "dve_step", "normalised") as (
            block, squared, summed, rooted, dve_step, normalised):
        pieces = [(j, a, min(a + 512, T_ALL)) for j in range(4) for a in range(0, T_ALL, 512)]

        @block.vector
        def _(dve):
            step = Step(dve, dve_step)
            step(*[dve.tensor_scalar(kk[:, j], k_[:, j], vT[:, 80 + j:81 + j], None, ALU.mult) for j in range(4)])
            dve.tensor_tensor(sq[:], kk, kk, ALU.mult).then_inc(squared, 1)
            for i, (j, a, b) in enumerate(pieces):
                dve.wait_ge(summed, i + 1)
                dve.tensor_scalar(sq[:, j, a:b], ps[:, i % 8, 0:b - a], 1e-24, None, ALU.max).then_inc(normalised, 1)
            dve.wait_ge(rooted, 1)
            step(dve.reciprocal(sq[:], sq[:]))
            step(dve.tensor_tensor(kk, kk, sq[:], ALU.mult))

        @block.tensor
        def _(pe):
            pe.wait_ge(squared, 1)
            for i, (j, a, b) in enumerate(pieces):
                if i >= 8:
                    pe.wait_ge(normalised, i - 7)
                pe.matmul(ps[:, i % 8, 0:b - a], blocks[:], sq[:, j, a:b], start=True, stop=True).then_inc(summed, 1)

        @block.scalar
        def _(act):
            act.wait_ge(normalised, len(pieces))
            act.activation(sq[:], sq[:], ACT.Sqrt).then_inc(rooted, 1)
    if c.dump:
        c.dump("kk", rw[:, 8:12])

    lora = rw[:, 12, :]
    y = c.at("y_rows", 58, [P, TILES, 512])
    lw = c.at("log_decay", 6, [P, 4, P])
    F = c.at("running_log", 8, [P, 4, P])
    e1 = c.at("exp_after", 10, [P, 4, P])
    e2 = c.at("exp_before", 12, [P, 4, P])
    e3 = c.at("exp_inverse", 14, [P, 4, P])
    rate = c.at("rate", 16, [P, 4, P])
    kd = c.at("key", 18, [P, 4, P])
    ar = c.at("a_and_r", 20, [P, 4, 2, P])
    bt = c.at("b_scaled", 24, [P, 4, P])
    kt = c.at("k_scaled", 26, [P, 4, P])
    bb = c.at("b_to_end", 28, [P, 4, P])
    kb = c.at("k_to_end", 30, [P, 4, P])
    rk = c.at("r_times_key", 32, [P, 4, P])
    sc = c.at("bonus_rows", 34, [P, TILES, 8])
    ge = c.at("decay_to_end", 34.25, [P, 8])
    St = c.at("state", 34.5, [P, 4, 64])
    SG = c.at("state_decayed", 35.5, [P, 4, 64])
    ka = c.at("k_a_vectors", 36.5, [P, 2, 4])
    half = c.at("half_biases", 36.625, [P, 16])
    rks = c.at("r_k_heads", 36.75, [P, 4, 8])
    mk = c.at("order_masks", 37, [P, 2, P])
    keep = c.at("chunk_starts", 0.75, [P, 512])
    m1 = c.at("neighbour_mask", 2.75, [P, P])
    m1T = c.at("neighbour_mask_turned", 3.25, [P, P])
    LB = c.at("L_b", 74, [P, 8, 2, P])
    LK = c.at("L_k", 82, [P, 8, 2, P])
    M = c.at("inverse", 90, [P, 8, P])
    MT = c.at("inverse_turned", 94, [P, 8, P])
    X = c.at("below_diagonal", 98, [P, 8, 64])
    tm = c.at("abk_rows", 100, [P, 3, 512])
    W1 = c.at("a_inverse", 106, [P, 4, P])
    LKV = c.at("L_k_v", 108, [P, 8, 64])
    P1 = c.at("from_values", 110, [P, 8, 64])
    Ub = c.at("U", 112, [P, 8, 64])
    w2 = c.at("lora_weights", 114, [64, 2, 512])
    lm = c.at("level_masks", 118, [P, 5, 64])
    DEC = float(np.exp(-0.5))
    load(c, [(keep[:], dram["const_chunk_starts"]),
             (w2[0:32], dram["decay_w2_2"][0].rearrange("a k n -> k a n")),
             (w2[32:64], dram["iclr_a2_2"][0].rearrange("a k n -> k a n"))])
    with stage(nc, "dve_step", "tanh_done") as (block, dve_step, tanh_done):
        @block.scalar
        def _(act):
            act.activation(rw[0:32, 12, :], rw[0:32, 12, :], ACT.Tanh).then_inc(tanh_done, 1)
            act.wait_ge(tanh_done, 1)

        @block.vector
        def _(dve):
            step = Step(dve, dve_step)
            step(dve.tensor_copy(ka[:, 0], vT[:, 84:88]),
                 dve.tensor_scalar(ka[:, 1], vT[:, 84:88], -1.0, 1.0, ALU.mult, ALU.add),
                 dve.tensor_scalar(half[:], vT[:, 64:80], 0.5, None, ALU.mult),
                 dve.memset(rks[:], 0.0), dve.memset(sc[:], 0.0))
            for h in range(8):
                r = slice(64 * (h % 2), 64 * (h % 2) + 64)
                step(dve.tensor_copy(rks[r, h // 2, h:h + 1], vT[r, 88 + h // 2:89 + h // 2]))
    for d in range(2):
        cm = dram["const_scan_masks"][d]
        load(c, [(mk[:], cm[:, 0:256].rearrange("p (a t) -> p a t", a=2)), (m1[:], cm[:, 256:384]),
                 (m1T[:], cm[:, 384:512]), (lm[:], cm[:, 512:832].rearrange("p (a t) -> p a t", a=5))])
        scan(c, d, list(range(NT)) if d == 0 else [1, 0] + list(range(NT - 1, 1, -1)), locals())

    hg = rw[0:96, 13, CTX:]
    sq = c.at("squares", 74, [P, TILES, 8, 64])
    lnw, lnb = c.at("lnx_w_rows", 90, [P, 512]), c.at("lnx_b_rows", 92, [P, 512])
    g2 = c.at("gate_g2", 94, [96, 512])
    st = c.at("stats", 96, [P, 3, TILES, 8])
    lneps = c.at("lnx_eps", 98, [P, 1])
    y4 = y[:].rearrange("p t (h e) -> p t h e", e=64)
    wide = lambda a: a.unsqueeze(3).to_broadcast([P, TILES, 8, 64])
    along = lambda a: a[:].unsqueeze(1).to_broadcast([P, TILES, 512])
    load(c, [(lnw[:], dram["lnx_w_2"][0].partition_broadcast(P)), (lnb[:], dram["lnx_b_2"][0].partition_broadcast(P)),
             (g2[:], dram["gate_g2_2"][0])])
    with stage(nc, "variance_ready", "root_ready", "gate_open", "gates_ready", "gated", "dve_step") as (
            block, variance, root, gate_open, gates_ready, gated, dve_step):
        @block.scalar
        def _(act):
            act.activation(hg, hg, ACT.Sigmoid).then_inc(gate_open, 1)
            act.wait_ge(variance, 1)
            act.activation(st[:, 1], st[:, 0], ACT.Sqrt, scale=1.0 / 64, bias=lneps[:, 0:1]).then_inc(root, 1)

        @block.tensor
        def _(pe):
            pe.wait_ge(gate_open, 1)
            for t in range(TILES):
                pe.matmul(ps[:, t, :], rw[0:96, 13, CTX + t * P:CTX + (t + 1) * P], g2[:], start=True, stop=True)\
                  .then_inc(gates_ready, 1)

        @block.vector
        def _(dve):
            step = Step(dve, dve_step)
            step(dve.memset(lneps[:], LNX_EPS))
            step(dve.tensor_reduce(st[:, 2], y4, AX.X, ALU.add))
            step(dve.tensor_scalar(st[:, 2], st[:, 2], 1.0 / 64, None, ALU.mult))
            step(dve.tensor_tensor(y4, y4, wide(st[:, 2]), ALU.subtract))
            step(dve.tensor_tensor(sq[:], y4, y4, ALU.mult))
            dve.tensor_reduce(st[:, 0], sq[:], AX.X, ALU.add).then_inc(variance, 1)
            dve.wait_ge(root, 1)
            step(dve.reciprocal(st[:, 2], st[:, 1]))
            step(dve.tensor_tensor(y4, y4, wide(st[:, 2]), ALU.mult),
                 dve.tensor_tensor(sq[:], vrow[:, 2:NT].rearrange("p t (h e) -> p t h e", e=64), wide(sc[:]), ALU.mult))
            step(dve.tensor_tensor(y[:], y[:], along(lnw), ALU.mult))
            step(dve.tensor_tensor(y[:], y[:], along(lnb), ALU.add))
            step(dve.tensor_tensor(y4, y4, sq[:], ALU.add))
            for t in range(TILES):
                dve.wait_ge(gates_ready, t + 1)
                dve.tensor_tensor(y[:, t], y[:, t], ps[:, t, :], ALU.mult).then_inc(gated, 1)
            dve.wait_ge(gated, TILES)
    return y


def scan(c, d, tiles, m):
    nc, ps = c.nc, c.psum
    (rw, vrow, y, lw, F, e1, e2, e3, rate, kd, ar, bt, kt, bb, kb, rk, sc, ge, St, SG, ka, half, rks, mk, keep, m1,
     m1T, LB, LK, M, MT, X, tm, W1, LKV, P1, Ub, w2, lm, kk, r_, k_, DEC) = (m[n] for n in (
         "rw vrow y lw F e1 e2 e3 rate kd ar bt kt bb kb rk sc ge St SG ka half rks mk keep m1 m1T LB LK M MT X tm "
         "W1 LKV P1 Ub w2 lm kk r_ k_ DEC").split())
    tok = lambda t: slice(t * P, (t + 1) * P)
    hp = lambda h: slice(64 * (h % 2), 64 * (h % 2) + 64)
    slot = lambda h: 4 * (h % 2) + h // 2
    order = (0, 1) if d == 0 else (1, 0)
    flat = lambda a: a[:].rearrange("p a b -> p (a b)")
    halves = lambda a: a[:].rearrange("p j (q n) -> p (j q) n", q=2)
    end = lambda a: a.unsqueeze(2).to_broadcast([P, 8, 64])

    def cols(a, level):
        n = 2 << level
        v = a.rearrange("p h (g two n) -> p h g two n", two=2, n=n)
        return v[:, :, :, d, :]

    def one_cols(a, level):
        n = 2 << level
        return a.rearrange("p (g two n) -> p g two n", two=2, n=n)[:, :, d, :]

    with stage(nc, "lora_done", "tanh_done", "logs_ready", "exps_ready", "scaled", "ends_scaled", "lb_done", "lk_done",
               "lb_masked", "lk_masked", "abk_turned", "abk_copied", "l_turned", "m_ready", "mt_started", "x_done",
               "x_masked", "m_done", "mt_turned", "mt_copied", "w1_done", "w1_copied", "lkv_done", "lkv_copied",
               "p1_done", "p1_copied", "u_done", "u_ready", "s_done", "state_ready", "y_done", "tile_done",
               "dve_step") as (
            block, lora_done, tanh_done, logs_ready, exps_ready, scaled, ends_scaled, lb_done, lk_done, lb_masked,
            lk_masked, abk_turned, abk_copied, l_turned, m_ready, mt_started, x_done, x_masked, m_done, mt_turned,
            mt_copied, w1_done, w1_copied, lkv_done, lkv_copied, p1_done, p1_copied, u_done, u_ready, s_done,
            state_ready, y_done, tile_done, dve_step):

        @block.tensor
        def _(pe):
            for i, t in enumerate(tiles):
                emit = t >= 2
                if i >= 1:
                    pe.wait_ge(tile_done, i)
                for bank, r in ((0, slice(0, 32)), (1, slice(32, 64))):
                    for j in range(4):
                        last = pe.matmul(ps[:, bank, j * P:(j + 1) * P], w2[r, d, j * P:(j + 1) * P],
                                         rw[r, 12, tok(t)], start=True, stop=True)
                last.then_inc(lora_done, 1)
                pe.wait_ge(scaled, i + 1)
                for h in range(8):
                    last = pe.matmul(ps[:, 2 + slot(h) // 2, (slot(h) % 2) * 256:(slot(h) % 2 + 1) * 256], bt[hp(h), h // 2],
                                     ar[hp(h), h // 2].rearrange("p a t -> p (a t)"), start=True, stop=True)
                last.then_inc(lb_done, 1)
                for h in range(8):
                    last = pe.matmul(ps[:, (6 + slot(h) // 2) % 8, (slot(h) % 2) * 256:(slot(h) % 2 + 1) * 256], kt[hp(h), h // 2],
                                     ar[hp(h), h // 2].rearrange("p a t -> p (a t)"), start=True, stop=True)
                last.then_inc(lk_done, 1)
                pe.wait_ge(lb_masked, i + 1)
                pe.wait_ge(ends_scaled, i + 1)
                for n, src in enumerate((ar[:, :, 0, :], bb, kb)):
                    for j in range(4):
                        last = pe.transpose(ps[:, 2 + n, j * P:(j + 1) * P], src[:, j], c.ident[:])
                last.then_inc(abk_turned, 1)
                pe.wait_ge(lk_masked, i + 1)
                for h in range(8):
                    last = pe.transpose(ps[:, 6 + h // 4, (h % 4) * P:(h % 4 + 1) * P], LB[:, h, 0, :], c.ident[:])
                last.then_inc(l_turned, 1)
                for h in range(8):
                    last = pe.matmul(ps[:, 5, slot(h) * 64:(slot(h) + 1) * 64], LK[:, slot(h), 0, :],
                                     vrow[:, t, h * 64:(h + 1) * 64], start=True, stop=True)
                last.then_inc(lkv_done, 1)
                pe.wait_ge(mt_started, i + 1)
                pe.wait_ge(abk_copied, i + 1)
                for level in range(5):
                    n = 5 * i + level
                    pe.wait_ge(m_ready, n + i + 1)
                    if level:
                        for h in range(8):
                            last = pe.transpose(ps[:, 2 + h // 4, (h % 4) * P:(h % 4 + 1) * P], M[:, h], c.ident[:])
                        last.then_inc(mt_turned, 1)
                    for h in range(8):
                        last = pe.matmul(ps[:, 0, h * 64:(h + 1) * 64], LB[:, h, 0, :], one_cols(M[:, h], level),
                                         start=True, stop=True)
                    last.then_inc(x_done, 1)
                    pe.wait_ge(x_masked, n + 1)
                    if level:
                        pe.wait_ge(mt_copied, n)
                    for h in range(8):
                        last = pe.matmul(ps[:, 1, h * 64:(h + 1) * 64], MT[:, h], X[:, h], start=True, stop=True)
                    last.then_inc(m_done, 1)
                pe.wait_ge(m_ready, 6 * i + 6)
                for h in range(8):
                    last = pe.transpose(ps[:, 2 + h // 4, (h % 4) * P:(h % 4 + 1) * P], M[:, h], c.ident[:])
                last.then_inc(mt_turned, 1)
                pe.wait_ge(mt_copied, 5 * i + 5)
                for h in range(8):
                    last = pe.matmul(ps[hp(h), 4, (h // 2) * P:(h // 2 + 1) * P], tm[:, 0, h * 64:(h + 1) * 64],
                                     MT[:, slot(h)], start=True, stop=True)
                last.then_inc(w1_done, 1)
                pe.wait_ge(lkv_copied, i + 1)
                for h in range(8):
                    last = pe.matmul(ps[:, 6, h * 64:(h + 1) * 64], MT[:, h], LKV[:, h], start=True, stop=True)
                last.then_inc(p1_done, 1)
                pe.wait_ge(w1_copied, i + 1)
                pe.wait_ge(p1_copied, i + 1)
                for q, cc in enumerate(order):
                    R = slice(64 * cc, 64 * cc + 64)
                    if 2 * i + q:
                        pe.wait_ge(state_ready, 2 * i + q)
                    for h in range(8):
                        last = pe.matmul(ps[R, 6 + h % 2, (h // 2) * 64:(h // 2 + 1) * 64], W1[hp(h), h // 2, R], St[hp(h), h // 2],
                                         start=True, stop=True)
                    last.then_inc(u_done, 1)
                    if emit:
                        for h in range(8):
                            pe.matmul(ps[R, 2 + h % 2, (h // 2) * 64:(h // 2 + 1) * 64], ar[hp(h), h // 2, 1, R], St[hp(h), h // 2],
                                      start=True, stop=True)
                    pe.wait_ge(u_ready, 2 * i + q + 1)
                    for h in range(8):
                        out = ps[hp(h), 1, (h // 2) * 64:(h // 2 + 1) * 64]
                        pe.matmul(out, tm[R, 1, h * 64:(h + 1) * 64], Ub[R, slot(h)], start=True, stop=False)
                        last = pe.matmul(out, tm[R, 2, h * 64:(h + 1) * 64], vrow[R, t, h * 64:(h + 1) * 64],
                                         start=False, stop=True)
                    last.then_inc(s_done, 1)
                if emit:
                    for h in range(8):
                        out = ps[:, 4, h * 64:(h + 1) * 64]
                        pe.matmul(out, LB[:, slot(h), 1, :], Ub[:, slot(h)], start=True, stop=False)
                        pe.matmul(out, LK[:, slot(h), 1, :], vrow[:, t, h * 64:(h + 1) * 64], start=False, stop=True)
                    for j in range(4):
                        last = pe.matmul(ps[:, 5, 0:8], rk[:, j], rks[:, j], start=(j == 0), stop=(j == 3))
                    last.then_inc(y_done, 1)

        @block.scalar
        def _(act):
            for i, t in enumerate(tiles):
                act.wait_ge(lora_done, i + 1)
                for bank, dst, b0 in ((0, lw, 0), (1, rate, 8)):
                    for j in range(4):
                        b = b0 + 4 * d + j
                        last = act.activation(dst[:, j], ps[:, bank, j * P:(j + 1) * P], ACT.Tanh, scale=0.5,
                                              bias=half[:, b:b + 1])
                last.then_inc(tanh_done, 1)
                act.wait_ge(logs_ready, i + 1)
                after = F if d == 0 else e1
                act.activation(e3[:], after[:], ACT.Exp, scale=-1.0)
                act.activation(e1[:], after[:], ACT.Exp)
                act.activation(e2[:], e2[:], ACT.Exp)
                act.activation(ge[:], halves(F)[:, :, 63], ACT.Exp).then_inc(exps_ready, 1)
                act.wait_ge(abk_turned, i + 1)
                act.activation(tm[:].rearrange("p a b -> p (a b)"), ps[:, 2:5, :].rearrange("p a b -> p (a b)"),
                               ACT.Copy).then_inc(abk_copied, 1)
                act.wait_ge(lkv_done, i + 1)
                act.activation(flat(LKV), ps[:, 5, :], ACT.Copy).then_inc(lkv_copied, 1)
                for level in range(5):
                    act.wait_ge(mt_turned, 5 * i + level + 1)
                    act.activation(flat(MT), ps[:, 2:4, :].rearrange("p a b -> p (a b)"), ACT.Copy)\
                       .then_inc(mt_copied, 1)
                act.wait_ge(w1_done, i + 1)
                act.activation(flat(W1), ps[:, 4, :], ACT.Copy).then_inc(w1_copied, 1)
                act.wait_ge(p1_done, i + 1)
                act.activation(flat(P1), ps[:, 6, :], ACT.Copy).then_inc(p1_copied, 1)

        @block.vector
        def _(dve):
            step = Step(dve, dve_step)
            step(dve.memset(St[:], 0.0))
            for i, t in enumerate(tiles):
                emit = t >= 2
                kkt, rt, kts = kk[:, :, tok(t)], r_[:, :, tok(t)], k_[:, :, tok(t)]
                dve.wait_ge(tanh_done, i + 1)
                step(dve.tensor_scalar(lw[:], lw[:], -DEC / 2, -DEC / 2, ALU.mult, ALU.add),
                     dve.tensor_scalar(rate[:], rate[:], 0.5, 0.5, ALU.mult, ALU.add))
                step(dve.tensor_tensor_scan(flat(F), keep[:], flat(lw), 0.0, ALU.mult, ALU.add))
                total = end(halves(F)[:, :, 63])
                if d == 0:
                    dve.tensor_tensor(e2[:], F[:], lw[:], ALU.subtract).then_inc(logs_ready, 1)
                else:
                    step(dve.tensor_tensor(halves(e2), total, halves(F), ALU.subtract))
                    dve.tensor_tensor(e1[:], e2[:], lw[:], ALU.add).then_inc(logs_ready, 1)
                step(*[dve.tensor_scalar(kd[:, j], rate[:, j], ka[:, 0, j:j + 1], ka[:, 1, j:j + 1], ALU.mult, ALU.add)
                       for j in range(4)], dve.tensor_tensor(bt[:], kkt, rate[:], ALU.mult))
                step(dve.tensor_tensor(kd[:], kd[:], kts, ALU.mult))
                dve.wait_ge(exps_ready, i + 1)
                step(dve.scalar_tensor_tensor(ar[:, :, 0, :], kkt, -1.0, e2[:], ALU.mult, ALU.mult),
                     dve.tensor_tensor(ar[:, :, 1, :], rt, e1[:], ALU.mult),
                     dve.tensor_tensor(bt[:], bt[:], e3[:], ALU.mult),
                     dve.tensor_tensor(rk[:], rt, kd[:], ALU.mult))
                dve.tensor_tensor(kt[:], kd[:], e3[:], ALU.mult).then_inc(scaled, 1)
                dve.wait_ge(scaled, i + 1)
                dve.tensor_tensor(halves(bb), halves(bt), end(ge[:]), ALU.mult)
                dve.tensor_tensor(halves(kb), halves(kt), end(ge[:]), ALU.mult).then_inc(ends_scaled, 1)
                masks = lambda n: mk[:].rearrange("p a t -> p (a t)").unsqueeze(1).to_broadcast([P, n, 256])
                dve.wait_ge(lb_done, i + 1)
                dve.tensor_tensor(LB[:].rearrange("p h a t -> p h (a t)"),
                                  ps[:, 2:6, :].rearrange("p b (h n) -> p (b h) n", h=2), masks(8), ALU.mult)\
                   .then_inc(lb_masked, 1)
                dve.wait_ge(lk_done, i + 1)
                for a, bank in ((0, 6), (4, 0)):
                    last = dve.tensor_tensor(LK[:, a:a + 4].rearrange("p h a t -> p h (a t)"),
                                             ps[:, bank:bank + 2, :].rearrange("p b (h n) -> p (b h) n", h=2),
                                             masks(4), ALU.mult)
                last.then_inc(lk_masked, 1)
                wide = lambda a: a.unsqueeze(1).to_broadcast([P, 8, a.shape[-1]])
                dve.wait_ge(lb_masked, i + 1)
                step(dve.tensor_tensor(MT[:], LB[:, :, 0, :], wide(m1T[:]), ALU.mult))
                dve.tensor_tensor(MT[:], MT[:], wide(c.ident[:]), ALU.add).then_inc(mt_started, 1)
                dve.wait_ge(l_turned, i + 1)
                step(dve.tensor_tensor(M[:], ps[:, 6:8, :].rearrange("p b (h n) -> p (b h) n", h=4), wide(m1[:]),
                                       ALU.mult))
                dve.tensor_tensor(M[:], M[:], wide(c.ident[:]), ALU.add).then_inc(m_ready, 1)
                for level in range(5):
                    n = 5 * i + level
                    dve.wait_ge(x_done, n + 1)
                    dve.tensor_tensor(X[:], ps[:, 0, :].rearrange("p (h n) -> p h n", h=8), wide(lm[:, level]),
                                      ALU.mult).then_inc(x_masked, 1)
                    dve.wait_ge(m_done, n + 1)
                    dve.wait_ge(m_ready, n + i + 1)
                    target = cols(M[:], level)
                    dve.tensor_tensor(target, target,
                                      ps[:, 1, :].rearrange("p (h g n) -> p h g n", h=8, n=2 << level), ALU.add)\
                       .then_inc(m_ready, 1)
                dve.wait_ge(p1_copied, i + 1)
                for q, cc in enumerate(order):
                    R = slice(64 * cc, 64 * cc + 64)
                    ends = ge[:].rearrange("p (j q) -> p j q", q=2)[:, :, cc].unsqueeze(2).to_broadcast([P, 4, 64])
                    step(dve.tensor_tensor(SG[:], St[:], ends, ALU.mult))
                    dve.wait_ge(u_done, 2 * i + q + 1)
                    dve.tensor_tensor(Ub[R].rearrange("p (a h) n -> p a (h n)", a=2), ps[R, 6:8, 0:256],
                                      P1[R].rearrange("p (a h) n -> p a (h n)", a=2), ALU.add)\
                       .then_inc(u_ready, 1)
                    dve.wait_ge(s_done, 2 * i + q + 1)
                    dve.tensor_tensor(St[:], ps[:, 1, 0:256].rearrange("p (j n) -> p j n", j=4), SG[:], ALU.add)\
                       .then_inc(state_ready, 1)
                    dve.wait_ge(state_ready, 2 * i + q + 1)
                if emit:
                    row = t - 2
                    by_half = y[:, row].rearrange("p (j a e) -> p a j e", a=2, e=64)
                    from_state = ps[:, 2:4, 0:256].rearrange("p a (j e) -> p a j e", e=64)
                    dve.wait_ge(y_done, sum(1 for s in tiles[:i + 1] if s >= 2))
                    if d == 0:
                        step(dve.tensor_copy(by_half, from_state),
                             dve.tensor_tensor(sc[:, row], sc[:, row], ps[:, 5, 0:8], ALU.add))
                    else:
                        step(dve.tensor_tensor(by_half, by_half, from_state, ALU.add),
                             dve.tensor_tensor(sc[:, row], sc[:, row], ps[:, 5, 0:8], ALU.add))
                    dve.tensor_tensor(y[:, row], y[:, row], ps[:, 4, :], ALU.add).then_inc(tile_done, 1)
                    dve.wait_ge(tile_done, i + 1)
                else:
                    dve.nop().then_inc(tile_done, 1)



def rope_tables():
    pos = np.arange(S, dtype=np.float32)
    inv = lambda theta, r: np.power(np.float32(theta), (-np.arange(r // 2, dtype=np.float32) * np.float32(2.0 / r)))
    angles = [pos[:, None] * inv(5e5, 16)[None], pos[:, None] * inv(5e5, 32)[None],
              (pos // 64)[:, None] * inv(1e4, 32)[None], (pos % 64)[:, None] * inv(1e4, 32)[None]]
    a = np.concatenate(angles, axis=1).astype(np.float32)
    return np.cos(a).astype(np.float32), np.sin(a).astype(np.float32)


def even_bias():
    dist = np.arange(1920)[None, :] - 896 - np.arange(P)[:, None]
    held = sum(((dist % dil == 0) & (abs(dist) <= win // 2)).astype(np.int64) for win, dil in
               ((128, 1), (512, 4), (2048, 16)))
    return np.where(held > 0, np.log(np.maximum(held, 1)) * HD ** 0.5, NEG).astype(np.float32)


def window_bias():
    q, k = np.arange(P)[:, None], np.arange(P)[None, :]
    before, after = np.where(k >= q, 0, NEG), np.where(k <= q, 0, NEG)
    opened = np.zeros((P, P))
    ctx = np.zeros((P, CTX))
    kinds = [np.concatenate([ctx, before, opened, after], 1), np.concatenate([ctx, opened, after, opened], 1)]
    return np.stack(kinds, 1).astype(np.float32)


def scan_masks():
    out = np.zeros((2, P, 832), np.float32)
    a, b = np.arange(P)[:, None], np.arange(P)[None, :]
    same = a // CHUNK == b // CHUNK
    out[0, :, 0:128], out[0, :, 128:256] = same & (a < b), same & (a <= b)
    out[1, :, 0:128], out[1, :, 128:256] = same & (a > b), same & (a >= b)
    out[0, :, 256:384] = (a % 2 == 1) & (b == a - 1)
    out[1, :, 256:384] = (a % 2 == 0) & (b == a + 1)
    for d in range(2):
        out[d, :, 384:512] = out[d, :, 256:384].T
    col = np.arange(64)
    for level in range(5):
        n = 2 << level
        for d in range(2):
            block = 2 * (col // n) + d
            out[d, :, 512 + 64 * level:576 + 64 * level] = a // n == (block + (1 if d == 0 else -1))[None, :]
    return out


def constants():
    cos, sin = rope_tables()
    starts = np.ones((P, 512), np.float32)
    starts[:, ::CHUNK] = 0
    half = np.arange(P) // 64
    return {"const_rope_cos": cos, "const_rope_sin": sin, "const_even_bias": even_bias(),
            "const_window_bias": window_bias(), "const_scan_masks": scan_masks(), "const_chunk_starts": starts,
            "const_head_blocks": (half[:, None] == half[None, :]).astype(np.float32),
            "const_identity": np.eye(P, dtype=np.float32)}


def build(nc, dram, out, dump=None, last=None, only=None):
    c = Chip(nc, dram)
    result_stored = nc.alloc_semaphore("result_stored")
    if dump:
        c.dump = lambda name, ap: dump(c, name, ap)
    c.ident = c.at("identity", 0, [P, P])
    c.eps = c.at("eps", 0.5, [P, 1])
    c.rope_cos = c.at("rope_cos", 0.75, [P, TILES, 56])
    c.rope_sin = c.at("rope_sin", 2.5, [P, TILES, 56])
    x = c.at("x", 6, [P, TILES, D])
    with stage(nc, "eps_set") as (block, eps_set):
        @block.gpsimd
        def _(pool):
            pool.memset(c.eps[:], EPS).then_inc(eps_set, 1)
            pool.wait_ge(eps_set, 1)
    load(c, [(c.ident[:], dram["const_identity"]), (x[:], dram["x"][0].rearrange("(t p) d -> p t d", p=P)),
             (c.rope_cos[:], dram["const_rope_cos"].rearrange("(t p) d -> p t d", p=P)),
             (c.rope_sin[:], dram["const_rope_sin"].rearrange("(t p) d -> p t d", p=P))])
    stages = [("even", lambda: even_mixer(c, x, dram["even_w_in"][0])), ("moe0", lambda: experts(c, x, 0)),
              ("odd", lambda: odd_mixer(c, x)), ("moe1", lambda: experts(c, x, 1)),
              ("final", lambda: norm_rows(c, x, x, TILES, dram["final_norm"], 102)),
              ("second", lambda: second_block(c, x))]
    for name, run in stages:
        if only and name != only:
            continue
        run()
        if c.dump:
            c.dump("x_" + name, x)
        if name == last:
            break
    rows = c.at("result_rows", 38, [P, TILES, D])
    norm_rows(c, x, rows, TILES, dram["norm_f_g_2"], 102)
    with nc.Block(no_gpsimd_drain=True) as block:
        @block.sync
        def _(sp):
            sp.dma_start(out[0].rearrange("(t p) d -> p t d", p=P), rows[:]).then_inc(result_stored, 16)
            sp.wait_ge(result_stored, 16)


def kernel(**inputs):
    import concourse.bacc as bacc
    from concourse.bass_utils import run_bass_kernel_spmd

    nc = bacc.Bacc("TRN2", target_bir_lowering=False, num_devices=1)
    arrays, dram = {}, {}
    for name, a in {**inputs, **constants()}.items():
        a = np.ascontiguousarray(a)
        arrays["in_" + name] = a
        dram[name] = nc.dram_tensor("in_" + name, a.shape, F32, kind="ExternalInput").ap()
    for name in ("h_scratch", "x_scratch"):
        dram[name] = nc.dram_tensor(name, (S, D), F32).ap()
    out = nc.dram_tensor("out", (1, S, D), F32, kind="ExternalOutput").ap()
    build(nc, dram, out)
    return run_bass_kernel_spmd(nc, [arrays], core_ids=[0]).results[0]["out"]
```

```python
from contextlib import ExitStack, contextmanager

import numpy as np

import concourse.bass as bass
from concourse import mybir

F32 = mybir.dt.float32
U32 = mybir.dt.uint32
ALU = mybir.AluOpType
ACT = mybir.ActivationFunctionType
AX = mybir.AxisListType

P = 128
D = 1024
S = 1024
TILES = S // P
KT = D // P
EPS = 1e-6
NEG = -1e30
HD = 64
BANK = 512
KB = 1024
ARENA = 16896

A_WIDTH, B_WIDTH, A_HEADS = 768, 256, 12
N_EXPERTS, CAP, FF = 16, 128, 512
CTX = 256
LNX_EPS = 1e-5 * 64
RW_CH = 4
T_ALL = CTX + S
CHUNK = 64


PHASES = 20
LAG = 10


class Stream:
    pass


class Step:

    def __init__(self, eng, sem):
        self.eng, self.sem, self.n = eng, sem, 0

    def __call__(self, *instructions):
        for i in instructions:
            i.then_inc(self.sem, 1)
            self.n += 1
        self.eng.wait_ge(self.sem, self.n)


STAGES = [0]


@contextmanager
def stage(nc, *names):
    STAGES[0] += 1
    sems = [nc.alloc_semaphore(f"{n}_s{STAGES[0]}") for n in names]
    with nc.Block(no_gpsimd_drain=True) as block:
        yield (block, *sems)
    nc.clear_and_free_semaphores(sems)
    nc.all_engine_barrier()


class Chip:

    def __init__(self, nc, dram):
        self.nc, self.dram, self.n = nc, dram, 0
        self.psum = nc.alloc_psum_tensor("psum", [P, 8, BANK], F32)
        self.dump = None

    def at(self, name, kb, shape, dt=F32):
        self.n += 1
        nbytes = int(np.prod(shape[1:])) * 4
        assert ARENA + kb * KB + nbytes <= 229344, (name, kb, shape)
        return self.nc.alloc_sbuf_tensor_at(f"{name}_{self.n}", shape, dt, offset=ARENA + int(kb * KB))


def bcast(ap, shape):
    return ap.to_broadcast(shape)



def load(c, pairs, small=False):
    with stage(c.nc, "tables_loaded") as (block, loaded):
        @block.sync
        def _(sp):
            for dst, src in pairs:
                sp.dma_start(dst, src, allow_slow_non_contiguous=small).then_inc(loaded, 16)
            sp.wait_ge(loaded, 16 * len(pairs))


def norm_rows(c, src, dst, tiles, gain, scr):
    nc = c.nc
    gain_b = c.at("gain_b", scr, [P, D])
    sq = c.at("squares", scr + 4, [P, 2, D])
    st = c.at("stats", scr + 12, [P, 3, tiles])
    with stage(nc, "gain_loaded", "squares_summed", "roots_taken", "rows_scaled", "dve_step") as (
            block, gain_loaded, summed, roots, scaled, dve_step):
        @block.sync
        def _(sp):
            sp.dma_start(gain_b[:], gain.partition_broadcast(P)).then_inc(gain_loaded, 16)
            sp.wait_ge(gain_loaded, 16)

        @block.scalar
        def _(act):
            for t in range(tiles):
                if t >= 2:
                    act.wait_ge(summed, t - 1)
                act.activation(sq[:, t % 2], src[:, t], ACT.Square, accum_out=st[:, 0, t:t + 1]).then_inc(summed, 1)
            act.wait_ge(summed, tiles)
            act.activation(st[:, 1], st[:, 0], ACT.Sqrt, scale=1.0 / D, bias=c.eps[:, 0:1]).then_inc(roots, 1)

        @block.vector
        def _(dve):
            step = Step(dve, dve_step)
            dve.wait_ge(roots, 1)
            step(dve.reciprocal(st[:, 2], st[:, 1]))
            dve.wait_ge(gain_loaded, 16)
            for t in range(tiles):
                dve.scalar_tensor_tensor(dst[:, t], src[:, t], st[:, 2, t:t + 1], gain_b[:],
                                         ALU.mult, ALU.mult).then_inc(scaled, 1)
            dve.wait_ge(scaled, tiles)


def transposes(c, groups):
    nc, ps = c.nc, c.psum
    n = len(groups)
    with stage(nc, "block_transposed", "act_copied", "dve_copied") as (block, done, act_copied, dve_copied):
        @block.tensor
        def _(pe):
            for i, (srcs, dst, _, _) in enumerate(groups):
                if i >= 8:
                    pe.wait_ge(act_copied if i % 2 else dve_copied, (i - 8) // 2 + 1)
                w = dst.shape[0]
                for j, s in enumerate(srcs):
                    last = pe.transpose(ps[0:w, i % 8, j * P:(j + 1) * P], s, c.ident[:])
                last.then_inc(done, 1)

        def copy(i, eng):
            srcs, dst, scale, shift = groups[i]
            w = dst.shape[0]
            src = ps[0:w, i % 8, 0:P * len(srcs)]
            eng.wait_ge(done, i + 1)
            if len(dst.shape) == 3:
                src = src.rearrange("p (a b) -> p a b", b=dst.shape[2])
            return src, dst, scale, shift

        @block.scalar
        def _(act):
            for i in range(1, n, 2):
                src, dst, scale, shift = copy(i, act)
                if scale is None:
                    act.activation(dst, src, ACT.Copy).then_inc(act_copied, 1)
                else:
                    act.activation(dst, src, ACT.Identity, bias=shift, scale=scale).then_inc(act_copied, 1)

        @block.vector
        def _(dve):
            for i in range(0, n, 2):
                src, dst, scale, shift = copy(i, dve)
                if scale is None:
                    dve.tensor_copy(dst, src).then_inc(dve_copied, 1)
                else:
                    dve.tensor_scalar(dst, src, scale, shift, ALU.mult, ALU.add).then_inc(dve_copied, 1)


def rows_to_cols(c, rows, cols, tiles, chunks, col0=0, scale=None, shift=None):
    groups = []
    for half in range(0, tiles, 4):
        m = min(4, tiles - half)
        for k in range(chunks):
            groups.append(([rows[:, t, col0 + k * P:col0 + (k + 1) * P] for t in range(half, half + m)],
                           cols[:, k, half * P:(half + m) * P],
                           None if scale is None else scale[:, k:k + 1],
                           None if shift is None else shift[:, k:k + 1]))
    transposes(c, groups)


def linear(c, kt, units, weights, ring, evacuate):
    nc, ps = c.nc, c.psum
    on_act, act_evacuate, dve_evacuate = evacuate
    before = {u: sum(1 for v in range(u) if on_act(v) == on_act(u)) for u in range(len(units))}
    last_use = {w: max(u for u, x in enumerate(units) if x[0] == w) for w in range(len(weights))}
    slots = len(ring)
    names = [f"weights_loaded_{i}" for i in range(slots)]
    with stage(nc, "unit_summed", "act_evacuated", "dve_evacuated", *names) as (
            block, summed, act_evac, dve_evac, *loaded):
        @block.sync
        def _(sp):
            for w, pairs in enumerate(weights):
                if w >= slots:
                    sp.wait_ge(summed, last_use[w - slots] + 1)
                dst, src = pairs(ring[w % slots])
                sp.dma_start(dst, src).then_inc(loaded[w % slots], 16)

        @block.tensor
        def _(pe):
            for u, (w, operands, shape) in enumerate(units):
                if weights:
                    pe.wait_ge(loaded[w % slots], 16 * (w // slots + 1))
                if u >= 8:
                    pe.wait_ge(act_evac if on_act(u - 8) else dve_evac, before[u - 8] + 1)
                out = ps[0:shape[0], u % 8, 0:shape[1]]
                for k in range(kt):
                    lhsT, rhs = operands(ring[w % slots], k)
                    last = pe.matmul(out, lhsT, rhs, start=(k == 0), stop=(k == kt - 1))
                last.then_inc(summed, 1)

        @block.scalar
        def _(act):
            for u, (_, _, shape) in enumerate(units):
                if on_act(u):
                    act.wait_ge(summed, u + 1)
                    act_evacuate(u, act, ps[0:shape[0], u % 8, 0:shape[1]]).then_inc(act_evac, 1)

        @block.vector
        def _(dve):
            for u, (_, _, shape) in enumerate(units):
                if not on_act(u):
                    dve.wait_ge(summed, u + 1)
                    dve_evacuate(u, dve, ps[0:shape[0], u % 8, 0:shape[1]]).then_inc(dve_evac, 1)


def linear_rows(c, cols, kt, w_dram, spans, ring_kb, slots, tiles, on_act, act_evac, dve_evac):
    ring = [c.at("weights", ring_kb + 2 * kt * i, [P, kt, BANK]) for i in range(slots)]
    w_rows = w_dram.rearrange("(k p) n -> p k n", p=P)
    weights, units = [], []
    for i, (a, b) in enumerate(spans):
        weights.append(lambda slot, a=a, b=b: (slot[:, :, 0:b - a], w_rows[:, :, a:b]))
        for t in range(tiles):
            units.append((i, lambda slot, k, t=t, a=a, b=b: (cols[:, k, t * P:(t + 1) * P], slot[:, k, 0:b - a]),
                          (P, b - a)))
    linear(c, kt, units, weights, ring, (
        lambda u: on_act(u // tiles),
        lambda u, act, psum: act_evac(u // tiles, u % tiles, act, psum),
        lambda u, dve, psum: dve_evac(u // tiles, u % tiles, dve, psum)))


def rope(step, dve, x1, x2, cos, sin, tmp):
    a, b, e, f = tmp
    step(dve.tensor_tensor(a, x1, cos, ALU.mult), dve.tensor_tensor(b, x2, sin, ALU.mult),
         dve.tensor_tensor(e, x1, sin, ALU.mult), dve.tensor_tensor(f, x2, cos, ALU.mult))
    step(dve.tensor_tensor(x1, a, b, ALU.subtract), dve.tensor_tensor(x2, e, f, ALU.add))


def attention(c, works, scale, tiles_kb, widths, sink=None):
    nc, ps = c.nc, c.psum
    n = len(works)
    biased = works[0][3] is not None
    at = lambda name, off, shape: c.at(name, tiles_kb + off, shape)
    s_b = at("scores", 0, [P, 2, 1024])
    p_b = at("probs", 8, [P, 2, 1024])
    pt_b = at("probs_turned", 16, [P, 2, 8, P])
    st = at("softmax_stats", 24, [P, 2, 8])
    with stage(nc, "scores_ready", "max_ready", "probs_ready", "probs_turned", "act_turned", "dve_turned",
               "weighted", "out_written", "dve_step", "sink_exp") as (
            block, scores_ready, max_ready, probs_ready, turned, act_turned, dve_turned, weighted,
            out_written, dve_step, sink_exp):
        S_ = lambda i: ps[:, 2 * (i % 2):2 * (i % 2) + 2, :].rearrange("p a b -> p (a b)")
        PT = lambda h: ps[:, 4 + h, :]
        O_ = lambda i: ps[:, 6 + i % 2, 0:HD]

        @block.tensor
        def _(pe):
            def scores(i):
                q, pieces, _, _, _, _ = works[i]
                if i >= 2:
                    pe.wait_ge(max_ready, i - 1)
                    pe.wait_ge(probs_ready, i - 1)
                for col, k in pieces:
                    last = pe.matmul(S_(i)[:, col:col + k.shape[-1]], q, k, start=True, stop=True)
                last.then_inc(scores_ready, 1)

            def turn(i):
                m = len(works[i][2])
                pe.wait_ge(probs_ready, i + 1)
                if i >= 1:
                    pe.wait_ge(act_turned, i)
                    pe.wait_ge(dve_turned, i)
                for j in range(m):
                    last = pe.transpose(PT(j // 4)[:, (j % 4) * P:(j % 4 + 1) * P],
                                        p_b[:, i % 2, j * P:(j + 1) * P], c.ident[:])
                last.then_inc(turned, 1)

            def weigh(i):
                v = works[i][2]
                pe.wait_ge(act_turned, i + 1)
                pe.wait_ge(dve_turned, i + 1)
                if i >= 2:
                    pe.wait_ge(out_written, i - 1)
                for j, vt in enumerate(v):
                    last = pe.matmul(O_(i), pt_b[:, i % 2, j, :], vt, start=(j == 0), stop=(j == len(v) - 1))
                last.then_inc(weighted, 1)

            scores(0)
            for i in range(n):
                if i + 1 < n:
                    scores(i + 1)
                if i >= 1:
                    weigh(i - 1)
                turn(i)
            weigh(n - 1)

        @block.scalar
        def _(act):
            def probs(i):
                w = widths(i)
                act.wait_ge(max_ready, i + 1)
                if i >= 2:
                    act.wait_ge(turned, i - 1)
                    act.wait_ge(out_written, i - 1)
                src = s_b[:, i % 2, 0:w] if biased else S_(i)[:, 0:w]
                if sink is not None:
                    act.activation(st[:, i % 2, 4:5], sink[1][:, works[i][5]:works[i][5] + 1], ACT.Exp,
                                   bias=st[:, i % 2, 1:2]).then_inc(sink_exp, 1)
                act.activation(p_b[:, i % 2, 0:w], src, ACT.Exp, bias=st[:, i % 2, 1:2], scale=scale,
                               accum_out=st[:, i % 2, 2:3]).then_inc(probs_ready, 1)

            probs(0)
            for i in range(n):
                if i + 1 < n:
                    probs(i + 1)
                act.wait_ge(turned, i + 1)
                if i >= 2:
                    act.wait_ge(weighted, i - 1)
                m = min(4, len(works[i][2]))
                act.activation(pt_b[:, i % 2, 0:m, :].rearrange("p a b -> p (a b)"), PT(0)[:, 0:m * P],
                               ACT.Copy).then_inc(act_turned, 1)

        @block.vector
        def _(dve):
            step = Step(dve, dve_step)

            def maxima(i):
                w = widths(i)
                dve.wait_ge(scores_ready, i + 1)
                if i >= 2:
                    dve.wait_ge(probs_ready, i - 1)
                if biased:
                    step(dve.tensor_tensor_reduce(s_b[:, i % 2, 0:w], S_(i)[:, 0:w], works[i][3], 1.0, NEG,
                                                  ALU.add, ALU.max, st[:, i % 2, 0:1]))
                else:
                    step(dve.tensor_reduce(st[:, i % 2, 0:1], S_(i)[:, 0:w], AX.X, ALU.max))
                if sink is not None:
                    k = works[i][5]
                    step(dve.tensor_tensor(st[:, i % 2, 0:1], st[:, i % 2, 0:1], sink[0][:, k:k + 1], ALU.max))
                dve.tensor_scalar(st[:, i % 2, 1:2], st[:, i % 2, 0:1], -scale, None, ALU.mult)\
                   .then_inc(max_ready, 1)

            def write(i):
                b = st[:, i % 2]
                dve.wait_ge(probs_ready, i + 1)
                if sink is not None:
                    dve.wait_ge(sink_exp, i + 1)
                    step(dve.tensor_tensor(b[:, 2:3], b[:, 2:3], b[:, 4:5], ALU.add))
                step(dve.reciprocal(b[:, 3:4], b[:, 2:3]))
                dve.wait_ge(weighted, i + 1)
                dve.tensor_scalar(works[i][4], O_(i), b[:, 3:4], None, ALU.mult).then_inc(out_written, 1)

            maxima(0)
            for i in range(n):
                if i + 1 < n:
                    maxima(i + 1)
                if i >= 1:
                    write(i - 1)
                dve.wait_ge(turned, i + 1)
                if i >= 2:
                    dve.wait_ge(weighted, i - 1)
                m = len(works[i][2])
                if m > 4:
                    dve.tensor_copy(pt_b[:, i % 2, 4:m, :].rearrange("p a b -> p (a b)"),
                                    PT(1)[:, 0:(m - 4) * P]).then_inc(dve_turned, 1)
                else:
                    dve.nop().then_inc(dve_turned, 1)
            write(n - 1)



def even_mixer(c, x, w):
    nc, dram = c.nc, c.dram
    hn = c.at("h_rows", 38 + 96, [P, TILES, D])
    hT = c.at("h_cols", 38, [P, KT, S])
    norm_rows(c, x, hn, TILES, dram["norm_mix"][0], 180)
    rows_to_cols(c, hn, hT, TILES, KT)
    qk = c.at("qk_rows", 118, [P, TILES, 2 * A_WIDTH])
    vz = c.at("vz_rows", 166, [P, TILES, A_WIDTH + 2 * B_WIDTH])
    v = lambda t, a, b: vz[:, t, a:b]
    spans = [(0, 512), (512, 1024), (1024, 1536), (1536, 2048), (2048, 2304), (2304, 2816)]

    def place(s, t):
        a, b = spans[s]
        return qk[:, t, a:b] if b <= 2 * A_WIDTH else vz[:, t, a - 2 * A_WIDTH:b - 2 * A_WIDTH]

    linear_rows(c, hT, KT, w, spans, 70, 3, TILES, lambda s: s == 5,
                lambda s, t, act, p: act.activation(place(s, t), p, ACT.Gelu_apprx_tanh),
                lambda s, t, dve, p: dve.tensor_copy(place(s, t), p))

    tmp = [c.at("rope_tmp", 70 + 6 * i, [P, TILES, 24, 8]) for i in range(4)]
    heads = qk[:].rearrange("p t (h e) -> p t h e", e=HD)
    with stage(nc, "dve_step") as (block, dve_step):
        @block.vector
        def _(dve):
            step = Step(dve, dve_step)
            cos = c.rope_cos[:, :, 0:8].unsqueeze(2).to_broadcast([P, TILES, 24, 8])
            sin = c.rope_sin[:, :, 0:8].unsqueeze(2).to_broadcast([P, TILES, 24, 8])
            rope(step, dve, heads[:, :, :, 0:8], heads[:, :, :, 8:16], cos, sin, [t[:] for t in tmp])
    qkT = c.at("qk_cols", 38, [P, 12, S])
    rows_to_cols(c, qk, qkT, TILES, 12)

    bias = c.at("window_bias", 86, [P, 1920])
    load(c, [(bias[:], dram["const_even_bias"])])
    ag = c.at("mix_rows", 118, [P, TILES, D])
    works = []
    for h in range(A_HEADS):
        r = slice(64 * (h % 2), 64 * (h % 2) + 64)
        for t in range(TILES):
            works.append((qkT[r, h // 2, t * P:(t + 1) * P],
                          [(0, qkT[r, 6 + h // 2, 0:512]), (512, qkT[r, 6 + h // 2, 512:1024])],
                          [vz[:, j, h * HD:(h + 1) * HD] for j in range(TILES)],
                          bias[:, 896 - 128 * t:896 - 128 * t + 1024], ag[:, t, h * HD:(h + 1) * HD], None))
    attention(c, works, HD ** -0.5, 94 - 0.5, lambda i: 1024)

    G = 4
    ws = c.at("w_spatial", 38, [P, G, P])
    wsT = c.at("w_spatial_turned", 40, [P, G, P])
    bs = c.at("b_spatial", 42, [P, G])
    gn = c.at("gmlp_gain", 42.5, [P, B_WIDTH])
    load(c, [(ws[:], dram["even_w_spatial"][0].rearrange("g p q -> p g q")),
             (bs[:], dram["even_b_spatial"][0].rearrange("g p -> p g")),
             (gn[:], dram["even_gmlp_norm"][0].rearrange("g c -> (g c)").partition_broadcast(P))], small=True)
    transposes(c, [([ws[:, g] for g in range(G)], wsT[:].rearrange("p g q -> p (g q)"), None, None)])
    vv = vz[:, :, A_WIDTH + B_WIDTH:A_WIDTH + 2 * B_WIDTH].rearrange("p t (g e) -> p t g e", e=64)
    u = vz[:, :, A_WIDTH:A_WIDTH + B_WIDTH]
    group_norm_rows(c, vv, gn[:].rearrange("p (g e) -> p g e", e=64).unsqueeze(1).to_broadcast([P, TILES, G, 64]),
                    TILES, G, 64, 44)
    ps = c.psum
    with stage(nc, "mixed", "gated") as (block, mixed, gated):
        @block.tensor
        def _(pe):
            for g in range(G):
                pe.matmul(ps[:, g, :].rearrange("p (t e) -> p t e", e=64), wsT[:, g], vv[:, :, g, :],
                          start=True, stop=True).then_inc(mixed, 1)

        @block.vector
        def _(dve):
            for g in range(G):
                dve.wait_ge(mixed, g + 1)
                dve.scalar_tensor_tensor(ag[:, :, A_WIDTH + g * 64:A_WIDTH + (g + 1) * 64],
                                         ps[:, g, :].rearrange("p (t e) -> p t e", e=64), bs[:, g:g + 1],
                                         u[:, :, g * 64:(g + 1) * 64], ALU.add, ALU.mult).then_inc(gated, 1)
    if c.dump:
        c.dump("g_out", ag)
    out_and_residual(c, x, ag, dram["even_w_out"][0], 38, 70)


def group_norm_rows(c, x, gain, tiles, groups, width, kb):
    sq = c.at("squares", kb, [P, tiles, groups, width])
    st = c.at("stats", kb + tiles * groups * width * 4 / KB, [P, 3, tiles, groups])
    with stage(c.nc, "sums_ready", "roots_ready", "dve_step") as (block, sums, roots, dve_step):
        @block.vector
        def _(dve):
            step = Step(dve, dve_step)
            step(dve.tensor_tensor(sq[:], x, x, ALU.mult))
            dve.tensor_reduce(st[:, 0], sq[:], AX.X, ALU.add).then_inc(sums, 1)
            dve.wait_ge(roots, 1)
            step(dve.reciprocal(st[:, 2], st[:, 1]))
            step(dve.tensor_tensor(x, x, st[:, 2].unsqueeze(3).to_broadcast([P, tiles, groups, width]), ALU.mult))
            step(dve.tensor_tensor(x, x, gain, ALU.mult))

        @block.scalar
        def _(act):
            act.wait_ge(sums, 1)
            act.activation(st[:, 1], st[:, 0], ACT.Sqrt, scale=1.0 / width, bias=c.eps[:, 0:1]).then_inc(roots, 1)


def out_and_residual(c, x, rows, w_dram, cols_kb, ring_kb):
    T = c.at("mix_cols", cols_kb, [P, KT, S])
    rows_to_cols(c, rows, T, TILES, KT)
    spans = [(0, 512), (512, 1024)]
    linear_rows(c, T, KT, w_dram, spans, ring_kb, 2, TILES, lambda s: False, None,
                lambda s, t, dve, p: dve.tensor_tensor(x[:, t, s * 512:(s + 1) * 512], p,
                                                       x[:, t, s * 512:(s + 1) * 512], ALU.add))



def experts(c, x, layer):
    nc, dram, ps = c.nc, c.dram, c.psum
    hn = c.at("h_rows", 38, [P, TILES, D])
    hT = c.at("h_cols", 70, [P, KT, S])
    norm_rows(c, x, hn, TILES, dram["norm_ffn"][layer], 102)
    rows_to_cols(c, hn, hT, TILES, KT)
    wr = c.at("w_router", 102, [P, KT, N_EXPERTS])
    lg = c.at("logits", 103, [P, TILES, N_EXPERTS])
    aff = c.at("affinity", 104, [N_EXPERTS, S])
    best = c.at("best_values", 108, [N_EXPERTS, CAP])
    besti = c.at("best_tokens", 109, [N_EXPERTS, CAP], U32)
    bestf = c.at("best_tokens_f", 110, [N_EXPERTS, CAP])
    sm = c.at("softmax_stats", 111, [P, 2, TILES])
    gates = c.at("gates", 4.5, [P, N_EXPERTS])
    tokens = c.at("tokens", 4.625, [P, N_EXPERTS], U32)
    h_dram, x_dram = dram["h_scratch"], dram["x_scratch"]
    with stage(nc, "stored", "router_loaded", "logits_ready", "max_off", "exp_ready", "aff_ready", "turned",
               "best_ready", "best_turned", "dve_step") as (
            block, stored, router_loaded, logits_ready, max_off, exp_ready, aff_ready, turned, best_ready,
            best_turned, dve_step):
        @block.sync
        def _(sp):
            sp.dma_start(wr[:], dram["moe_w_router"][layer].rearrange("(k p) e -> p k e", p=P))\
              .then_inc(router_loaded, 16)
            sp.dma_start(h_dram.rearrange("(t p) d -> p t d", p=P), hn[:]).then_inc(stored, 16)
            sp.dma_start(x_dram.rearrange("(t p) d -> p t d", p=P), x[:]).then_inc(stored, 16)
            sp.wait_ge(stored, 32)

        @block.tensor
        def _(pe):
            pe.wait_ge(router_loaded, 16)
            for t in range(TILES):
                for k in range(KT):
                    last = pe.matmul(ps[:, 0, t * 16:(t + 1) * 16], hT[:, k, t * P:(t + 1) * P], wr[:, k],
                                     start=(k == 0), stop=(k == KT - 1))
            last.then_inc(logits_ready, 1)
            pe.wait_ge(aff_ready, 1)
            for t in range(TILES):
                last = pe.transpose(ps[0:16, 1 + t // 4, (t % 4) * P:(t % 4 + 1) * P], lg[:, t], c.ident[:])
            last.then_inc(turned, 1)
            pe.wait_ge(best_ready, 1)
            pe.transpose(ps[:, 3, 0:16], best[:], c.ident[0:16, 0:16])
            pe.transpose(ps[:, 3, 16:32], bestf[:], c.ident[0:16, 0:16]).then_inc(best_turned, 1)

        @block.scalar
        def _(act):
            act.wait_ge(max_off, 1)
            act.activation(lg[:], lg[:], ACT.Exp).then_inc(exp_ready, 1)

        @block.vector
        def _(dve):
            step = Step(dve, dve_step)
            flat = ps[:, 0, 0:128].rearrange("p (t e) -> p t e", e=16)
            wide = lambda a: a.unsqueeze(2).to_broadcast([P, TILES, 16])
            dve.wait_ge(logits_ready, 1)
            step(dve.tensor_reduce(sm[:, 0], flat, AX.X, ALU.max))
            dve.tensor_tensor(lg[:], flat, wide(sm[:, 0]), ALU.subtract).then_inc(max_off, 1)
            dve.wait_ge(exp_ready, 1)
            step(dve.tensor_reduce(sm[:, 0], lg[:], AX.X, ALU.add))
            step(dve.reciprocal(sm[:, 1], sm[:, 0]))
            dve.tensor_tensor(lg[:], lg[:], wide(sm[:, 1]), ALU.mult).then_inc(aff_ready, 1)
            dve.wait_ge(turned, 1)
            step(dve.tensor_copy(aff[:], ps[0:16, 1:3, :].rearrange("p a b -> p (a b)")))
            for r in range(CAP // 8):
                b = best[:, r * 8:(r + 1) * 8]
                step(dve.max(b, aff[:]))
                step(dve.max_index(besti[:, r * 8:(r + 1) * 8], b, aff[:]))
                step(dve.match_replace(aff[:], b, aff[:], -1.0))
            dve.tensor_copy(bestf[:], besti[:]).then_inc(best_ready, 1)
            dve.wait_ge(best_turned, 1)
            step(dve.tensor_copy(gates[:], ps[:, 3, 0:16]), dve.tensor_copy(tokens[:], ps[:, 3, 16:32]))
    if c.dump:
        c.dump("gates", gates)

    NE = N_EXPERTS
    wg = c.at("w_gate", 38, [P, 2, KT, FF])
    wu = c.at("w_up", 70, [P, 2, KT, FF])
    wd = c.at("w_down", 102, [P, 2, 4, D])
    xs = c.at("picked", 134, [P, 2, D])
    xT = c.at("picked_cols", 142, [P, 2, KT, P])
    sg = c.at("silu_gate", 150, [P, 2, FF])
    ac = c.at("activated", 154, [P, 2, FF])
    aT = c.at("activated_cols", 158, [P, 2, 4, P])
    y = c.at("expert_out", 162, [P, 2, D])
    with stage(nc, "gate_up_loaded_0", "gate_up_loaded_1", "down_loaded_0", "down_loaded_1", "picked_0", "picked_1",
               "picked_turned", "picked_copied", "gate_up_done", "silu_done", "activated", "act_turned",
               "act_copied", "down_done", "scaled_dve", "scattered", "scaled_act") as (
            block, gu0, gu1, dn0, dn1, pk0, pk1, turned, copied, gate_up, silu, activated, aturned, acopied, down,
            scaled, scattered, scaled_act):
        gu, dn, pk = (gu0, gu1), (dn0, dn1), (pk0, pk1)

        @block.sync
        def _(sp):
            for e in range(NE):
                b = e % 2
                if e >= 2:
                    sp.wait_ge(gate_up, e - 1)
                sp.dma_start(wg[:, b], dram["moe_w_gate"][layer, e].rearrange("(k p) f -> p k f", p=P)).then_inc(gu[b], 16)
                sp.dma_start(wu[:, b], dram["moe_w_up"][layer, e].rearrange("(k p) f -> p k f", p=P)).then_inc(gu[b], 16)
                if e >= 2:
                    sp.wait_ge(down, e - 1)
                sp.dma_start(wd[:, b], dram["moe_w_down"][layer, e].rearrange("(k p) f -> p k f", p=P)).then_inc(dn[b], 16)

        @block.gpsimd
        def _(pool):
            def pick(e):
                if e >= 2:
                    pool.wait_ge(turned, e - 1)
                pool.indirect_dma_start(xs[:, e % 2], None, h_dram,
                                        bass.IndirectOffsetOnAxis(tokens[:, e:e + 1], 0)).then_inc(pk[e % 2], 16)

            pick(0)
            for e in range(NE):
                if e + 1 < NE:
                    pick(e + 1)
                pool.wait_ge(scaled, e + 1)
                pool.wait_ge(scaled_act, e + 1)
                if e >= 1:
                    pool.wait_ge(scattered, 16 * e)
                pool.indirect_dma_start(x_dram, bass.IndirectOffsetOnAxis(tokens[:, e:e + 1], 0), y[:, e % 2], None,
                                        compute_op=ALU.add).then_inc(scattered, 16)
            pool.wait_ge(scattered, 16 * NE)

        @block.tensor
        def _(pe):
            def turn(e):
                pe.wait_ge(pk[e % 2], 16 * (e // 2 + 1))
                if e >= 1:
                    pe.wait_ge(copied, 2 * e)
                for k in range(KT):
                    last = pe.transpose(ps[:, k // 4, (k % 4) * P:(k % 4 + 1) * P], xs[:, e % 2, k * P:(k + 1) * P],
                                        c.ident[:])
                last.then_inc(turned, 1)

            turn(0)
            for e in range(NE):
                b = e % 2
                pe.wait_ge(copied, 2 * e + 2)
                pe.wait_ge(gu[b], 32 * (e // 2 + 1))
                if e >= 1:
                    pe.wait_ge(activated, e)
                for bank, wt in ((2, wg), (3, wu)):
                    for k in range(KT):
                        last = pe.matmul(ps[:, bank, :], xT[:, b, k], wt[:, b, k], start=(k == 0), stop=(k == KT - 1))
                last.then_inc(gate_up, 1)
                if e + 1 < NE:
                    turn(e + 1)
                pe.wait_ge(activated, e + 1)
                if e >= 1:
                    pe.wait_ge(acopied, e)
                for k in range(4):
                    last = pe.transpose(ps[:, 4, k * P:(k + 1) * P], ac[:, b, k * P:(k + 1) * P], c.ident[:])
                last.then_inc(aturned, 1)
                pe.wait_ge(acopied, e + 1)
                pe.wait_ge(dn[b], 16 * (e // 2 + 1))
                if e >= 1:
                    pe.wait_ge(scaled, e)
                    pe.wait_ge(scaled_act, e)
                for half in range(2):
                    for k in range(4):
                        last = pe.matmul(ps[:, 5 + half, :], aT[:, b, k], wd[:, b, k, half * 512:(half + 1) * 512],
                                         start=(k == 0), stop=(k == 3))
                last.then_inc(down, 1)

        @block.scalar
        def _(act):
            for e in range(NE):
                b = e % 2
                act.wait_ge(gate_up, e + 1)
                if e >= 2:
                    act.wait_ge(activated, e - 1)
                act.activation(sg[:, b], ps[:, 2, :], ACT.Silu).then_inc(silu, 1)
                act.wait_ge(down, e + 1)
                if e >= 2:
                    act.wait_ge(scattered, 16 * (e - 1))
                act.activation(y[:, b, 512:1024], ps[:, 6, :], ACT.Copy, scale=gates[:, e:e + 1])\
                   .then_inc(scaled_act, 1)

        @block.vector
        def _(dve):
            def copy_rows(e):
                dve.wait_ge(turned, e + 1)
                if e >= 2:
                    dve.wait_ge(gate_up, e - 1)
                for h in range(2):
                    dve.tensor_copy(xT[:, e % 2, 4 * h:4 * h + 4].rearrange("p a b -> p (a b)"), ps[:, h, :])\
                       .then_inc(copied, 1)

            copy_rows(0)
            for e in range(NE):
                b = e % 2
                dve.wait_ge(silu, e + 1)
                if e >= 2:
                    dve.wait_ge(aturned, e - 1)
                dve.tensor_tensor(ac[:, b], sg[:, b], ps[:, 3, :], ALU.mult).then_inc(activated, 1)
                if e + 1 < NE:
                    copy_rows(e + 1)
                dve.wait_ge(aturned, e + 1)
                if e >= 2:
                    dve.wait_ge(down, e - 1)
                dve.tensor_copy(aT[:, b].rearrange("p a b -> p (a b)"), ps[:, 4, :]).then_inc(acopied, 1)
                dve.wait_ge(down, e + 1)
                if e >= 2:
                    dve.wait_ge(scattered, 16 * (e - 1))
                dve.tensor_scalar(y[:, b, 0:512], ps[:, 5, :], gates[:, e:e + 1], None, ALU.mult).then_inc(scaled, 1)
    load(c, [(x[:], x_dram.rearrange("(t p) d -> p t d", p=P))])



def odd_mixer(c, x):
    dram = c.dram
    hn = c.at("h_rows", 134, [P, TILES, D])
    hT = c.at("h_cols", 38, [P, KT, S])
    norm_rows(c, x, hn, TILES, dram["norm_mix"][1], 180)
    rows_to_cols(c, hn, hT, TILES, KT)
    low = c.at("latent_rows", 118, [P, TILES, 416])
    dqk = c.at("d_rows", 131, [P, TILES, 768])
    dv = c.at("dv_rows", 155, [P, TILES, 128])
    spans = [(0, 416), (416, 928), (928, 1184)]

    def copy_out(s, t, act, p):
        if s == 0:
            return act.activation(low[:, t], p, ACT.Copy)
        if s == 1:
            return act.activation(dqk[:, t, 0:512], p, ACT.Copy)
        act.activation(dqk[:, t, 512:640], p[:, 0:128], ACT.Copy)
        return act.activation(dv[:, t], p[:, 128:256], ACT.Copy)

    linear_rows(c, hT, KT, dram["odd_w_in"][0], spans, 70, 3, TILES, lambda s: True, copy_out, None)

    gains = c.at("norm_gains", 38, [P, 512])
    load(c, [(gains[:, 0:256], dram["odd_cq_norm"][0].partition_broadcast(P)),
             (gains[:, 256:384], dram["odd_ckv_norm"][0].partition_broadcast(P)),
             (gains[:, 384:448], dram["odd_dq_norm"][0].partition_broadcast(P)),
             (gains[:, 448:512], dram["odd_dk_norm"][0].partition_broadcast(P))])
    wide = lambda a, g, w: a.unsqueeze(1).unsqueeze(1).to_broadcast([P, TILES, g, w])
    group_norm_rows(c, low[:, :, 0:256].unsqueeze(2), wide(gains[:, 0:256], 1, 256), TILES, 1, 256, 40)
    group_norm_rows(c, low[:, :, 256:384].unsqueeze(2), wide(gains[:, 256:384], 1, 128), TILES, 1, 128, 40)
    heads = dqk[:].rearrange("p t (h e) -> p t h e", e=HD)
    group_norm_rows(c, heads[:, :, 0:8], wide(gains[:, 384:448], 8, 64), TILES, 8, 64, 40)
    group_norm_rows(c, heads[:, :, 8:10], wide(gains[:, 448:512], 2, 64), TILES, 2, 64, 40)
    tmp = [c.at("rope_tmp", 40 + 5 * i, [P, TILES, 10, 16]) for i in range(4)]
    table = lambda t, a, b, g: t[:, :, a:b].unsqueeze(2).to_broadcast([P, TILES, g, b - a])
    with stage(c.nc, "dve_step") as (block, dve_step):
        @block.vector
        def _(dve):
            step = Step(dve, dve_step)
            for off, a in ((0, 24), (32, 40)):
                rope(step, dve, heads[:, :, 0:10, off:off + 16], heads[:, :, 0:10, off + 16:off + 32],
                     table(c.rope_cos, a, a + 16, 10), table(c.rope_sin, a, a + 16, 10), [t[:] for t in tmp])
            kr = low[:, :, 384:416].unsqueeze(2)
            rope(step, dve, kr[:, :, :, 0:16], kr[:, :, :, 16:32], table(c.rope_cos, 8, 24, 1),
                 table(c.rope_sin, 8, 24, 1), [t[:, :, 0:1] for t in tmp])
            step(dve.tensor_copy(dqk[:, :, 640:704], dqk[:, :, 576:640]),
                 dve.tensor_copy(dqk[:, :, 704:768], dqk[:, :, 512:576]))

    mix = c.at("mix_rows", 175, [P, TILES, D])
    dT = c.at("d_cols", 38, [P, 6, S])
    rows_to_cols(c, dqk, dT, TILES, 6)
    works = []
    for h in range(8):
        r, kv = slice(64 * (h % 2), 64 * (h % 2) + 64), h // 4
        kc = 4 if h % 2 == kv else 5
        for t in range(TILES):
            works.append((dT[r, h // 2, t * P:(t + 1) * P], [(0, dT[r, kc, 0:512]), (512, dT[r, kc, 512:1024])],
                          [dv[:, j, kv * 64:(kv + 1) * 64] for j in range(TILES)], None,
                          mix[:, t, 512 + h * 64:512 + (h + 1) * 64], None))
    attention(c, works, HD ** -0.5, 62, lambda i: 1024)

    lowT = c.at("latent_cols", 38, [P, 3, S])
    rows_to_cols(c, low, lowT, TILES, 3)
    wq = c.at("w_cq_up", 50, [P, 2, 768])
    wkv = c.at("w_ckv_up", 56, [P, 1024])
    q = c.at("c_q_rows", 60, [P, TILES, 768])
    load(c, [(wq[:], dram["odd_w_cq_up"][0].rearrange("(k p) n -> p k n", p=P)), (wkv[:], dram["odd_w_ckv_up"][0])])
    linear(c, 2, [(0, lambda slot, k, t=t, h=h: (lowT[:, k, t * P:(t + 1) * P], wq[:, k, h * 384:(h + 1) * 384]), (P, 384))
                  for h in range(2) for t in range(TILES)], [], [None],
           (lambda u: True,
            lambda u, act, p: act.activation(q[:, u % 8, (u // 8) * 384:(u // 8 + 1) * 384], p, ACT.Copy), None))
    qr = q[:].rearrange("p t (h e) -> p t h e", e=96)
    tmp = [c.at("rope_tmp", 84 + 4 * i, [P, TILES, 8, 16]) for i in range(4)]
    with stage(c.nc, "dve_step") as (block, dve_step):
        @block.vector
        def _(dve):
            step = Step(dve, dve_step)
            rope(step, dve, qr[:, :, :, 64:80], qr[:, :, :, 80:96], table(c.rope_cos, 8, 24, 8),
                 table(c.rope_sin, 8, 24, 8), [t[:] for t in tmp])
    qT = c.at("c_q_cols", 143, [96, 8, S])
    transposes(c, [([q[:, t, h * 96:(h + 1) * 96] for t in range(a, a + 4)], qT[:, h, a * P:(a + 4) * P], None, None)
                   for a in (0, 4) for h in range(8)])
    vc = c.at("c_v_rows", 60, [P, TILES, 512])
    kc = c.at("c_k_rows", 76, [P, TILES, 768])
    kcr = kc[:].rearrange("p t (h e) -> p t h e", e=96)
    vcr = vc[:].rearrange("p t (h e) -> p t h e", e=64)

    def split_kv(u, dve, p):
        t, h = u % 8, u // 8
        p4 = p.rearrange("p (h e) -> p h e", e=128)
        dve.tensor_copy(kcr[:, t, 4 * h:4 * h + 4, 0:64], p4[:, :, 0:64])
        dve.tensor_copy(kcr[:, t, 4 * h:4 * h + 4, 64:96], low[:, t, 384:416].unsqueeze(1).to_broadcast([P, 4, 32]))
        return dve.tensor_copy(vcr[:, t, 4 * h:4 * h + 4, :], p4[:, :, 64:128])

    linear(c, 1, [(0, lambda slot, k, t=t, h=h: (lowT[:, 2, t * P:(t + 1) * P], wkv[:, h * 512:(h + 1) * 512]), (P, 512))
                  for h in range(2) for t in range(TILES)], [], [None], (lambda u: False, None, split_kv))
    kT = c.at("c_k_cols", 101, [96, 8, S])
    transposes(c, [([kc[:, t, h * 96:(h + 1) * 96] for t in range(a, a + 4)], kT[:, h, a * P:(a + 4) * P], None, None)
                   for a in (0, 4) for h in range(8)])
    works = [(qT[:, h, t * P:(t + 1) * P], [(0, kT[:, h, 0:512]), (512, kT[:, h, 512:1024])],
              [vc[:, j, h * 64:(h + 1) * 64] for j in range(TILES)], None, mix[:, t, h * 64:(h + 1) * 64], None)
             for h in range(8) for t in range(TILES)]
    attention(c, works, 96.0 ** -0.5, 76, lambda i: 1024)
    if c.dump:
        c.dump("odd_mix", mix)
    out_and_residual(c, x, mix, dram["odd_w_out"][0], 38, 70)



def second_block(c, x):
    nc, dram, ps = c.nc, c.dram, c.psum
    va, vb = c.at("vector_rows", 38, [P, P]), c.at("conv_rows", 38.5, [P, P])
    vT = c.at("vector_cols", 4.75, [P, 92])
    conv = c.at("conv_cols", 5.25, [P, 42])
    mod = c.at("modulation", 5.5, [P, 96])
    flat = lambda a: a.rearrange("(r p) -> r p", p=P)
    rows = [(0, flat(dram["b_ada_2"][0])), (48, flat(dram["c_2"][0])), (56, flat(dram["c_ctx_2"])),
            (64, dram["decay_w0_2"][0].rearrange("a (r p) -> (a r) p", p=P)),
            (72, dram["iclr_a0_2"][0].rearrange("a (r p) -> (a r) p", p=P)),
            (80, flat(dram["k_k_2"][0])), (84, flat(dram["k_a_2"][0])),
            (88, dram["r_k_2"][0].rearrange("(r a) e -> r (a e)", a=2))]
    with stage(nc, "cleared", "loaded", "turned", "copied") as (block, cleared, loaded, turned, copied):
        @block.gpsimd
        def _(pool):
            pool.memset(va[:], 0.0).then_inc(cleared, 1)
            pool.memset(vb[:], 0.0).then_inc(cleared, 1)

        @block.sync
        def _(sp):
            sp.wait_ge(cleared, 2)
            for r, src in rows:
                sp.dma_start(va[r:r + src.shape[0], :], src).then_inc(loaded, 16)
            for tap in range(3):
                cw = dram["conv_w_2"][0, tap]
                sp.dma_start(vb[14 * tap:14 * tap + 12, :], flat(cw[0:1536])).then_inc(loaded, 16)
                sp.dma_start(vb[14 * tap + 12:14 * tap + 13, 0:64], cw[1536:1600].unsqueeze(0)).then_inc(loaded, 16)
                sp.dma_start(vb[14 * tap + 13:14 * tap + 14, 0:96], cw[1600:1696].unsqueeze(0)).then_inc(loaded, 16)

        @block.tensor
        def _(pe):
            pe.wait_ge(loaded, 16 * (len(rows) + 9))
            pe.transpose(ps[:, 0, 0:P], va[:], c.ident[:])
            pe.transpose(ps[:, 1, 0:P], vb[:], c.ident[:]).then_inc(turned, 1)

        @block.vector
        def _(dve):
            dve.wait_ge(turned, 1)
            dve.tensor_copy(conv[:], ps[:, 1, 0:42])
            dve.tensor_copy(vT[:, 0:48], ps[:, 0, 0:48])
            dve.tensor_copy(vT[:, 64:92], ps[:, 0, 64:92]).then_inc(copied, 1)
            dve.wait_ge(copied, 1)

        @block.scalar
        def _(act):
            act.wait_ge(copied, 1)
            act.activation(vT[:, 48:64], ps[:, 0, 48:64], ACT.Silu).then_inc(copied, 1)
            act.wait_ge(copied, 2)

    cond = vT[:, 48:64].rearrange("p (a k) -> p k a", k=KT)
    w_ada = dram["w_ada_2"][0].rearrange("(k p) n -> p k n", p=P)
    ring = [c.at("weights", 38 + 16 * i, [P, KT, BANK]) for i in range(4)]
    linear(c, KT, [(u // 4, lambda slot, k, u=u: (slot[:, k, (u % 4) * P:(u % 4 + 1) * P], cond[:, k]), (P, 2))
                   for u in range(48)],
           [lambda slot, w=w: (slot[:], w_ada[:, :, w * BANK:(w + 1) * BANK]) for w in range(12)], ring,
           (lambda u: False, None,
            lambda u, dve, p: dve.tensor_scalar(mod[:, 2 * u:2 * u + 2], p, vT[:, u:u + 1], None, ALU.add)))
    mod3 = mod[:].rearrange("p (i k a) -> p i k a", i=6, k=KT)
    mods = c.at("modulation_scales", 5.875, [P, 3, KT])
    with stage(nc, "dve_step") as (block, dve_step):
        @block.vector
        def _(dve):
            step = Step(dve, dve_step)
            step(dve.tensor_scalar(mods[:, 0], mod3[:, 1, :, 0], 1.0, None, ALU.add),
                 dve.tensor_scalar(mods[:, 1], mod3[:, 1, :, 1], 1.0, None, ALU.add),
                 dve.tensor_scalar(mods[:, 2], mod3[:, 4, :, 0], 1.0, None, ALU.add))

    hn = c.at("h_rows", 134, [P, TILES, D])
    hT = c.at("h_cols", 38, [P, KT, S])
    norm_rows(c, x, hn, TILES, dram["norm1_g_2"][0], 180)
    rows_to_cols(c, hn, hT, TILES, KT, 0, mods[:, 0], mod3[:, 0, :, 0])
    xc, hcn = c.at("ctx_rows", 134, [P, 2, D]), c.at("h_ctx_rows", 142, [P, 2, D])
    hcT = c.at("h_ctx_cols", 70, [P, KT, CTX])
    load(c, [(xc[:], dram["ctx_2"][0].rearrange("(t p) d -> p t d", p=P))])
    norm_rows(c, xc, hcn, 2, dram["norm1_g_2"][0], 180)
    rows_to_cols(c, hcn, hcT, 2, KT, 0, mods[:, 1], mod3[:, 0, :, 1])
    if c.dump:
        c.dump("h2", hT)

    w_in = dram["w_in_2"][0]
    qk = c.at("qk_rows", 126, [P, TILES, 768])
    v = c.at("v_rows", 150, [P, 2 + TILES, 128])
    kx = c.at("ctx_k_rows", 155, [P, 2, 256])
    spans = [(0, 512), (512, 768)]

    def copy_out(s, t, act, p):
        if s == 0:
            return act.activation(qk[:, t, 0:512], p, ACT.Copy)
        act.activation(qk[:, t, 512:640], p[:, 0:128], ACT.Copy)
        return act.activation(v[:, 2 + t], p[:, 128:256], ACT.Copy)

    def copy_ctx(s, t, act, p):
        act.activation(kx[:, t, 0:128], p[:, 0:128], ACT.Copy)
        act.activation(kx[:, t, 128:192], p[:, 64:128], ACT.Copy)
        act.activation(kx[:, t, 192:256], p[:, 0:64], ACT.Copy)
        return act.activation(v[:, t], p[:, 128:256], ACT.Copy)

    linear_rows(c, hT, KT, w_in, spans, 78, 3, TILES, lambda s: True, copy_out, None)
    linear_rows(c, hcT, KT, w_in, [(512, 768)], 78, 3, 2, lambda s: True, copy_ctx, None)
    heads = qk[:].rearrange("p t (h e) -> p t h e", e=HD)
    tmp = [c.at("rope_tmp", 78 + 10 * i, [P, TILES, 10, 32]) for i in range(4)]
    table = lambda t: t[:, :, 24:56].unsqueeze(2).to_broadcast([P, TILES, 10, 32])
    with stage(nc, "stored", "dve_step") as (block, stored, dve_step):
        @block.sync
        def _(sp):
            sp.dma_start(dram["h_scratch"].rearrange("(k p) s -> p k s", p=P), hT[:]).then_inc(stored, 16)
            sp.dma_start(dram["x_scratch"].rearrange("(t p) d -> p t d", p=P), x[:]).then_inc(stored, 16)
            sp.wait_ge(stored, 32)

        @block.vector
        def _(dve):
            step = Step(dve, dve_step)
            rope(step, dve, heads[:, :, 0:10, 0:32], heads[:, :, 0:10, 32:64], table(c.rope_cos),
                 table(c.rope_sin), [t[:] for t in tmp])
            step(dve.tensor_copy(qk[:, :, 640:704], qk[:, :, 576:640]),
                 dve.tensor_copy(qk[:, :, 704:768], qk[:, :, 512:576]))
    qkT = c.at("qk_cols", 157, [P, 6, T_ALL])
    rows_to_cols(c, qk, qkT[:, :, CTX:], TILES, 6)
    rows_to_cols(c, kx, qkT[:, 4:6, 0:CTX], 2, 2)
    bias = c.at("window_bias", 103, [P, 2, 640])
    sinks = c.at("sinks", 108, [P, 2, 8])
    ya = c.at("ya_rows", 108.5, [P, TILES, 512])
    load(c, [(bias[:], dram["const_window_bias"]), (sinks[:, 1], dram["sink_2"][0].partition_broadcast(P))])
    with stage(nc, "dve_step") as (block, dve_step):
        @block.vector
        def _(dve):
            Step(dve, dve_step)(dve.tensor_scalar(sinks[:, 0], sinks[:, 1], float(HD) ** 0.5, None, ALU.mult))
    works = []
    for h in range(8):
        r, kv = slice(64 * (h % 2), 64 * (h % 2) + 64), h // 4
        kc = 4 if h % 2 == kv else 5
        for t in range(TILES):
            a, b = max(t - 1, 0), min(t + 2, TILES)
            n = (b - a) * P
            first = min(n, 256)
            pieces = [(0, qkT[r, kc, 0:CTX]), (CTX, qkT[r, kc, CTX + a * P:CTX + a * P + first])]
            if n > first:
                pieces.append((512, qkT[r, kc, CTX + a * P + first:CTX + b * P]))
            works.append((qkT[r, h // 2, CTX + t * P:CTX + (t + 1) * P], pieces,
                          [v[:, j, kv * 64:(kv + 1) * 64] for j in [0, 1] + list(range(2 + a, 2 + b))],
                          bias[:, 0 if t else 1, 0:CTX + n], ya[:, t, h * 64:(h + 1) * 64], h))
    attention(c, works, HD ** -0.5, 78, lambda i: works[i][3].shape[1], (sinks[:, 0], sinks[:, 1]))
    if c.dump:
        c.dump("ya", ya)
    yaT = c.at("ya_cols", 191, [P, 4, S])
    rows_to_cols(c, ya, yaT, TILES, 4)

    yr = rwkv(c, hT, hcT, w_in, conv, vT)
    if c.dump:
        c.dump("yr", yr)
    yrT = c.at("yr_cols", 169, [P, 4, S])
    rows_to_cols(c, yr, yrT, TILES, 4)
    load(c, [(hT[:], dram["h_scratch"].rearrange("(k p) s -> p k s", p=P)),
             (x[:], dram["x_scratch"].rearrange("(t p) d -> p t d", p=P))])

    W = 256
    NW = D // W
    wgt = c.at("gate_weights", 70, [P, 2, 2, KT, W])
    wbr = c.at("branch_weights", 102, [P, 2, 2, 4, W])
    m = c.at("merged_rows", 118, [P, TILES, D])
    sg = c.at("gates", 150, [P, 2, 2, W])
    pr = c.at("gated", 154, [P, 2, 2, W])
    gates_a = w_in[:, 2464:3488].rearrange("(k p) n -> p k n", p=P)
    gates_r = w_in[:, 3488:4512].rearrange("(k p) n -> p k n", p=P)
    wa = dram["w_branch_attn_2"][0].rearrange("(k p) n -> p k n", p=P)
    wr = dram["w_branch_rwkv_2"][0].rearrange("(k p) n -> p k n", p=P)
    with stage(nc, "weights_loaded_0", "weights_loaded_1", "products_ready", "sigmoids_ready", "branches_gated",
               "merged") as (block, l0, l1, products, sigmoids, gated, merged):
        loaded = (l0, l1)

        @block.sync
        def _(sp):
            for n in range(NW):
                if n >= 2:
                    sp.wait_ge(products, (n - 1) * TILES)
                cols = slice(n * W, (n + 1) * W)
                for dst, src in ((wgt[:, n % 2, 0], gates_a), (wgt[:, n % 2, 1], gates_r),
                                 (wbr[:, n % 2, 0], wa), (wbr[:, n % 2, 1], wr)):
                    sp.dma_start(dst, src[:, :, cols]).then_inc(loaded[n % 2], 16)

        @block.tensor
        def _(pe):
            for i in range(NW * TILES):
                n, t = divmod(i, TILES)
                pe.wait_ge(loaded[n % 2], 64 * (n // 2 + 1))
                if i >= 2:
                    pe.wait_ge(sigmoids, 2 * (i - 1))
                    pe.wait_ge(gated, i - 1)
                b, tok = 4 * (i % 2), slice(t * P, (t + 1) * P)
                for j in range(2):
                    for k in range(KT):
                        pe.matmul(ps[:, b + j, 0:W], hT[:, k, tok], wgt[:, n % 2, j, k], start=(k == 0),
                                  stop=(k == KT - 1))
                for j, y in enumerate((yaT, yrT)):
                    for k in range(4):
                        last = pe.matmul(ps[:, b + 2 + j, 0:W], y[:, k, tok], wbr[:, n % 2, j, k], start=(k == 0),
                                         stop=(k == 3))
                last.then_inc(products, 1)

        @block.scalar
        def _(act):
            for i in range(NW * TILES):
                act.wait_ge(products, i + 1)
                if i >= 2:
                    act.wait_ge(gated, i - 1)
                for j in range(2):
                    act.activation(sg[:, i % 2, j], ps[:, 4 * (i % 2) + j, 0:W], ACT.Sigmoid).then_inc(sigmoids, 1)

        @block.vector
        def _(dve):
            for i in range(NW * TILES):
                n, t = divmod(i, TILES)
                dve.wait_ge(sigmoids, 2 * i + 2)
                if i >= 2:
                    dve.wait_ge(merged, i - 1)
                dve.tensor_tensor(pr[:, i % 2], sg[:, i % 2], ps[:, 4 * (i % 2) + 2:4 * (i % 2) + 4, 0:W],
                                  ALU.mult).then_inc(gated, 1)
                dve.wait_ge(gated, i + 1)
                dve.tensor_tensor(m[:, t, n * W:(n + 1) * W], pr[:, i % 2, 0], pr[:, i % 2, 1], ALU.add)\
                   .then_inc(merged, 1)
            dve.wait_ge(merged, NW * TILES)

    mT = c.at("merged_cols", 38, [P, KT, S])
    rows_to_cols(c, m, mT, TILES, KT)
    g1, g2 = c.at("gate1_rows", 102, [P, D]), c.at("gate2_rows", 106, [P, D])
    spread = c.at("gate_spread", 110, [P, 2, KT, P])
    for j, (g, i) in enumerate(((g1, 2), (g2, 5))):
        with stage(nc, "spread_out") as (block, spread_out):
            @block.vector
            def _(dve):
                dve.tensor_copy(spread[:, j], mod3[:, i, :, 0].unsqueeze(2).to_broadcast([P, KT, P]))\
                   .then_inc(spread_out, 1)
                dve.wait_ge(spread_out, 1)
        transposes(c, [([spread[:, j, k] for k in range(a, a + 4)], g[:, a * P:(a + 4) * P], None, None)
                       for a in (0, 4)])
    gt = c.at("gated_out", 118, [P, 2, BANK])
    with ExitStack():
        counter = c.nc.alloc_semaphore("gated_out_ready")

        def add_gated(s, t, dve, p):
            u = s * TILES + t
            cols = slice(s * 512, (s + 1) * 512)
            dve.tensor_tensor(gt[:, u % 2], p, g1[:, cols], ALU.mult).then_inc(counter, 1)
            dve.wait_ge(counter, u + 1)
            return dve.tensor_tensor(x[:, t, cols], x[:, t, cols], gt[:, u % 2], ALU.add)

        linear_rows(c, mT, KT, dram["w_out_2"][0], [(0, 512), (512, 1024)], 70, 2, TILES, lambda s: False, None,
                    add_gated)
        c.nc.clear_and_free_semaphores([counter])
        c.nc.all_engine_barrier()
    if c.dump:
        c.dump("x_merge", x)

    g2k = c.at("gate2_rows_kept", 200, [P, D])
    with stage(nc, "moved") as (block, moved):
        @block.vector
        def _(dve):
            dve.tensor_copy(g2k[:], g2[:]).then_inc(moved, 1)
            dve.wait_ge(moved, 1)
    norm_rows(c, x, hn, TILES, dram["norm2_g_2"][0], 180)
    rows_to_cols(c, hn, hT, TILES, KT, 0, mods[:, 2], mod3[:, 3, :, 0])
    wu = c.at("w_up", 70, [P, 2, KT, 512])
    wd = c.at("w_down", 102, [P, 2, 4, D])
    aT = c.at("hidden_cols", 134, [P, 2, 4, S])
    acc = c.at("mlp_rows", 166, [P, TILES, D])
    rl = c.at("relu", 198, [P, 1, 512])
    mlp(c, x, hT, wu, wd, aT, acc, rl, g2k)


def mlp(c, x, hT, wu, wd, aT, acc, rl, gate):
    nc, dram, ps = c.nc, c.dram, c.psum
    steps = 4 * D // 512
    w_up = dram["w_mlp_up_2"][0].rearrange("(k p) n -> p k n", p=P)
    w_down = dram["w_mlp_down_2"][0].rearrange("(s k p) n -> s p k n", p=P, k=4)
    with stage(nc, "up_loaded_0", "up_loaded_1", "down_loaded_0", "down_loaded_1", "up_done", "relu_done",
               "squared", "down_done", "added", "dve_step") as (
            block, u0, u1, d0, d1, up_done, relu_done, squared, down_done, added, dve_step):
        up_loaded, down_loaded = (u0, u1), (d0, d1)

        @block.sync
        def _(sp):
            for s in range(steps):
                if s >= 2:
                    sp.wait_ge(up_done, 8 * (s - 1))
                sp.dma_start(wu[:, s % 2], w_up[:, :, s * 512:(s + 1) * 512]).then_inc(up_loaded[s % 2], 16)
                if s >= 2:
                    sp.wait_ge(down_done, 16 * (s - 1))
                sp.dma_start(wd[:, s % 2], w_down[s]).then_inc(down_loaded[s % 2], 16)

        @block.tensor
        def _(pe):
            def up(s):
                pe.wait_ge(up_loaded[s % 2], 16 * (s // 2 + 1))
                for i in range(8):
                    u = 8 * s + i
                    if u >= 4:
                        pe.wait_ge(relu_done, u - 3)
                    f, half = i // 2, i % 2
                    for k in range(KT):
                        last = pe.matmul(ps[:, i % 4, :], wu[:, s % 2, k, f * P:(f + 1) * P],
                                         hT[:, k, half * 512:(half + 1) * 512], start=(k == 0), stop=(k == KT - 1))
                    last.then_inc(up_done, 1)

            def down(s):
                pe.wait_ge(squared, 8 * (s + 1))
                pe.wait_ge(down_loaded[s % 2], 16 * (s // 2 + 1))
                for i in range(16):
                    u = 16 * s + i
                    if u >= 4:
                        pe.wait_ge(added, u - 3)
                    t, half = i // 2, i % 2
                    for k in range(4):
                        last = pe.matmul(ps[:, 4 + i % 4, :], aT[:, s % 2, k, t * P:(t + 1) * P],
                                         wd[:, s % 2, k, half * 512:(half + 1) * 512], start=(k == 0), stop=(k == 3))
                    last.then_inc(down_done, 1)

            up(0)
            for s in range(steps):
                if s + 1 < steps:
                    up(s + 1)
                down(s)

        @block.scalar
        def _(act):
            for s in range(steps):
                for i in range(8):
                    u = 8 * s + i
                    act.wait_ge(up_done, u + 1)
                    if u >= 1:
                        act.wait_ge(squared, u)
                    act.activation(rl[:, 0], ps[:, i % 4, :], ACT.Relu).then_inc(relu_done, 1)
                    act.wait_ge(relu_done, u + 1)
                    if s >= 2:
                        act.wait_ge(down_done, 16 * (s - 1))
                    act.activation(aT[:, s % 2, i // 2, (i % 2) * 512:(i % 2 + 1) * 512], rl[:, 0],
                                   ACT.Square).then_inc(squared, 1)

        @block.vector
        def _(dve):
            for s in range(steps):
                for i in range(16):
                    u = 16 * s + i
                    t, cols = i // 2, slice((i % 2) * 512, (i % 2 + 1) * 512)
                    dve.wait_ge(down_done, u + 1)
                    if s == 0:
                        dve.tensor_copy(acc[:, t, cols], ps[:, 4 + i % 4, :]).then_inc(added, 1)
                    else:
                        dve.wait_ge(added, u - 15)
                        dve.tensor_tensor(acc[:, t, cols], acc[:, t, cols], ps[:, 4 + i % 4, :], ALU.add)\
                           .then_inc(added, 1)
            dve.wait_ge(added, 16 * steps)
            step = Step(dve, dve_step)
            step(dve.tensor_tensor(acc[:], acc[:], gate[:].unsqueeze(1).to_broadcast([P, TILES, D]), ALU.mult))
            step(dve.tensor_tensor(x[:], x[:], acc[:], ALU.add))



def rwkv(c, hT, hcT, w_in, conv, vT):
    nc, dram, ps = c.nc, c.dram, c.psum
    widths = [P] * 12 + [64, 96]
    starts = [768 + P * j for j in range(12)] + [768 + 1536, 768 + 1600]
    U0, U1 = 1, CTX + 2
    ub = c.at("conv_in", 110, [P, 2, T_ALL + 3])
    rw = c.at("rwkv_cols", 120.5, [P, 14, T_ALL])
    ring = [c.at("weights", 78 + 16 * i, [P, KT, BANK]) for i in range(2)]
    rw_w = w_in[:, 768:2464].rearrange("(k p) n -> p k n", p=P)
    cuts = [(0, 512), (512, 1024), (1024, 1536), (1536, 1696)]
    parts = [(0, CTX, U0), (0, 512, U1), (512, 1024, U1 + 512)]
    with stage(nc, "weights_loaded_0", "weights_loaded_1", "edges_cleared", "summed", "copied", "convolved",
               "dve_step") as (block, l0, l1, edges, summed, copied, convolved, dve_step):
        loaded = (l0, l1)

        @block.sync
        def _(sp):
            for w, (a, b) in enumerate(cuts):
                if w >= 2:
                    sp.wait_ge(summed, 3 * 4 * (w - 1))
                sp.dma_start(ring[w % 2][:, :, 0:b - a], rw_w[:, :, a:b]).then_inc(loaded[w % 2], 16)

        @block.gpsimd
        def _(pool):
            for col in (0, CTX + 1, T_ALL + 2):
                pool.memset(ub[:, :, col:col + 1], 0.0).then_inc(edges, 1)

        @block.tensor
        def _(pe):
            for j in range(14):
                w = j // 4
                pe.wait_ge(loaded[w % 2], 16 * (w // 2 + 1))
                o = starts[j] - 768 - 512 * w
                for i, (a, b, _) in enumerate(parts):
                    u = 3 * j + i
                    if u >= 6:
                        pe.wait_ge(copied, u - 5)
                    for k in range(KT):
                        rhs = hcT[:, k, a:b] if i == 0 else hT[:, k, a:b]
                        last = pe.matmul(ps[0:widths[j], u % 6, 0:b - a], ring[w % 2][:, k, o:o + widths[j]], rhs,
                                         start=(k == 0), stop=(k == KT - 1))
                    last.then_inc(summed, 1)

        @block.scalar
        def _(act):
            for j in range(14):
                if j >= 2:
                    act.wait_ge(convolved, j - 1)
                for i, (a, b, o) in enumerate(parts):
                    u = 3 * j + i
                    act.wait_ge(summed, u + 1)
                    act.activation(ub[0:widths[j], j % 2, o:o + b - a], ps[0:widths[j], u % 6, 0:b - a], ACT.Copy)\
                       .then_inc(copied, 1)

        @block.vector
        def _(dve):
            step = Step(dve, dve_step)
            dve.wait_ge(edges, 3)
            for j in range(14):
                dve.wait_ge(copied, 3 * j + 3)
                n = widths[j]
                tap = lambda i: conv[0:n, 14 * i + j:14 * i + j + 1]
                for s, (o, n_tok, d) in enumerate(((U0, CTX, 0), (U1, S, CTX))):
                    u, out = ub[0:n, j % 2], rw[0:n, j, d:d + n_tok]
                    step(dve.tensor_scalar(out, u[:, o - 1:o - 1 + n_tok], tap(0), None, ALU.mult))
                    step(dve.scalar_tensor_tensor(out, u[:, o:o + n_tok], tap(1), out, ALU.mult, ALU.add))
                    step(dve.scalar_tensor_tensor(out, u[:, o + 1:o + 1 + n_tok], tap(2), out, ALU.mult, ALU.add))
                dve.nop().then_inc(convolved, 1)
    if c.dump:
        c.dump("rw", rw[:, 0:12])

    NT = T_ALL // P
    vrow = c.at("v_rows", 38, [P, NT, 512])
    rows = []
    for a in range(0, NT, 4):
        n = min(4, NT - a)
        for j in range(4):
            for t in range(a, a + n):
                rows.append(([rw[:, 8 + j, t * P:(t + 1) * P]], vrow[:, t, j * P:(j + 1) * P], None, None))
    transposes(c, rows)

    kk = rw[:, 8:12, :]
    r_, k_ = rw[:, 0:4, :], rw[:, 4:8, :]
    sq = c.at("kk_squares", 58, [P, 4, T_ALL])
    blocks = c.at("head_blocks", 98, [P, P])
    load(c, [(blocks[:], dram["const_head_blocks"])])
    with stage(nc, "squared", "summed", "rooted", "dve_step", "normalised") as (
            block, squared, summed, rooted, dve_step, normalised):
        pieces = [(j, a, min(a + 512, T_ALL)) for j in range(4) for a in range(0, T_ALL, 512)]

        @block.vector
        def _(dve):
            step = Step(dve, dve_step)
            step(*[dve.tensor_scalar(kk[:, j], k_[:, j], vT[:, 80 + j:81 + j], None, ALU.mult) for j in range(4)])
            dve.tensor_tensor(sq[:], kk, kk, ALU.mult).then_inc(squared, 1)
            for i, (j, a, b) in enumerate(pieces):
                dve.wait_ge(summed, i + 1)
                dve.tensor_scalar(sq[:, j, a:b], ps[:, i % 8, 0:b - a], 1e-24, None, ALU.max).then_inc(normalised, 1)
            dve.wait_ge(rooted, 1)
            step(dve.reciprocal(sq[:], sq[:]))
            step(dve.tensor_tensor(kk, kk, sq[:], ALU.mult))

        @block.tensor
        def _(pe):
            pe.wait_ge(squared, 1)
            for i, (j, a, b) in enumerate(pieces):
                if i >= 8:
                    pe.wait_ge(normalised, i - 7)
                pe.matmul(ps[:, i % 8, 0:b - a], blocks[:], sq[:, j, a:b], start=True, stop=True).then_inc(summed, 1)

        @block.scalar
        def _(act):
            act.wait_ge(normalised, len(pieces))
            act.activation(sq[:], sq[:], ACT.Sqrt).then_inc(rooted, 1)
    if c.dump:
        c.dump("kk", rw[:, 8:12])

    lora = rw[:, 12, :]
    y = c.at("y_rows", 58, [P, TILES, 512])
    sc = c.at("bonus_rows", 34, [P, TILES, 8])
    ka = c.at("k_a_vectors", 36.5, [P, 2, 4])
    half = c.at("half_biases", 36.625, [P, 16])
    rks = c.at("r_k_heads", 36.75, [P, 4, 8])
    mk = c.at("order_masks", 37, [P, 2, 64])
    keep = c.at("chunk_starts", 0.75, [P, 512])
    m1 = c.at("neighbour_mask", 2.75, [P, 64])
    m1T = c.at("neighbour_mask_turned", 3, [P, 64])
    eye = c.at("chunk_identity", 3.25, [P, 64])
    lm = c.at("level_masks", 3.5, [P, 5, 32])
    w2 = c.at("lora_weights", 114, [64, 2, 512])
    streams = []
    for g in (0, 1):
        b = Stream()
        (b.lw, b.F, b.e1, b.e2, b.e3, b.rate, b.kd, b.bt, b.kt, b.bb, b.kb, b.rk) = (
            c.at(name, 6 + 14 * g + n, [P, 2, P]) for n, name in enumerate((
                "log_decay", "running_log", "exp_after", "exp_before", "exp_inverse", "rate", "key", "b_scaled",
                "k_scaled", "b_to_end", "k_to_end", "r_times_key")))
        b.ar = c.at("a_and_r", 18 + 14 * g, [P, 2, 2, P])
        H = 74 + 14.625 * g
        b.LL = c.at("pairs", H, [P, 2, 2, 2, 2, 64])
        b.M = c.at("inverse", H + 4, [P, 4, 64])
        b.MT = c.at("inverse_turned", H + 5, [P, 4, 64])
        b.X = c.at("below_diagonal", H + 6, [P, 4, 32])
        b.tm = c.at("abk_rows", H + 6.5, [P, 3, 256])
        b.W1 = c.at("a_inverse", H + 9.5, [P, 2, 2, 64])
        b.LKV = c.at("L_k_v", H + 10.5, [P, 4, 64])
        b.P1 = c.at("from_values", H + 11.5, [P, 4, 64])
        b.U = c.at("U", H + 12.5, [P, 4, 64])
        b.S = c.at("state", H + 13.5, [P, 2, 64])
        b.SG = c.at("state_decayed", H + 14, [P, 2, 64])
        b.ge = c.at("decay_to_end", H + 14.5, [P, 4])
        streams.append(b)
    DEC = float(np.exp(-0.5))
    load(c, [(keep[:], dram["const_chunk_starts"]), (eye[:], dram["const_chunk_identity"])])
    with stage(nc, "dve_step", "tanh_done") as (block, dve_step, tanh_done):
        @block.scalar
        def _(act):
            act.activation(rw[0:32, 12, :], rw[0:32, 12, :], ACT.Tanh).then_inc(tanh_done, 1)
            act.wait_ge(tanh_done, 1)

        @block.vector
        def _(dve):
            step = Step(dve, dve_step)
            step(dve.tensor_copy(ka[:, 0], vT[:, 84:88]),
                 dve.tensor_scalar(ka[:, 1], vT[:, 84:88], -1.0, 1.0, ALU.mult, ALU.add),
                 dve.tensor_scalar(half[:], vT[:, 64:80], 0.5, None, ALU.mult),
                 dve.memset(rks[:], 0.0), dve.memset(sc[:], 0.0), dve.memset(w2[:], 0.0))
            for h in range(8):
                r = slice(64 * (h % 2), 64 * (h % 2) + 64)
                step(dve.tensor_copy(rks[r, h // 2, h:h + 1], vT[r, 88 + h // 2:89 + h // 2]))
    for d in range(2):
        cm = dram["const_scan_masks"][d]
        load(c, [(mk[:], cm[:, 0:128].rearrange("p (a t) -> p a t", a=2)), (m1[:], cm[:, 128:192]),
                 (m1T[:], cm[:, 192:256]), (lm[:], cm[:, 256:416].rearrange("p (a t) -> p a t", a=5)),
                 (w2[0:32, 0], dram["decay_w2_2"][0, d]), (w2[32:64, 1], dram["iclr_a2_2"][0, d])])
        scan(c, d, list(range(NT)) if d == 0 else [1, 0] + list(range(NT - 1, 1, -1)), locals())

    hg = rw[0:96, 13, CTX:]
    sq = c.at("squares", 74, [P, TILES, 8, 64])
    lnw, lnb = c.at("lnx_w_rows", 90, [P, 512]), c.at("lnx_b_rows", 92, [P, 512])
    g2 = c.at("gate_g2", 94, [96, 512])
    st = c.at("stats", 96, [P, 3, TILES, 8])
    lneps = c.at("lnx_eps", 98, [P, 1])
    y4 = y[:].rearrange("p t (h e) -> p t h e", e=64)
    wide = lambda a: a.unsqueeze(3).to_broadcast([P, TILES, 8, 64])
    along = lambda a: a[:].unsqueeze(1).to_broadcast([P, TILES, 512])
    load(c, [(lnw[:], dram["lnx_w_2"][0].partition_broadcast(P)), (lnb[:], dram["lnx_b_2"][0].partition_broadcast(P)),
             (g2[:], dram["gate_g2_2"][0])])
    with stage(nc, "variance_ready", "root_ready", "gate_open", "gates_ready", "gated", "dve_step") as (
            block, variance, root, gate_open, gates_ready, gated, dve_step):
        @block.scalar
        def _(act):
            act.activation(hg, hg, ACT.Sigmoid).then_inc(gate_open, 1)
            act.wait_ge(variance, 1)
            act.activation(st[:, 1], st[:, 0], ACT.Sqrt, scale=1.0 / 64, bias=lneps[:, 0:1]).then_inc(root, 1)

        @block.tensor
        def _(pe):
            pe.wait_ge(gate_open, 1)
            for t in range(TILES):
                pe.matmul(ps[:, t, :], rw[0:96, 13, CTX + t * P:CTX + (t + 1) * P], g2[:], start=True, stop=True)\
                  .then_inc(gates_ready, 1)

        @block.vector
        def _(dve):
            step = Step(dve, dve_step)
            step(dve.memset(lneps[:], LNX_EPS))
            step(dve.tensor_reduce(st[:, 2], y4, AX.X, ALU.add))
            step(dve.tensor_scalar(st[:, 2], st[:, 2], 1.0 / 64, None, ALU.mult))
            step(dve.tensor_tensor(y4, y4, wide(st[:, 2]), ALU.subtract))
            step(dve.tensor_tensor(sq[:], y4, y4, ALU.mult))
            dve.tensor_reduce(st[:, 0], sq[:], AX.X, ALU.add).then_inc(variance, 1)
            dve.wait_ge(root, 1)
            step(dve.reciprocal(st[:, 2], st[:, 1]))
            step(dve.tensor_tensor(y4, y4, wide(st[:, 2]), ALU.mult),
                 dve.tensor_tensor(sq[:], vrow[:, 2:NT].rearrange("p t (h e) -> p t h e", e=64), wide(sc[:]), ALU.mult))
            step(dve.tensor_tensor(y[:], y[:], along(lnw), ALU.mult))
            step(dve.tensor_tensor(y[:], y[:], along(lnb), ALU.add))
            step(dve.tensor_tensor(y4, y4, sq[:], ALU.add))
            for t in range(TILES):
                dve.wait_ge(gates_ready, t + 1)
                dve.tensor_tensor(y[:, t], y[:, t], ps[:, t, :], ALU.mult).then_inc(gated, 1)
            dve.wait_ge(gated, TILES)
    return y


def take_turns(first, second, lag):
    live = [first, second]
    for _ in range(lag):
        next(first)
    while live:
        for s in list(live):
            if next(s, "end") == "end":
                live.remove(s)


def scan(c, d, tiles, m):
    nc, ps = c.nc, c.psum
    (rw, vrow, y, sc, ka, half, rks, mk, keep, m1, m1T, w2, lm, eye, kk, r_, k_, DEC) = (m[n] for n in (
        "rw vrow y sc ka half rks mk keep m1 m1T w2 lm eye kk r_ k_ DEC").split())
    streams = m["streams"]
    tok = lambda t: slice(t * P, (t + 1) * P)
    half_of = lambda par: slice(64 * par, 64 * par + 64)
    order = (0, 1) if d == 0 else (1, 0)
    flat = lambda a: a[:].rearrange("p a b -> p (a b)")
    halves = lambda a: a[:].rearrange("p j (q n) -> p (j q) n", q=2)
    end = lambda a: a.unsqueeze(2).to_broadcast([P, 4, 64])
    HEADS = [(par, jj) for par in (0, 1) for jj in (0, 1)]
    slot = lambda par, jj: 2 * par + jj
    CH = [(cc, half_of(cc)) for cc in (0, 1)]

    def first_blocks(a, level):
        v = a.rearrange("p (g two n) -> p g two n", two=2, n=2 << level) if len(a.shape) == 2 else \
            a.rearrange("p h (g two n) -> p h g two n", two=2, n=2 << level)
        return v[:, :, d, :] if len(a.shape) == 2 else v[:, :, :, d, :]

    names = ("lora_done", "tanh_done", "logs_ready", "exps_ready", "scaled", "ends_scaled", "pairs_done",
             "pairs_masked", "abk_turned", "abk_copied", "l_turned", "m_ready", "mt_started", "x_done", "x_masked",
             "m_done", "mt_turned", "mt_copied", "w1_done", "w1_copied", "lkv_done", "lkv_copied", "p1_done",
             "p1_copied", "u_done", "u_ready", "s_done", "state_ready", "y_done", "tile_done", "state_cleared")
    both = [f"{n}_{g}" for g in (0, 1) for n in names]
    with stage(nc, "dve_step", *both) as (block, dve_step, *sems):
        sem = [dict(zip(names, sems[g * len(names):(g + 1) * len(names)])) for g in (0, 1)]

        @block.tensor
        def _(pe):
            def stream(g):
                b, s = streams[g], sem[g]
                B = 4 * g
                for i, t in enumerate(tiles):
                    emit = t >= 2
                    if i >= 1:
                        pe.wait_ge(s["tile_done"], i)
                    for kind in (0, 1):
                        for jj in (0, 1):
                            j = 2 * g + jj
                            last = pe.matmul(ps[:, B, (2 * kind + jj) * P:(2 * kind + jj + 1) * P],
                                             w2[:, kind, j * P:(j + 1) * P], rw[0:64, 12, tok(t)], start=True, stop=True)
                    last.then_inc(s["lora_done"], 1)
                    yield
                    yield
                    pe.wait_ge(s["scaled"], i + 1)
                    for kind, key in ((0, b.bt), (1, b.kt)):
                        for jj in (0, 1):
                            for cc, C in CH:
                                for par in (0, 1):
                                    o = (2 * kind + jj) * P
                                    last = pe.matmul(ps[C, B + 1 + par, o:o + P].rearrange("p (a n) -> p a n", a=2),
                                                     key[half_of(par), jj, C], b.ar[half_of(par), jj, :, C],
                                                     start=True, stop=True)
                    last.then_inc(s["pairs_done"], 1)
                    yield
                    pe.wait_ge(s["ends_scaled"], i + 1)
                    pe.wait_ge(s["tanh_done"], i + 1)
                    for n, src in enumerate((b.ar[:, :, 0, :], b.bb, b.kb)):
                        for jj in (0, 1):
                            col = n * 256 + jj * P
                            last = pe.transpose(ps[:, B + 3 if n < 2 else B, col % 512:col % 512 + P], src[:, jj],
                                                c.ident[:])
                    last.then_inc(s["abk_turned"], 1)
                    pe.wait_ge(s["pairs_masked"], i + 1)
                    for par, jj in HEADS:
                        for cc, C in CH:
                            last = pe.matmul(ps[C, B + 1, slot(par, jj) * 64:(slot(par, jj) + 1) * 64],
                                             b.LL[C, par, 0, jj, 0, :], c.ident[C, C], start=True, stop=True)
                    last.then_inc(s["l_turned"], 1)
                    for par, jj in HEADS:
                        h = 4 * g + 2 * jj + par
                        for cc, C in CH:
                            last = pe.matmul(ps[C, B + 2, slot(par, jj) * 64:(slot(par, jj) + 1) * 64],
                                             b.LL[C, par, 1, jj, 0, :], vrow[C, t, h * 64:(h + 1) * 64],
                                             start=True, stop=True)
                    last.then_inc(s["lkv_done"], 1)
                    yield
                    pe.wait_ge(s["mt_started"], i + 1)
                    pe.wait_ge(s["abk_copied"], i + 1)
                    pe.wait_ge(s["lkv_copied"], i + 1)

                    def turn_inverse():
                        for h4 in range(4):
                            for cc, C in CH:
                                last = pe.matmul(ps[C, B + 3, h4 * 64:(h4 + 1) * 64], b.M[C, h4], c.ident[C, C],
                                                 start=True, stop=True)
                        last.then_inc(s["mt_turned"], 1)

                    for level in range(5):
                        n = 5 * i + level
                        pe.wait_ge(s["m_ready"], n + i + 1)
                        if level:
                            turn_inverse()
                        for par, jj in HEADS:
                            h4 = slot(par, jj)
                            for cc, C in CH:
                                last = pe.matmul(ps[C, B + 1, h4 * 32:(h4 + 1) * 32], b.LL[C, par, 0, jj, 0, :],
                                                 first_blocks(b.M[C, h4], level), start=True, stop=True)
                        last.then_inc(s["x_done"], 1)
                        yield
                        pe.wait_ge(s["x_masked"], n + 1)
                        if level:
                            pe.wait_ge(s["mt_copied"], n)
                        for h4 in range(4):
                            for cc, C in CH:
                                last = pe.matmul(ps[C, B + 2, h4 * 32:(h4 + 1) * 32], b.MT[C, h4], b.X[C, h4],
                                                 start=True, stop=True)
                        last.then_inc(s["m_done"], 1)
                        yield
                    pe.wait_ge(s["m_ready"], 6 * i + 6)
                    turn_inverse()
                    yield
                    pe.wait_ge(s["mt_copied"], 5 * i + 5)
                    for h4 in range(4):
                        for cc, C in CH:
                            last = pe.matmul(ps[C, B + 2, h4 * 64:(h4 + 1) * 64], b.MT[C, h4], b.LKV[C, h4],
                                             start=True, stop=True)
                    last.then_inc(s["p1_done"], 1)
                    for par, jj in HEADS:
                        col = (2 * jj + par) * 64
                        for cc, C in CH:
                            last = pe.matmul(ps[half_of(par), B + cc, jj * 64:(jj + 1) * 64],
                                             b.tm[C, 0, col:col + 64], b.MT[C, slot(par, jj)], start=True, stop=True)
                    last.then_inc(s["w1_done"], 1)
                    yield
                    pe.wait_ge(s["p1_copied"], i + 1)
                    pe.wait_ge(s["w1_copied"], i + 1)
                    if i == 0:
                        pe.wait_ge(s["state_cleared"], 1)
                    for q, cc in enumerate(order):
                        C = half_of(cc)
                        if 2 * i + q:
                            pe.wait_ge(s["state_ready"], 2 * i + q)
                        for jj in (0, 1):
                            for par in (0, 1):
                                last = pe.matmul(ps[C, B + 2 + par, jj * 64:(jj + 1) * 64], b.W1[half_of(par), cc, jj],
                                                 b.S[half_of(par), jj], start=True, stop=True)
                        last.then_inc(s["u_done"], 1)
                        if emit:
                            for jj in (0, 1):
                                for par in (0, 1):
                                    pe.matmul(ps[C, B + par, jj * 64:(jj + 1) * 64], b.ar[half_of(par), jj, 1, C],
                                              b.S[half_of(par), jj], start=True, stop=True)
                        yield
                        pe.wait_ge(s["u_ready"], 2 * i + q + 1)
                        for par, jj in HEADS:
                            col, h = (2 * jj + par) * 64, 4 * g + 2 * jj + par
                            out = ps[half_of(par), B + 3, 128 + jj * 64:128 + (jj + 1) * 64]
                            pe.matmul(out, b.tm[C, 1, col:col + 64], b.U[C, slot(par, jj)], start=True, stop=False)
                            last = pe.matmul(out, b.tm[C, 2, col:col + 64], vrow[C, t, h * 64:(h + 1) * 64],
                                             start=False, stop=True)
                        last.then_inc(s["s_done"], 1)
                        yield
                    if emit:
                        for par, jj in HEADS:
                            h = 4 * g + 2 * jj + par
                            for cc, C in CH:
                                out = ps[C, B + 2, slot(par, jj) * 64:(slot(par, jj) + 1) * 64]
                                pe.matmul(out, b.LL[C, par, 0, jj, 1, :], b.U[C, slot(par, jj)], start=True, stop=False)
                                pe.matmul(out, b.LL[C, par, 1, jj, 1, :], vrow[C, t, h * 64:(h + 1) * 64],
                                          start=False, stop=True)
                        for jj in (0, 1):
                            last = pe.matmul(ps[:, B + 2, 256:260], b.rk[:, jj], rks[:, 2 * g + jj, 4 * g:4 * g + 4],
                                             start=(jj == 0), stop=(jj == 1))
                        last.then_inc(s["y_done"], 1)
                    yield

            take_turns(stream(0), stream(1), LAG)

        @block.scalar
        def _(act):
            def stream(g):
                b, s = streams[g], sem[g]
                B = 4 * g
                for i, t in enumerate(tiles):
                    act.wait_ge(s["lora_done"], i + 1)
                    for kind, dst in ((0, b.lw), (1, b.rate)):
                        for jj in (0, 1):
                            k = 8 * kind + 4 * d + 2 * g + jj
                            last = act.activation(dst[:, jj], ps[:, B, (2 * kind + jj) * P:(2 * kind + jj + 1) * P],
                                                  ACT.Tanh, scale=0.5, bias=half[:, k:k + 1])
                    last.then_inc(s["tanh_done"], 1)
                    yield
                    act.wait_ge(s["logs_ready"], i + 1)
                    after = b.F if d == 0 else b.e1
                    act.activation(b.e3[:], after[:], ACT.Exp, scale=-1.0)
                    act.activation(b.e1[:], after[:], ACT.Exp)
                    act.activation(b.e2[:], b.e2[:], ACT.Exp)
                    act.activation(b.ge[:], halves(b.F)[:, :, 63], ACT.Exp).then_inc(s["exps_ready"], 1)
                    yield
                    yield
                    act.wait_ge(s["abk_turned"], i + 1)
                    act.activation(b.tm[:, 0:2].rearrange("p a b -> p (a b)"), ps[:, B + 3, :], ACT.Copy)
                    act.activation(b.tm[:, 2], ps[:, B, 0:256], ACT.Copy).then_inc(s["abk_copied"], 1)
                    act.wait_ge(s["lkv_done"], i + 1)
                    act.activation(flat(b.LKV), ps[:, B + 2, 0:256], ACT.Copy).then_inc(s["lkv_copied"], 1)
                    yield

                    def copy_inverse(n):
                        act.wait_ge(s["mt_turned"], n)
                        act.activation(flat(b.MT), ps[:, B + 3, 0:256], ACT.Copy).then_inc(s["mt_copied"], 1)

                    for level in range(5):
                        if level:
                            copy_inverse(5 * i + level)
                        yield
                        yield
                    copy_inverse(5 * i + 5)
                    yield
                    act.wait_ge(s["p1_done"], i + 1)
                    act.activation(flat(b.P1), ps[:, B + 2, 0:256], ACT.Copy).then_inc(s["p1_copied"], 1)
                    act.wait_ge(s["w1_done"], i + 1)
                    act.activation(b.W1[:].rearrange("p a j n -> p a (j n)"), ps[:, B:B + 2, 0:128], ACT.Copy)\
                       .then_inc(s["w1_copied"], 1)
                    for _ in range(6):
                        yield

            take_turns(stream(0), stream(1), LAG)

        @block.gpsimd
        def _(pool):
            def stream(g):
                b, s = streams[g], sem[g]
                pool.memset(b.S[:], 0.0).then_inc(s["state_cleared"], 1)
                for i, t in enumerate(tiles):
                    yield
                    yield
                    pool.wait_ge(s["scaled"], i + 1)
                    pool.tensor_tensor(halves(b.bb), halves(b.bt), end(b.ge[:]), ALU.mult)
                    pool.tensor_tensor(halves(b.kb), halves(b.kt), end(b.ge[:]), ALU.mult)
                    pool.tensor_tensor(b.rk[:], r_[:, 2 * g:2 * g + 2, tok(t)], b.kd[:], ALU.mult)\
                        .then_inc(s["ends_scaled"], 1)
                    for _ in range(PHASES - 2):
                        yield

            take_turns(stream(0), stream(1), LAG)

        @block.vector
        def _(dve):
            step = Step(dve, dve_step)

            def stream(g):
                b, s = streams[g], sem[g]
                B = 4 * g
                pair = slice(2 * g, 2 * g + 2)
                wide = lambda a: a.unsqueeze(1).to_broadcast([P, 4, a.shape[-1]])
                for i, t in enumerate(tiles):
                    emit = t >= 2
                    kkt, rt, kts = kk[:, pair, tok(t)], r_[:, pair, tok(t)], k_[:, pair, tok(t)]
                    dve.wait_ge(s["tanh_done"], i + 1)
                    step(dve.tensor_scalar(b.lw[:], b.lw[:], -DEC / 2, -DEC / 2, ALU.mult, ALU.add),
                         dve.tensor_scalar(b.rate[:], b.rate[:], 0.5, 0.5, ALU.mult, ALU.add))
                    step(dve.tensor_tensor_scan(flat(b.F), keep[:, 0:256], flat(b.lw), 0.0, ALU.mult, ALU.add))
                    total = end(halves(b.F)[:, :, 63])
                    if d == 0:
                        dve.tensor_tensor(b.e2[:], b.F[:], b.lw[:], ALU.subtract).then_inc(s["logs_ready"], 1)
                    else:
                        step(dve.tensor_tensor(halves(b.e2), total, halves(b.F), ALU.subtract))
                        dve.tensor_tensor(b.e1[:], b.e2[:], b.lw[:], ALU.add).then_inc(s["logs_ready"], 1)
                    yield
                    if i >= 1:
                        dve.wait_ge(s["ends_scaled"], i)
                    step(*[dve.tensor_scalar(b.kd[:, jj], b.rate[:, jj], ka[:, 0, 2 * g + jj:2 * g + jj + 1],
                                             ka[:, 1, 2 * g + jj:2 * g + jj + 1], ALU.mult, ALU.add)
                           for jj in (0, 1)], dve.tensor_tensor(b.bt[:], kkt, b.rate[:], ALU.mult))
                    step(dve.tensor_tensor(b.kd[:], b.kd[:], kts, ALU.mult))
                    dve.wait_ge(s["exps_ready"], i + 1)
                    step(dve.scalar_tensor_tensor(b.ar[:, :, 0, :], kkt, -1.0, b.e2[:], ALU.mult, ALU.mult),
                         dve.tensor_tensor(b.ar[:, :, 1, :], rt, b.e1[:], ALU.mult),
                         dve.tensor_tensor(b.bt[:], b.bt[:], b.e3[:], ALU.mult))
                    dve.tensor_tensor(b.kt[:], b.kd[:], b.e3[:], ALU.mult).then_inc(s["scaled"], 1)
                    yield
                    dve.wait_ge(s["pairs_done"], i + 1)
                    dve.tensor_tensor(b.LL[:].rearrange("p a b j r n -> p (a b j) (r n)"),
                                      ps[:, B + 1:B + 3, :].rearrange("p a (b n) -> p (a b) n", n=P),
                                      mk[:].rearrange("p a t -> p (a t)").unsqueeze(1).to_broadcast([P, 8, P]),
                                      ALU.mult).then_inc(s["pairs_masked"], 1)
                    dve.wait_ge(s["pairs_masked"], i + 1)
                    step(*[dve.tensor_tensor(b.MT[:, 2 * par:2 * par + 2], b.LL[:, par, 0, :, 0, :],
                                             m1T[:].unsqueeze(1).to_broadcast([P, 2, 64]), ALU.mult)
                           for par in (0, 1)])
                    dve.tensor_tensor(b.MT[:], b.MT[:], wide(eye[:]), ALU.add).then_inc(s["mt_started"], 1)
                    yield
                    dve.wait_ge(s["l_turned"], i + 1)
                    step(dve.tensor_tensor(b.M[:], ps[:, B + 1, 0:256].rearrange("p (h n) -> p h n", h=4),
                                           wide(m1[:]), ALU.mult))
                    dve.tensor_tensor(b.M[:], b.M[:], wide(eye[:]), ALU.add).then_inc(s["m_ready"], 1)
                    yield
                    for level in range(5):
                        n = 5 * i + level
                        dve.wait_ge(s["x_done"], n + 1)
                        dve.tensor_tensor(b.X[:], ps[:, B + 1, 0:128].rearrange("p (h n) -> p h n", h=4),
                                          wide(lm[:, level]), ALU.mult).then_inc(s["x_masked"], 1)
                        yield
                        dve.wait_ge(s["m_done"], n + 1)
                        dve.wait_ge(s["m_ready"], n + i + 1)
                        target = first_blocks(b.M[:], level)
                        dve.tensor_tensor(target, target, ps[:, B + 2, 0:128]
                                          .rearrange("p (h g n) -> p h g n", h=4, n=2 << level), ALU.add)\
                           .then_inc(s["m_ready"], 1)
                        yield
                    yield
                    dve.wait_ge(s["p1_copied"], i + 1)
                    yield
                    for q, cc in enumerate(order):
                        C = half_of(cc)
                        ends = b.ge[:].rearrange("p (j q) -> p j q", q=2)[:, :, cc].unsqueeze(2)\
                                .to_broadcast([P, 2, 64])
                        if i == 0 and q == 0:
                            dve.wait_ge(s["state_cleared"], 1)
                        step(dve.tensor_tensor(b.SG[:], b.S[:], ends, ALU.mult))
                        dve.wait_ge(s["u_done"], 2 * i + q + 1)
                        dve.tensor_tensor(b.U[C].rearrange("p (a h) n -> p a (h n)", a=2), ps[C, B + 2:B + 4, 0:128],
                                          b.P1[C].rearrange("p (a h) n -> p a (h n)", a=2), ALU.add)\
                           .then_inc(s["u_ready"], 1)
                        yield
                        dve.wait_ge(s["s_done"], 2 * i + q + 1)
                        dve.tensor_tensor(b.S[:], ps[:, B + 3, 128:256].rearrange("p (j n) -> p j n", j=2), b.SG[:],
                                          ALU.add).then_inc(s["state_ready"], 1)
                        dve.wait_ge(s["state_ready"], 2 * i + q + 1)
                        yield
                    if emit:
                        row = t - 2
                        out = y[:, row, 256 * g:256 * g + 256].rearrange("p (j a e) -> p a j e", a=2, e=64)
                        from_state = ps[:, B:B + 2, 0:128].rearrange("p a (j e) -> p a j e", e=64)
                        inside = ps[:, B + 2, 0:256].rearrange("p (a j e) -> p a j e", a=2, e=64)
                        bonus = sc[:, row, 4 * g:4 * g + 4]
                        dve.wait_ge(s["y_done"], sum(1 for x in tiles[:i + 1] if x >= 2))
                        if d == 0:
                            step(dve.tensor_copy(out, from_state),
                                 dve.tensor_tensor(bonus, bonus, ps[:, B + 2, 256:260], ALU.add))
                        else:
                            step(dve.tensor_tensor(out, out, from_state, ALU.add),
                                 dve.tensor_tensor(bonus, bonus, ps[:, B + 2, 256:260], ALU.add))
                        dve.tensor_tensor(out, out, inside, ALU.add).then_inc(s["tile_done"], 1)
                        dve.wait_ge(s["tile_done"], i + 1)
                    else:
                        dve.nop().then_inc(s["tile_done"], 1)
                    yield

            take_turns(stream(0), stream(1), LAG)



def rope_tables():
    pos = np.arange(S, dtype=np.float32)
    inv = lambda theta, r: np.power(np.float32(theta), (-np.arange(r // 2, dtype=np.float32) * np.float32(2.0 / r)))
    angles = [pos[:, None] * inv(5e5, 16)[None], pos[:, None] * inv(5e5, 32)[None],
              (pos // 64)[:, None] * inv(1e4, 32)[None], (pos % 64)[:, None] * inv(1e4, 32)[None]]
    a = np.concatenate(angles, axis=1).astype(np.float32)
    return np.cos(a).astype(np.float32), np.sin(a).astype(np.float32)


def even_bias():
    dist = np.arange(1920)[None, :] - 896 - np.arange(P)[:, None]
    held = sum(((dist % dil == 0) & (abs(dist) <= win // 2)).astype(np.int64) for win, dil in
               ((128, 1), (512, 4), (2048, 16)))
    return np.where(held > 0, np.log(np.maximum(held, 1)) * HD ** 0.5, NEG).astype(np.float32)


def window_bias():
    q, k = np.arange(P)[:, None], np.arange(P)[None, :]
    before, after = np.where(k >= q, 0, NEG), np.where(k <= q, 0, NEG)
    opened = np.zeros((P, P))
    ctx = np.zeros((P, CTX))
    kinds = [np.concatenate([ctx, before, opened, after], 1), np.concatenate([ctx, opened, after, opened], 1)]
    return np.stack(kinds, 1).astype(np.float32)


def scan_masks():
    out = np.zeros((2, P, 416), np.float32)
    a, b = np.arange(P)[:, None] % CHUNK, np.arange(CHUNK)[None, :]
    out[0, :, 0:64], out[0, :, 64:128] = a < b, a <= b
    out[1, :, 0:64], out[1, :, 64:128] = a > b, a >= b
    out[0, :, 128:192] = (a % 2 == 1) & (b == a - 1)
    out[1, :, 128:192] = (a % 2 == 0) & (b == a + 1)
    out[0, :, 192:256] = (b % 2 == 1) & (a == b - 1)
    out[1, :, 192:256] = (b % 2 == 0) & (a == b + 1)
    col = np.arange(32)
    for level in range(5):
        n = 2 << level
        for d in range(2):
            block = 2 * (col // n) + d
            out[d, :, 256 + 32 * level:288 + 32 * level] = a // n == (block + (1 if d == 0 else -1))[None, :]
    return out


def constants():
    cos, sin = rope_tables()
    starts = np.ones((P, 512), np.float32)
    starts[:, ::CHUNK] = 0
    half = np.arange(P) // 64
    return {"const_rope_cos": cos, "const_rope_sin": sin, "const_even_bias": even_bias(),
            "const_window_bias": window_bias(), "const_scan_masks": scan_masks(), "const_chunk_starts": starts,
            "const_head_blocks": (half[:, None] == half[None, :]).astype(np.float32),
            "const_chunk_identity": np.tile(np.eye(CHUNK, dtype=np.float32), (2, 1)),
            "const_identity": np.eye(P, dtype=np.float32)}


def build(nc, dram, out, dump=None, last=None, only=None):
    c = Chip(nc, dram)
    result_stored = nc.alloc_semaphore("result_stored")
    if dump:
        c.dump = lambda name, ap: dump(c, name, ap)
    c.ident = c.at("identity", 0, [P, P])
    c.eps = c.at("eps", 0.5, [P, 1])
    c.rope_cos = c.at("rope_cos", 0.75, [P, TILES, 56])
    c.rope_sin = c.at("rope_sin", 2.5, [P, TILES, 56])
    x = c.at("x", 6, [P, TILES, D])
    with stage(nc, "eps_set") as (block, eps_set):
        @block.gpsimd
        def _(pool):
            pool.memset(c.eps[:], EPS).then_inc(eps_set, 1)
            pool.wait_ge(eps_set, 1)
    load(c, [(c.ident[:], dram["const_identity"]), (x[:], dram["x"][0].rearrange("(t p) d -> p t d", p=P)),
             (c.rope_cos[:], dram["const_rope_cos"].rearrange("(t p) d -> p t d", p=P)),
             (c.rope_sin[:], dram["const_rope_sin"].rearrange("(t p) d -> p t d", p=P))])
    stages = [("even", lambda: even_mixer(c, x, dram["even_w_in"][0])), ("moe0", lambda: experts(c, x, 0)),
              ("odd", lambda: odd_mixer(c, x)), ("moe1", lambda: experts(c, x, 1)),
              ("final", lambda: norm_rows(c, x, x, TILES, dram["final_norm"], 102)),
              ("second", lambda: second_block(c, x))]
    for name, run in stages:
        if only and name != only:
            continue
        run()
        if c.dump:
            c.dump("x_" + name, x)
        if name == last:
            break
    rows = c.at("result_rows", 38, [P, TILES, D])
    norm_rows(c, x, rows, TILES, dram["norm_f_g_2"], 102)
    with nc.Block(no_gpsimd_drain=True) as block:
        @block.sync
        def _(sp):
            sp.dma_start(out[0].rearrange("(t p) d -> p t d", p=P), rows[:]).then_inc(result_stored, 16)
            sp.wait_ge(result_stored, 16)


def kernel(**inputs):
    import concourse.bacc as bacc
    from concourse.bass_utils import run_bass_kernel_spmd

    nc = bacc.Bacc("TRN2", target_bir_lowering=False, num_devices=1)
    arrays, dram = {}, {}
    for name, a in {**inputs, **constants()}.items():
        a = np.ascontiguousarray(a)
        arrays["in_" + name] = a
        dram[name] = nc.dram_tensor("in_" + name, a.shape, F32, kind="ExternalInput").ap()
    for name in ("h_scratch", "x_scratch"):
        dram[name] = nc.dram_tensor(name, (S, D), F32).ap()
    out = nc.dram_tensor("out", (1, S, D), F32, kind="ExternalOutput").ap()
    build(nc, dram, out)
    return run_bass_kernel_spmd(nc, [arrays], core_ids=[0]).results[0]["out"]
```

```python
from contextlib import contextmanager

import numpy as np

import concourse.bass as bass
from concourse import mybir

F32 = mybir.dt.float32
F32R = mybir.dt.float32r
U32 = mybir.dt.uint32
BF16 = mybir.dt.bfloat16
ALU = mybir.AluOpType
ACT = mybir.ActivationFunctionType
AX = mybir.AxisListType

P = 128
D = 1024
S = 1024
TILES = S // P
KT = D // P
EPS = 1e-6
NEG = -1e30
HD = 64
BANK = 512
KB = 1024
ARENA = 16896

A_WIDTH, B_WIDTH, A_HEADS = 768, 256, 12
N_EXPERTS, CAP, FF = 16, 128, 512
CTX = 256
LNX_EPS = 1e-5 * 64
RW_CH = 4
T_ALL = CTX + S
CHUNK = 64


PARTS = [(0, 0), (0, 1), (1, 0)]

PHASES = 20
LAG = 10


class Stream:
    pass


class Step:

    def __init__(self, eng, sem):
        self.eng, self.sem, self.n = eng, sem, 0

    def __call__(self, *instructions):
        for i in instructions:
            i.then_inc(self.sem, 1)
            self.n += 1
        self.eng.wait_ge(self.sem, self.n)


STAGES = [0]


@contextmanager
def stage(nc, *names):
    STAGES[0] += 1
    sems = [nc.alloc_semaphore(f"{n}_s{STAGES[0]}") for n in names]
    with nc.Block(no_gpsimd_drain=True) as block:
        yield (block, *sems)
    nc.clear_and_free_semaphores(sems)
    nc.all_engine_barrier()


class Chip:

    def __init__(self, nc, dram):
        self.nc, self.dram, self.n = nc, dram, 0
        self.psum = nc.alloc_psum_tensor("psum", [P, 8, BANK], F32)

    def at(self, name, kb, shape, dt=F32):
        self.n += 1
        nbytes = int(np.prod(shape[1:])) * (2 if dt == BF16 else 4)
        assert ARENA + kb * KB + nbytes <= 229344, (name, kb, shape)
        return self.nc.alloc_sbuf_tensor_at(f"{name}_{self.n}", shape, dt, offset=ARENA + int(kb * KB))


def keep_warm(c, pe, out):
    rows, n = out.shape
    pe.matmul(out, c.idle[:, 0:rows], c.idle[:, 0:1].to_broadcast([P, n]), start=True, stop=True)



def load(c, pairs, small=False):
    with stage(c.nc, "tables_loaded") as (block, loaded):
        @block.sync
        def _(sp):
            for dst, src in pairs:
                sp.dma_start(dst, src, allow_slow_non_contiguous=small).then_inc(loaded, 16)
            sp.wait_ge(loaded, 16 * len(pairs))


def norm_rows(c, src, dst, tiles, gain, scr, keep=None, result=None):
    nc = c.nc
    half = tiles // 2
    gain_b = c.at("gain_b", scr, [P, D])
    sq = c.at("squares", scr + 4, [P, 2, D])
    st = c.at("stats", scr + 12, [P, 3, tiles])
    with stage(nc, "gain_loaded", "src_stored", "squares_summed", "roots_taken", "rows_scaled", "dve_step") as (
            block, gain_loaded, src_stored, summed, roots, scaled, dve_step):
        @block.sync
        def _(sp):
            sp.dma_start(gain_b[:], gain.partition_broadcast(P)).then_inc(gain_loaded, 16)
            sp.wait_ge(gain_loaded, 16)
            if keep is not None:
                sp.dma_start(keep, src[:]).then_inc(src_stored, 16)
                sp.wait_ge(src_stored, 16)
            if result is not None:
                for t in range(0, tiles, 2):
                    sp.wait_ge(scaled, t + 2)
                    sp.dma_start(result[0][:, t:t + 2], dst[:, t:t + 2]).then_inc(result[1], 16)
                sp.wait_ge(result[1], 16 * (tiles // 2))

        @block.scalar
        def _(act):
            for t in range(tiles):
                if t >= 2:
                    act.wait_ge(summed, t - 1)
                act.activation(sq[:, t % 2], src[:, t], ACT.Square, accum_out=st[:, 0, t:t + 1]).then_inc(summed, 1)
                if (t + 1) % half == 0:
                    act.wait_ge(summed, t + 1)
                    part = slice(t + 1 - half, t + 1)
                    act.activation(st[:, 1, part], st[:, 0, part], ACT.Sqrt, scale=1.0 / D, bias=c.eps[:, 0:1])\
                       .then_inc(roots, 1)

        @block.vector
        def _(dve):
            step = Step(dve, dve_step)
            dve.wait_ge(gain_loaded, 16)
            for t in range(tiles):
                if t % half == 0:
                    dve.wait_ge(roots, t // half + 1)
                    step(dve.reciprocal(st[:, 2, t:t + half], st[:, 1, t:t + half]))
                dve.scalar_tensor_tensor(dst[:, t], src[:, t], st[:, 2, t:t + 1], gain_b[:],
                                         ALU.mult, ALU.mult).then_inc(scaled, 1)
            dve.wait_ge(scaled, tiles)


def transposes(c, groups, loads=()):
    nc, ps = c.nc, c.psum
    n = len(groups)
    with stage(nc, "block_transposed", "act_copied", "dve_copied", "loads_done") as (
            block, done, act_copied, dve_copied, loads_done):
        @block.sync
        def _(sp):
            for to, source in loads:
                sp.dma_start(to, source).then_inc(loads_done, 16)
            if loads:
                sp.wait_ge(loads_done, 16 * len(loads))

        @block.tensor
        def _(pe):
            for i, (srcs, dst, _, _) in enumerate(groups):
                if i >= 8:
                    pe.wait_ge(act_copied if i % 2 else dve_copied, (i - 8) // 2 + 1)
                w = dst.shape[0]
                for j, s in enumerate(srcs):
                    last = pe.transpose(ps[0:w, i % 8, j * P:(j + 1) * P], s, c.ident[:])
                last.then_inc(done, 1)

        def copy(i, eng):
            srcs, dst, scale, shift = groups[i]
            w = dst.shape[0]
            src = ps[0:w, i % 8, 0:P * len(srcs)]
            eng.wait_ge(done, i + 1)
            if len(dst.shape) == 3:
                src = src.rearrange("p (a b) -> p a b", b=dst.shape[2])
            return src, dst, scale, shift

        @block.scalar
        def _(act):
            for i in range(1, n, 2):
                src, dst, scale, shift = copy(i, act)
                if scale is None:
                    act.activation(dst, src, ACT.Copy).then_inc(act_copied, 1)
                else:
                    act.activation(dst, src, ACT.Identity, bias=shift, scale=scale).then_inc(act_copied, 1)

        @block.vector
        def _(dve):
            for i in range(0, n, 2):
                src, dst, scale, shift = copy(i, dve)
                if scale is None:
                    dve.tensor_copy(dst, src).then_inc(dve_copied, 1)
                else:
                    dve.tensor_scalar(dst, src, scale, shift, ALU.mult, ALU.add).then_inc(dve_copied, 1)


def rows_to_cols(c, rows, cols, tiles, chunks, col0=0, scale=None, shift=None, loads=()):
    groups = []
    for half in range(0, tiles, 4):
        m = min(4, tiles - half)
        for k in range(chunks):
            groups.append(([rows[:, t, col0 + k * P:col0 + (k + 1) * P] for t in range(half, half + m)],
                           cols[:, k, half * P:(half + m) * P],
                           None if scale is None else scale[:, k:k + 1],
                           None if shift is None else shift[:, k:k + 1]))
    transposes(c, groups, loads)


def cols_in_parts(c, rows, cols, tiles, chunks, turned=None, scale=None, shift=None, loads=()):
    ps = c.psum
    groups = [(h, k) for h in range(0, tiles, 4) for k in range(chunks)]
    with stage(c.nc, "block_transposed", "act_value_ready", "dve_value_ready", "high_ready", "low_ready",
               "loads_done") as (block, done, act_value, dve_value, high, low, loads_done):
        @block.sync
        def _(sp):
            for to, source in loads:
                sp.dma_start(to, source).then_inc(loads_done, 16)
            if loads:
                sp.wait_ge(loads_done, 16 * len(loads))

        @block.tensor
        def _(pe):
            for i, (h, k) in enumerate(groups):
                if i >= 8:
                    if scale is None:
                        pe.wait_ge(low, i - 7)
                    else:
                        pe.wait_ge(act_value if i % 2 else dve_value, (i - 8) // 2 + 1)
                for j in range(min(4, tiles - h)):
                    last = pe.transpose(ps[:, i % 8, j * P:(j + 1) * P], rows[:, h + j, k * P:(k + 1) * P],
                                        c.ident[:])
                last.then_inc(done, 1)

        def place(i):
            h, k = groups[i]
            n = P * min(4, tiles - h)
            src = ps[:, i % 8, 0:n] if scale is None else turned[:, i % 2, 0:n]
            return k, n, src, cols[:, 0, k, h * P:h * P + n], cols[:, 1, k, h * P:h * P + n]

        @block.scalar
        def _(act):
            for i in range(len(groups)):
                k, n, src, hi, _ = place(i)
                act.wait_ge(done, i + 1)
                if scale is not None and i % 2 == 0:
                    act.wait_ge(dve_value, i // 2 + 1)
                if scale is not None and i % 2:
                    if i >= 2:
                        act.wait_ge(low, i - 1)
                    act.activation(src, ps[:, i % 8, 0:n], ACT.Identity, bias=shift[:, k:k + 1],
                                   scale=scale[:, k:k + 1]).then_inc(act_value, 1)
                    act.wait_ge(act_value, i // 2 + 1)
                act.activation(hi, src, ACT.Copy).then_inc(high, 1)

        @block.vector
        def _(dve):
            def value(i):
                if scale is not None and i % 2 == 0 and i < len(groups):
                    k, n, src, _, _ = place(i)
                    dve.wait_ge(done, i + 1)
                    if i >= 2:
                        dve.wait_ge(low, i - 1)
                    dve.tensor_scalar(src, ps[:, i % 8, 0:n], scale[:, k:k + 1], shift[:, k:k + 1], ALU.mult, ALU.add)\
                       .then_inc(dve_value, 1)

            value(0)
            for i in range(len(groups)):
                value(i + 1)
                _, _, src, hi, lo = place(i)
                dve.wait_ge(high, i + 1)
                dve.tensor_tensor(lo, src, hi.bitcast(F32), ALU.subtract).then_inc(low, 1)


def linear(c, kt, units, weights, ring, evacuate):
    nc, ps = c.nc, c.psum
    on_act, act_evacuate, dve_evacuate = evacuate
    before = {u: sum(1 for v in range(u) if on_act(v) == on_act(u)) for u in range(len(units))}
    last_use = {w: max(u for u, x in enumerate(units) if x[0] == w) for w in range(len(weights))}
    slots = len(ring)
    names = [f"weights_loaded_{i}" for i in range(slots)]
    with stage(nc, "unit_summed", "act_evacuated", "dve_evacuated", *names) as (
            block, summed, act_evac, dve_evac, *loaded):
        @block.sync
        def _(sp):
            for w, pairs in enumerate(weights):
                if w >= slots:
                    sp.wait_ge(summed, last_use[w - slots] + 1)
                dst, src = pairs(ring[w % slots])
                sp.dma_start(dst, src).then_inc(loaded[w % slots], 16)

        @block.tensor
        def _(pe):
            for u, (w, operands, shape) in enumerate(units):
                if weights:
                    pe.wait_ge(loaded[w % slots], 16 * (w // slots + 1))
                if u >= 8:
                    pe.wait_ge(act_evac if on_act(u - 8) else dve_evac, before[u - 8] + 1)
                out = ps[0:shape[0], u % 8, 0:shape[1]]
                for k in range(kt):
                    lhsT, rhs = operands(ring[w % slots], k)
                    last = pe.matmul(out, lhsT, rhs, start=(k == 0), stop=(k == kt - 1))
                last.then_inc(summed, 1)

        @block.scalar
        def _(act):
            for u, (_, _, shape) in enumerate(units):
                if on_act(u):
                    act.wait_ge(summed, u + 1)
                    act_evacuate(u, act, ps[0:shape[0], u % 8, 0:shape[1]]).then_inc(act_evac, 1)

        @block.vector
        def _(dve):
            for u, (_, _, shape) in enumerate(units):
                if not on_act(u):
                    dve.wait_ge(summed, u + 1)
                    dve_evacuate(u, dve, ps[0:shape[0], u % 8, 0:shape[1]]).then_inc(dve_evac, 1)


def first_weights(c, w_dram, spans, raw_kb, kt=KT):
    raw = c.at("weights_raw", raw_kb, [P, 2, kt, 256])
    w_rows = w_dram.rearrange("(k p) n -> p k n", p=P)
    return raw, [(raw[:, s, :, 0:b - a], w_rows[:, :, a:b]) for s, (a, b) in enumerate(spans[:2])]


def linear_in_parts(c, cols, w_dram, spans, raw_kb, parts_kb, tiles, on_act, evacuate, kt=KT, store=None,
                    first=False):
    ps, W = c.psum, 256
    raw = first[0] if first else c.at("weights_raw", raw_kb, [P, 2, kt, W])
    part = c.at("weight_parts", parts_kb, [P, 2, 2, kt, W], F32R)
    w_rows = w_dram.rearrange("(k p) n -> p k n", p=P)
    n = len(spans)
    mine = lambda act, s: on_act(spans[s][0]) == act
    before = lambda s: tiles * sum(1 for v in range(s) if mine(on_act(spans[s][0]), v))
    with stage(c.nc, "weights_loaded_0", "weights_loaded_1", "high_ready", "low_ready", "unit_summed",
               "act_evacuated", "dve_evacuated", "span_stored") as (
            block, l0, l1, high, low, summed, act_evac, dve_evac, stored):
        loaded = (l0, l1)

        def store_span(sp, s):
            a, b = (v - spans[0][0] for v in spans[s])
            sp.wait_ge(act_evac if mine(True, s) else dve_evac, before(s) + tiles)
            sp.dma_start(store[0][:, :, a:b], store[1][:, :, a:b]).then_inc(stored, 16)

        @block.sync
        def _(sp):
            for s, (a, b) in enumerate(spans):
                if s >= 2:
                    sp.wait_ge(low, s - 1)
                if s >= 2 or not first:
                    sp.dma_start(raw[:, s % 2, :, 0:b - a], w_rows[:, :, a:b]).then_inc(loaded[s % 2], 16)
                if store and s >= 1:
                    store_span(sp, s - 1)
            if store:
                store_span(sp, n - 1)
                sp.wait_ge(stored, 16 * n)

        @block.tensor
        def _(pe):
            for s, (a, b) in enumerate(spans):
                pe.wait_ge(low, s + 1)
                for t in range(tiles):
                    u = s * tiles + t
                    if u >= 8:
                        v, r = divmod(u - 8, tiles)
                        pe.wait_ge(act_evac if mine(True, v) else dve_evac, before(v) + r + 1)
                    for m, (i, j) in enumerate(PARTS):
                        for k in range(kt):
                            last = pe.matmul(ps[:, u % 8, 0:b - a], cols[:, i, k, t * P:(t + 1) * P],
                                             part[:, s % 2, j, k, 0:b - a], start=(m == 0 and k == 0),
                                             stop=(m == 2 and k == kt - 1))
                    last.then_inc(summed, 1)

        def units(eng, act, counter, split):
            split(0)
            for s, (a, b) in enumerate(spans):
                if s + 1 < n:
                    split(s + 1)
                if mine(act, s):
                    for t in range(tiles):
                        u = s * tiles + t
                        eng.wait_ge(summed, u + 1)
                        evacuate(a, b, t, eng, ps[:, u % 8, 0:b - a]).then_inc(counter, 1)

        @block.scalar
        def _(act):
            def split(s):
                if s >= 2 or not first:
                    act.wait_ge(loaded[s % 2], 16 * (s // 2 + (0 if first else 1)))
                if s >= 2:
                    act.wait_ge(summed, (s - 1) * tiles)
                width = spans[s][1] - spans[s][0]
                act.activation(part[:, s % 2, 0, :, 0:width], raw[:, s % 2, :, 0:width], ACT.Copy).then_inc(high, 1)

            units(act, True, act_evac, split)

        @block.vector
        def _(dve):
            def split(s):
                dve.wait_ge(high, s + 1)
                width = spans[s][1] - spans[s][0]
                dve.tensor_tensor(part[:, s % 2, 1, :, 0:width], raw[:, s % 2, :, 0:width],
                                  part[:, s % 2, 0, :, 0:width].bitcast(F32), ALU.subtract).then_inc(low, 1)

            units(dve, False, dve_evac, split)


def rope(step, dve, x1, x2, cos, sin, tmp):
    a, b, e, f = tmp
    step(dve.tensor_tensor(a, x1, cos, ALU.mult), dve.tensor_tensor(b, x2, sin, ALU.mult),
         dve.tensor_tensor(e, x1, sin, ALU.mult), dve.tensor_tensor(f, x2, cos, ALU.mult))
    step(dve.tensor_tensor(x1, a, b, ALU.subtract), dve.tensor_tensor(x2, e, f, ALU.add))


def attention(c, works, scale, tiles_kb, widths, sink=None, fillers=0):
    nc, ps = c.nc, c.psum
    n = len(works)
    biased = works[0][3] is not None
    at = lambda name, off, shape: c.at(name, tiles_kb + off, shape)
    s_b = at("scores", 0, [P, 2, 1024])
    p_b = at("probs", 8, [P, 2, 1024])
    pt_b = at("probs_turned", 16, [P, 2, 8, P])
    st = at("softmax_stats", 24, [P, 4, 8])
    with stage(nc, "scores_ready", "max_ready", "probs_ready", "probs_turned", "act_turned", "dve_turned",
               "weighted", "out_written", "dve_step", "sink_exp") as (
            block, scores_ready, max_ready, probs_ready, turned, act_turned, dve_turned, weighted,
            out_written, dve_step, sink_exp):
        S_ = lambda i: ps[:, 2 * (i % 2):2 * (i % 2) + 2, :].rearrange("p a b -> p (a b)")
        PT = lambda h: ps[:, 4 + h, :]
        O_ = lambda i: ps[:, 6 + i % 2, 0:HD]

        @block.tensor
        def _(pe):
            def scores(i):
                q, pieces, _, _, _, _ = works[i]
                if i >= 2:
                    pe.wait_ge(max_ready, i - 1)
                    pe.wait_ge(probs_ready, i - 1)
                for col, k in pieces:
                    products = PARTS if len(q) == 2 else [(0, 0)]
                    for m, (a, b) in enumerate(products):
                        last = pe.matmul(S_(i)[:, col:col + k[b].shape[-1]], q[a], k[b], start=(m == 0),
                                         stop=(m == len(products) - 1))
                last.then_inc(scores_ready, 1)

            def turn(i):
                m = len(works[i][2])
                pe.wait_ge(probs_ready, i + 1)
                if i >= 1:
                    pe.wait_ge(act_turned, i)
                    pe.wait_ge(dve_turned, i)
                for j in range(m):
                    last = pe.transpose(PT(j // 4)[:, (j % 4) * P:(j % 4 + 1) * P],
                                        p_b[:, i % 2, j * P:(j + 1) * P], c.ident[:])
                last.then_inc(turned, 1)

            def weigh(i):
                v = works[i][2]
                pe.wait_ge(act_turned, i + 1)
                pe.wait_ge(dve_turned, i + 1)
                if i >= 2:
                    pe.wait_ge(out_written, i - 1)
                for _ in range(fillers):
                    keep_warm(c, pe, ps[0:64, 6 + i % 2, 256:512])
                for j, vt in enumerate(v):
                    last = pe.matmul(O_(i), pt_b[:, i % 2, j, :], vt, start=(j == 0), stop=(j == len(v) - 1))
                last.then_inc(weighted, 1)

            scores(0)
            for i in range(n):
                if i + 1 < n:
                    scores(i + 1)
                if i >= 1:
                    weigh(i - 1)
                turn(i)
            weigh(n - 1)

        @block.scalar
        def _(act):
            def probs(i):
                w = widths(i)
                act.wait_ge(max_ready, i + 1)
                if i >= 2:
                    act.wait_ge(turned, i - 1)
                if i >= 4:
                    act.wait_ge(out_written, i - 3)
                src = s_b[:, i % 2, 0:w] if biased else S_(i)[:, 0:w]
                if sink is not None:
                    act.activation(st[:, i % 4, 4:5], sink[1][:, works[i][5]:works[i][5] + 1], ACT.Exp,
                                   bias=st[:, i % 4, 1:2]).then_inc(sink_exp, 1)
                act.activation(p_b[:, i % 2, 0:w], src, ACT.Exp, bias=st[:, i % 4, 1:2], scale=scale,
                               accum_out=st[:, i % 4, 2:3]).then_inc(probs_ready, 1)

            probs(0)
            for i in range(n):
                if i + 1 < n:
                    probs(i + 1)
                act.wait_ge(turned, i + 1)
                if i >= 2:
                    act.wait_ge(weighted, i - 1)
                m = min(4, len(works[i][2]))
                act.activation(pt_b[:, i % 2, 0:m, :].rearrange("p a b -> p (a b)"), PT(0)[:, 0:m * P],
                               ACT.Copy).then_inc(act_turned, 1)

        @block.vector
        def _(dve):
            step = Step(dve, dve_step)

            def maxima(i):
                w = widths(i)
                dve.wait_ge(scores_ready, i + 1)
                if i >= 2:
                    dve.wait_ge(probs_ready, i - 1)
                if biased:
                    step(dve.tensor_tensor_reduce(s_b[:, i % 2, 0:w], S_(i)[:, 0:w], works[i][3], 1.0, NEG,
                                                  ALU.add, ALU.max, st[:, i % 4, 0:1]))
                else:
                    step(dve.tensor_reduce(st[:, i % 4, 0:1], S_(i)[:, 0:w], AX.X, ALU.max))
                if sink is not None:
                    k = works[i][5]
                    step(dve.tensor_tensor(st[:, i % 4, 0:1], st[:, i % 4, 0:1], sink[0][:, k:k + 1], ALU.max))
                dve.tensor_scalar(st[:, i % 4, 1:2], st[:, i % 4, 0:1], -scale, None, ALU.mult)\
                   .then_inc(max_ready, 1)

            def write(i):
                b = st[:, i % 4]
                dve.wait_ge(probs_ready, i + 1)
                if sink is not None:
                    dve.wait_ge(sink_exp, i + 1)
                    step(dve.tensor_tensor(b[:, 2:3], b[:, 2:3], b[:, 4:5], ALU.add))
                step(dve.reciprocal(b[:, 3:4], b[:, 2:3]))
                dve.wait_ge(weighted, i + 1)
                dve.tensor_scalar(works[i][4], O_(i), b[:, 3:4], None, ALU.mult).then_inc(out_written, 1)

            maxima(0)
            for i in range(n):
                if i + 1 < n:
                    maxima(i + 1)
                if i >= 1:
                    write(i - 1)
                dve.wait_ge(turned, i + 1)
                if i >= 2:
                    dve.wait_ge(weighted, i - 1)
                m = len(works[i][2])
                if m > 4:
                    dve.tensor_copy(pt_b[:, i % 2, 4:m, :].rearrange("p a b -> p (a b)"),
                                    PT(1)[:, 0:(m - 4) * P]).then_inc(dve_turned, 1)
                else:
                    dve.nop().then_inc(dve_turned, 1)
            write(n - 1)



def even_mixer(c, x, w):
    nc, dram = c.nc, c.dram
    hn = c.at("h_rows", 38 + 96, [P, TILES, D])
    h = c.at("h_parts", 38, [P, 2, KT, S], F32R)
    norm_rows(c, x, hn, TILES, dram["norm_mix"][0], 180)
    spans = [(a, a + 256) for a in range(0, 3 * A_WIDTH + 2 * B_WIDTH, 256)]
    first = first_weights(c, w, spans, 102)
    cols_in_parts(c, hn, h, TILES, KT, loads=first[1])
    qk = c.at("qk_rows", 118, [P, TILES, 2 * A_WIDTH])
    vz = c.at("vz_rows", 166, [P, TILES, A_WIDTH + 2 * B_WIDTH])
    v = lambda t, a, b: vz[:, t, a:b]

    def copy_out(a, b, t, eng, p):
        dst = qk[:, t, a:b] if b <= 2 * A_WIDTH else vz[:, t, a - 2 * A_WIDTH:b - 2 * A_WIDTH]
        if a >= 3 * A_WIDTH:
            return eng.activation(dst, p, ACT.Gelu_apprx_tanh)
        return eng.tensor_copy(dst, p)

    linear_in_parts(c, h, w, spans, 102, 6, TILES, lambda a: a >= 3 * A_WIDTH, copy_out, first=first)

    tmp = [c.at("rope_tmp", 70 + 6 * i, [P, TILES, 24, 8]) for i in range(4)]
    heads = qk[:].rearrange("p t (h e) -> p t h e", e=HD)
    with stage(nc, "dve_step") as (block, dve_step):
        @block.vector
        def _(dve):
            step = Step(dve, dve_step)
            cos = c.rope_cos[:, :, 0:8].unsqueeze(2).to_broadcast([P, TILES, 24, 8])
            sin = c.rope_sin[:, :, 0:8].unsqueeze(2).to_broadcast([P, TILES, 24, 8])
            rope(step, dve, heads[:, :, :, 0:8], heads[:, :, :, 8:16], cos, sin, [t[:] for t in tmp])
    qkT = c.at("qk_parts", 6, [P, 2, 12, S], F32R)
    cols_in_parts(c, qk, qkT, TILES, 12)

    bias = c.at("window_bias", 126.25, [P, 1920])
    load(c, [(bias[:], dram["const_even_bias"])])
    ag = c.at("mix_rows", 134, [P, TILES, D])
    works = []
    for h in range(A_HEADS):
        r = slice(64 * (h % 2), 64 * (h % 2) + 64)
        for t in range(TILES):
            works.append(([qkT[r, i, h // 2, t * P:(t + 1) * P] for i in (0, 1)],
                          [(a, [qkT[r, i, 6 + h // 2, a:a + 512] for i in (0, 1)]) for a in (0, 512)],
                          [vz[:, j, h * HD:(h + 1) * HD] for j in range(TILES)],
                          bias[:, 896 - 128 * t:896 - 128 * t + 1024], ag[:, t, h * HD:(h + 1) * HD], None))
    attention(c, works, HD ** -0.5, 102, lambda i: 1024)

    G = 4
    ws = c.at("w_spatial", 38, [P, G, P])
    wsT = c.at("w_spatial_turned", 40, [P, G, P])
    bs = c.at("b_spatial", 42, [P, G])
    gn = c.at("gmlp_gain", 42.5, [P, B_WIDTH])
    load(c, [(ws[:], dram["even_w_spatial"][0].rearrange("g p q -> p g q")),
             (bs[:], dram["even_b_spatial"][0].rearrange("g p -> p g")),
             (x[:], dram["x"][0].rearrange("(t p) d -> p t d", p=P)),
             (gn[:], dram["even_gmlp_norm"][0].rearrange("g c -> (g c)").partition_broadcast(P))], small=True)
    transposes(c, [([ws[:, g] for g in range(G)], wsT[:].rearrange("p g q -> p (g q)"), None, None)])
    vv = vz[:, :, A_WIDTH + B_WIDTH:A_WIDTH + 2 * B_WIDTH].rearrange("p t (g e) -> p t g e", e=64)
    u = vz[:, :, A_WIDTH:A_WIDTH + B_WIDTH]
    group_norm_rows(c, vv, gn[:].rearrange("p (g e) -> p g e", e=64).unsqueeze(1).to_broadcast([P, TILES, G, 64]),
                    TILES, G, 64, 44)
    ps = c.psum
    with stage(nc, "mixed", "gated") as (block, mixed, gated):
        @block.tensor
        def _(pe):
            for g in range(G):
                pe.matmul(ps[:, g, :].rearrange("p (t e) -> p t e", e=64), wsT[:, g], vv[:, :, g, :],
                          start=True, stop=True).then_inc(mixed, 1)

        @block.vector
        def _(dve):
            for g in range(G):
                dve.wait_ge(mixed, g + 1)
                dve.scalar_tensor_tensor(ag[:, :, A_WIDTH + g * 64:A_WIDTH + (g + 1) * 64],
                                         ps[:, g, :].rearrange("p (t e) -> p t e", e=64), bs[:, g:g + 1],
                                         u[:, :, g * 64:(g + 1) * 64], ALU.add, ALU.mult).then_inc(gated, 1)
    out_and_residual(c, x, ag, dram["even_w_out"][0])


def group_norm_rows(c, x, gain, tiles, groups, width, kb):
    sq = c.at("squares", kb, [P, tiles, groups, width])
    st = c.at("stats", kb + tiles * groups * width * 4 / KB, [P, 3, tiles, groups])
    with stage(c.nc, "sums_ready", "roots_ready", "dve_step") as (block, sums, roots, dve_step):
        @block.vector
        def _(dve):
            step = Step(dve, dve_step)
            step(dve.tensor_tensor(sq[:], x, x, ALU.mult))
            dve.tensor_reduce(st[:, 0], sq[:], AX.X, ALU.add).then_inc(sums, 1)
            dve.wait_ge(roots, 1)
            step(dve.reciprocal(st[:, 2], st[:, 1]))
            step(dve.tensor_tensor(x, x, st[:, 2].unsqueeze(3).to_broadcast([P, tiles, groups, width]), ALU.mult))
            step(dve.tensor_tensor(x, x, gain, ALU.mult))

        @block.scalar
        def _(act):
            act.wait_ge(sums, 1)
            act.activation(st[:, 1], st[:, 0], ACT.Sqrt, scale=1.0 / width, bias=c.eps[:, 0:1]).then_inc(roots, 1)


def out_and_residual(c, x, rows, w_dram):
    T = c.at("mix_parts", 38, [P, 2, KT, S], F32R)
    spans = [(a, a + 256) for a in range(0, D, 256)]
    first = first_weights(c, w_dram, spans, 102)
    cols_in_parts(c, rows, T, TILES, KT, loads=first[1])
    linear_in_parts(c, T, w_dram, spans, 102, 118, TILES, lambda a: False,
                    lambda a, b, t, dve, p: dve.tensor_tensor(x[:, t, a:b], p, x[:, t, a:b], ALU.add), first=first)



class Modulation:
    CHUNKS, SLOTS = 6, 4

    def __init__(self, c, part, kb):
        self.c, self.part = c, part
        self.ring = c.at("w_ada", kb, [P, self.SLOTS, KT, BANK])
        self.rows = c.at("ada_rows", kb + 16 * self.SLOTS, [P, 2, BANK])
        self.cond = c.at("cond_padded", kb + 16 * self.SLOTS + 4, [P, KT, 32])
        self.pick = c.at("quarters_sum", kb + 16 * self.SLOTS + 5, [P, 2])

    NAMES = ("ada_cond_ready", "ada_pick_ready", "ada_summed", "ada_copied", "ada_turned", "ada_done",
             *[f"w_ada_loaded_{i}" for i in range(SLOTS)])

    def take(self, sems):
        (self.cond_ready, self.pick_ready, self.summed, self.copied, self.turned, self.done, *self.loaded) = sems

    def on_sync(self, sp):
        w_ada = self.c.dram["w_ada_2"][0].rearrange("(k p) n -> p k n", p=P)
        for i in range(self.CHUNKS):
            w = self.CHUNKS * self.part + i
            if i >= self.SLOTS:
                sp.wait_ge(self.summed, i - self.SLOTS + 1)
            sp.dma_start(self.ring[:, i % self.SLOTS], w_ada[:, :, w * BANK:(w + 1) * BANK])\
              .then_inc(self.loaded[i % self.SLOTS], 16)

    def on_pool(self, pool):
        pool.memset(self.cond[:], 0.0).then_inc(self.cond_ready, 1)
        pool.wait_ge(self.cond_ready, 1)
        pool.tensor_copy(self.cond[:, :, 0:2], self.c.vT[:, 48:64].rearrange("p (a k) -> p k a", k=KT))\
            .then_inc(self.cond_ready, 1)

    def on_tensor(self, pe):
        ps = self.c.psum
        pe.wait_ge(self.cond_ready, 2)
        pe.wait_ge(self.pick_ready, 1)

        def turn(i):
            pe.wait_ge(self.copied, i + 1)
            for j in range(4):
                u = 4 * i + j
                last = pe.matmul(ps[:, 6, 2 * u:2 * u + 2], self.rows[:, i % 2, j * P:(j + 1) * P], self.pick[:],
                                 start=True, stop=True)
            last.then_inc(self.turned, 1)

        for i in range(self.CHUNKS):
            pe.wait_ge(self.loaded[i % self.SLOTS], 16 * (i // self.SLOTS + 1))
            if i >= 2:
                pe.wait_ge(self.copied, i - 1)
            for k in range(KT):
                q = k % 4
                last = pe.matmul(ps[32 * q:32 * q + 32, 4 + i % 2, :], self.cond[:, k],
                                 self.ring[:, i % self.SLOTS, k], start=(k < 4), stop=(k >= 4))
            last.then_inc(self.summed, 1)
            if i >= 1:
                turn(i - 1)
        turn(self.CHUNKS - 1)

    def on_scalar(self, act):
        for i in range(self.CHUNKS):
            act.wait_ge(self.summed, i + 1)
            if i >= 2:
                act.wait_ge(self.turned, i - 1)
            act.activation(self.rows[:, i % 2], self.c.psum[:, 4 + i % 2, :], ACT.Copy).then_inc(self.copied, 1)

    def on_vector_first(self, dve):
        dve.tensor_reduce(self.pick[:], self.c.ident[:].rearrange("p (g n) -> p n g", n=32)[:, 0:2], AX.X, ALU.add)\
           .then_inc(self.pick_ready, 1)

    def on_vector_last(self, dve):
        n, u0 = 4 * self.CHUNKS, 4 * self.CHUNKS * self.part
        dve.wait_ge(self.turned, self.CHUNKS)
        dve.tensor_tensor(self.c.mod[:, 2 * u0:2 * (u0 + n)].rearrange("p (u a) -> p u a", a=2),
                          self.c.psum[:, 6, 0:2 * n].rearrange("p (u a) -> p u a", a=2),
                          self.c.vT[:, u0:u0 + n].unsqueeze(2).to_broadcast([P, n, 2]), ALU.add)\
           .then_inc(self.done, 1)
        dve.wait_ge(self.done, 1)



def experts(c, x, layer):
    nc, dram, ps = c.nc, c.dram, c.psum
    hn = c.at("h_rows", 38, [P, TILES, D])
    hT = c.at("h_cols", 70, [P, KT, S])
    norm_rows(c, x, hn, TILES, dram["norm_ffn"][layer], 102)
    wr = c.at("w_router", 102, [P, KT, 32])
    with stage(nc, "cleared") as (block, cleared):
        @block.gpsimd
        def _(pool):
            pool.memset(wr[:, :, N_EXPERTS:32], 0.0).then_inc(cleared, 1)
            pool.wait_ge(cleared, 1)
    rows_to_cols(c, hn, hT, TILES, KT,
                 loads=[(wr[:, :, 0:N_EXPERTS], dram["moe_w_router"][layer].rearrange("(k p) e -> p k e", p=P))])
    lg = c.at("logits", 103, [P, TILES, N_EXPERTS])
    aff = c.at("affinity", 104, [N_EXPERTS, S])
    best = c.at("best_values", 108, [N_EXPERTS, CAP])
    besti = c.at("best_tokens", 109, [N_EXPERTS, CAP], U32)
    bestf = c.at("best_tokens_f", 110, [N_EXPERTS, CAP])
    sm = c.at("softmax_stats", 111, [P, 2, TILES])
    pick = c.at("quarters_sum", 111.25, [P, N_EXPERTS])
    quarters = c.at("quarter_sums", 186, [P, S])
    gates = c.at("gates", 4.5, [P, N_EXPERTS])
    tokens = c.at("tokens", 4.625, [P, N_EXPERTS], U32)
    h_dram, x_dram = dram["h_scratch"], dram["x_scratch"]
    NE = N_EXPERTS
    RAW_SLOTS, PART_SLOTS = 6, 5
    raw = c.at("weights_raw", 38, [P, RAW_SLOTS, 4, BANK])
    part = c.at("weight_parts", 38 + 8 * RAW_SLOTS, [P, PART_SLOTS, 2, 4, BANK], F32R)
    kb = 38 + 8 * RAW_SLOTS + 16 * PART_SLOTS
    xs = c.at("picked", kb, [P, 2, D])
    xT = c.at("picked_parts", kb + 8, [P, 2, KT, P], F32R)
    sg = c.at("silu_gate", kb + 16, [P, FF])
    ac = c.at("activated", kb + 18, [P, FF])
    aT = c.at("activated_parts", kb + 20, [P, 2, 4, P], F32R)
    y = c.at("expert_out", kb + 24, [P, 2, D])
    pieces = []
    for e in range(NE + 1):
        if e < NE:
            pieces += [("gate", e, 0), ("gate", e, 1), ("up", e, 0), ("up", e, 1)]
        if e >= 1:
            pieces += [("down", e - 1, 0), ("down", e - 1, 1)]
    at_piece = {q: n for n, q in enumerate(pieces)}
    AHEAD = PART_SLOTS - 3

    def source(kind, e, h):
        if kind == "down":
            return dram["moe_w_down"][layer, e].rearrange("(h k p) n -> h p k n", p=P, k=2)[h]
        return dram["moe_w_" + kind][layer, e].rearrange("(h k p) f -> h p k f", p=P, k=4)[h]

    def load_piece(sp, n):
        slot = raw[:, n % RAW_SLOTS]
        if pieces[n][0] == "down":
            slot = slot.rearrange("p (k g) f -> p k (g f)", g=2)
        return sp.dma_start(slot, source(*pieces[n]))

    ada = Modulation(c, layer, 114)
    with stage(nc, *ada.NAMES, "h_stored", "x_stored", "first_loaded", "pick_ready", "quarters_ready",
               "quarters_copied", "logits_ready", "max_off", "exp_ready", "aff_ready", "turned",
               "best_ready", "best_turned", "dve_step") as (
            block, *sems):
        ada.take(sems[:len(ada.NAMES)])
        (h_stored, x_stored, first_loaded, pick_ready, quarters_ready, quarters_copied, logits_ready, max_off, exp_ready, aff_ready, turned,
         best_ready, best_turned, dve_step) = sems[len(ada.NAMES):]

        @block.sync
        def _(sp):
            sp.dma_start(h_dram.rearrange("(t p) d -> p t d", p=P), hn[:]).then_inc(h_stored, 16)
            sp.wait_ge(quarters_ready, 2)
            sp.wait_ge(h_stored, 16)
            for n in range(RAW_SLOTS):
                load_piece(sp, n).then_inc(first_loaded, 16)
            sp.dma_start(x_dram.rearrange("(t p) d -> p t d", p=P), x[:]).then_inc(x_stored, 16)
            ada.on_sync(sp)
            sp.wait_ge(first_loaded, 16 * RAW_SLOTS)
            sp.wait_ge(x_stored, 16)

        @block.gpsimd
        def _(pool):
            ada.on_pool(pool)

        @block.tensor
        def _(pe):
            for half in range(2):
                for k in range(KT):
                    q = k % 4
                    last = pe.matmul(ps[32 * q:32 * q + 32, 1 + half, :], wr[:, k],
                                     hT[:, k, half * 512:(half + 1) * 512], start=(k < 4), stop=(k >= 4))
                last.then_inc(quarters_ready, 1)
            pe.wait_ge(pick_ready, 1)
            for t in range(TILES):
                if t % 4 == 0:
                    pe.wait_ge(quarters_copied, t // 4 + 1)
                last = pe.matmul(ps[:, 0, t * 16:(t + 1) * 16], quarters[:, t * P:(t + 1) * P], pick[:],
                                 start=True, stop=True)
            last.then_inc(logits_ready, 1)
            pe.wait_ge(aff_ready, 1)
            for t in range(TILES):
                last = pe.transpose(ps[0:16, 1 + t // 4, (t % 4) * P:(t % 4 + 1) * P], lg[:, t], c.ident[:])
            last.then_inc(turned, 1)
            ada.on_tensor(pe)
            pe.wait_ge(best_ready, 1)
            pe.transpose(ps[:, 3, 0:16], best[:], c.ident[0:16, 0:16])
            pe.transpose(ps[:, 3, 16:32], bestf[:], c.ident[0:16, 0:16]).then_inc(best_turned, 1)

        @block.scalar
        def _(act):
            for half in range(2):
                act.wait_ge(quarters_ready, half + 1)
                act.activation(quarters[:, half * 512:(half + 1) * 512], ps[:, 1 + half, :], ACT.Copy)\
                   .then_inc(quarters_copied, 1)
            act.wait_ge(max_off, 1)
            act.activation(lg[:], lg[:], ACT.Exp).then_inc(exp_ready, 1)
            ada.on_scalar(act)

        @block.vector
        def _(dve):
            step = Step(dve, dve_step)
            dve.tensor_reduce(pick[:], c.ident[:].rearrange("p (g n) -> p n g", n=32)[:, 0:N_EXPERTS], AX.X, ALU.add)\
               .then_inc(pick_ready, 1)
            ada.on_vector_first(dve)
            flat = ps[:, 0, 0:128].rearrange("p (t e) -> p t e", e=16)
            wide = lambda a: a.unsqueeze(2).to_broadcast([P, TILES, 16])
            dve.wait_ge(logits_ready, 1)
            step(dve.tensor_reduce(sm[:, 0], flat, AX.X, ALU.max))
            dve.tensor_tensor(lg[:], flat, wide(sm[:, 0]), ALU.subtract).then_inc(max_off, 1)
            dve.wait_ge(exp_ready, 1)
            step(dve.tensor_reduce(sm[:, 0], lg[:], AX.X, ALU.add))
            step(dve.reciprocal(sm[:, 1], sm[:, 0]))
            dve.tensor_tensor(lg[:], lg[:], wide(sm[:, 1]), ALU.mult).then_inc(aff_ready, 1)
            dve.wait_ge(turned, 1)
            step(dve.tensor_copy(aff[:], ps[0:16, 1:3, :].rearrange("p a b -> p (a b)")))
            for r in range(CAP // 8):
                b = best[:, r * 8:(r + 1) * 8]
                step(dve.max(b, aff[:]))
                step(dve.max_index(besti[:, r * 8:(r + 1) * 8], b, aff[:]))
                step(dve.match_replace(aff[:], b, aff[:], -1.0))
            dve.tensor_copy(bestf[:], besti[:]).then_inc(best_ready, 1)
            ada.on_vector_last(dve)
            dve.wait_ge(best_turned, 1)
            step(dve.tensor_copy(gates[:], ps[:, 3, 0:16]), dve.tensor_copy(tokens[:], ps[:, 3, 16:32]))

    with stage(nc, "picked_0", "picked_1", "picked_turned", "picked_high", "picked_low", "high_ready", "low_ready",
               "piece_used", "silu_done", "activated", "act_turned", "act_high", "act_low", "scaled", "scattered",
               *[f"piece_loaded_{i}" for i in range(RAW_SLOTS)]) as (
            block, pk0, pk1, turned, picked_high, picked_low, high, low, used, silu, activated, aturned, act_high,
            act_low, scaled, scattered, *loaded):
        pk = (pk0, pk1)

        @block.sync
        def _(sp):
            for n in range(RAW_SLOTS, len(pieces)):
                sp.wait_ge(low, n - RAW_SLOTS + 1)
                load_piece(sp, n).then_inc(loaded[n % RAW_SLOTS], 16)

        @block.gpsimd
        def _(pool):
            def pick(e):
                if e >= 2:
                    pool.wait_ge(turned, e - 1)
                pool.indirect_dma_start(xs[:, e % 2], None, h_dram,
                                        bass.IndirectOffsetOnAxis(tokens[:, e:e + 1], 0)).then_inc(pk[e % 2], 16)

            pick(0)
            pick(1)
            for e in range(NE):
                if e + 2 < NE:
                    pick(e + 2)
                pool.wait_ge(scaled, 2 * e + 2)
                if e >= 1:
                    pool.wait_ge(scattered, 16 * e)
                pool.indirect_dma_start(x_dram, bass.IndirectOffsetOnAxis(tokens[:, e:e + 1], 0), y[:, e % 2], None,
                                        compute_op=ALU.add).then_inc(scattered, 16)
            pool.wait_ge(scattered, 16 * NE)

        @block.tensor
        def _(pe):
            def turn(e):
                pe.wait_ge(pk[e % 2], 16 * (e // 2 + 1))
                if e >= 1:
                    pe.wait_ge(picked_low, 2 * e)
                for k in range(KT):
                    last = pe.transpose(ps[:, k // 4, (k % 4) * P:(k % 4 + 1) * P], xs[:, e % 2, k * P:(k + 1) * P],
                                        c.ident[:])
                last.then_inc(turned, 1)

            turn(0)
            for n, (kind, e, h) in enumerate(pieces):
                w = part[:, n % PART_SLOTS]
                if h == 0 and kind == "gate":
                    pe.wait_ge(picked_low, 2 * e + 2)
                    if e >= 1:
                        pe.wait_ge(activated, e)
                if h == 0 and kind == "down":
                    pe.wait_ge(act_low, e + 1)
                    if e >= 1:
                        pe.wait_ge(scaled, 2 * e)
                pe.wait_ge(low, n + 1)
                for m, (a, b) in enumerate(PARTS):
                    first, final = h == 0 and m == 0, h == 1 and m == 2
                    if kind == "down":
                        for half in range(2):
                            for k in range(2):
                                last = pe.matmul(ps[:, 5 + half, :], aT[:, a, 2 * h + k], w[:, b, 2 * k + half],
                                                 start=(first and k == 0), stop=(final and k == 1))
                    else:
                        for k in range(4):
                            last = pe.matmul(ps[:, 2 if kind == "gate" else 3, :], xT[:, a, 4 * h + k], w[:, b, k],
                                             start=(first and k == 0), stop=(final and k == 3))
                last.then_inc(used, 1)
                if (kind, h) == ("up", 1) and e + 1 < NE:
                    turn(e + 1)
                e_act = 0 if (kind, e, h) == ("up", 0, 1) else e + 1 if (kind, h) == ("down", 1) and e + 1 < NE else None
                if e_act is not None:
                    pe.wait_ge(activated, e_act + 1)
                    if e_act >= 1:
                        pe.wait_ge(act_low, e_act)
                    for k in range(4):
                        last = pe.transpose(ps[:, 4, k * P:(k + 1) * P], ac[:, k * P:(k + 1) * P], c.ident[:])
                    last.then_inc(aturned, 1)

        def behind(n, gate_up_done, down_done):
            if 0 <= n - AHEAD < len(pieces):
                kind, e, h = pieces[n - AHEAD]
                if (kind, h) == ("up", 1):
                    gate_up_done(e)
                    if e == 0:
                        down_done(-1)
                if (kind, h) == ("down", 1):
                    down_done(e)

        @block.scalar
        def _(act):
            def gate_up_done(e):
                act.wait_ge(used, at_piece["up", e, 1] + 1)
                if e >= 1:
                    act.wait_ge(activated, e)
                act.activation(sg[:], ps[:, 2, :], ACT.Silu).then_inc(silu, 1)
                if e + 1 < NE:
                    picked_hi(e + 1)

            def picked_hi(e):
                act.wait_ge(turned, e + 1)
                for h in range(2):
                    act.activation(xT[:, 0, 4 * h:4 * h + 4].rearrange("p a b -> p (a b)"), ps[:, h, :], ACT.Copy)\
                       .then_inc(picked_high, 1)

            def down_done(e):
                if e + 1 < NE:
                    act.wait_ge(aturned, e + 2)
                    act.activation(aT[:, 0].rearrange("p a b -> p (a b)"), ps[:, 4, :], ACT.Copy)\
                       .then_inc(act_high, 1)
                if e >= 0:
                    act.wait_ge(used, at_piece["down", e, 1] + 1)
                    if e >= 2:
                        act.wait_ge(scattered, 16 * (e - 1))
                    for half in range(2):
                        act.activation(y[:, e % 2, half * 512:(half + 1) * 512], ps[:, 5 + half, :], ACT.Copy,
                                       scale=gates[:, e:e + 1]).then_inc(scaled, 1)

            picked_hi(0)
            for n in range(len(pieces) + AHEAD):
                if n < len(pieces):
                    if n >= RAW_SLOTS:
                        act.wait_ge(loaded[n % RAW_SLOTS], 16 * (n // RAW_SLOTS))
                    if n >= PART_SLOTS:
                        act.wait_ge(used, n - PART_SLOTS + 1)
                    act.activation(part[:, n % PART_SLOTS, 0], raw[:, n % RAW_SLOTS], ACT.Copy).then_inc(high, 1)
                behind(n, gate_up_done, down_done)

        @block.vector
        def _(dve):
            def gate_up_done(e):
                dve.wait_ge(silu, e + 1)
                if e >= 1:
                    dve.wait_ge(aturned, e)
                dve.tensor_tensor(ac[:], sg[:], ps[:, 3, :], ALU.mult).then_inc(activated, 1)
                if e + 1 < NE:
                    picked_lo(e + 1)

            def picked_lo(e):
                for h in range(2):
                    dve.wait_ge(picked_high, 2 * e + h + 1)
                    lo, hi = (xT[:, i, 4 * h:4 * h + 4].rearrange("p a b -> p (a b)") for i in (1, 0))
                    dve.tensor_tensor(lo, ps[:, h, :], hi.bitcast(F32), ALU.subtract).then_inc(picked_low, 1)

            def down_done(e):
                if e + 1 < NE:
                    dve.wait_ge(act_high, e + 2)
                    lo, hi = (aT[:, i].rearrange("p a b -> p (a b)") for i in (1, 0))
                    dve.tensor_tensor(lo, ps[:, 4, :], hi.bitcast(F32), ALU.subtract).then_inc(act_low, 1)

            picked_lo(0)
            for n in range(len(pieces) + AHEAD):
                if n < len(pieces):
                    dve.wait_ge(high, n + 1)
                    dve.tensor_tensor(part[:, n % PART_SLOTS, 1], raw[:, n % RAW_SLOTS],
                                      part[:, n % PART_SLOTS, 0].bitcast(F32), ALU.subtract).then_inc(low, 1)
                behind(n, gate_up_done, down_done)
    load(c, [(x[:], x_dram.rearrange("(t p) d -> p t d", p=P))])



def odd_mixer(c, x):
    dram = c.dram
    hn = c.at("h_rows", 134, [P, TILES, D])
    h = c.at("h_parts", 38, [P, 2, KT, S], F32R)
    norm_rows(c, x, hn, TILES, dram["norm_mix"][1], 180)
    spans = [(0, 256), (256, 416), (416, 672), (672, 928), (928, 1184)]
    first = first_weights(c, dram["odd_w_in"][0], spans, 102)
    cols_in_parts(c, hn, h, TILES, KT, loads=first[1])
    low = c.at("latent_rows", 118, [P, TILES, 416])
    dqk = c.at("d_rows", 131, [P, TILES, 768])
    dv = c.at("dv_rows", 155, [P, TILES, 128])

    def copy_out(a, b, t, act, p):
        if b <= 416:
            return act.activation(low[:, t, a:b], p, ACT.Copy)
        if b <= 928:
            return act.activation(dqk[:, t, a - 416:b - 416], p, ACT.Copy)
        act.activation(dqk[:, t, 512:640], p[:, 0:128], ACT.Copy)
        return act.activation(dv[:, t], p[:, 128:256], ACT.Copy)

    linear_in_parts(c, h, dram["odd_w_in"][0], spans, 102, 160, TILES, lambda a: True, copy_out, first=first)

    gains = c.at("norm_gains", 38, [P, 512])
    load(c, [(gains[:, 0:256], dram["odd_cq_norm"][0].partition_broadcast(P)),
             (gains[:, 256:384], dram["odd_ckv_norm"][0].partition_broadcast(P)),
             (gains[:, 384:448], dram["odd_dq_norm"][0].partition_broadcast(P)),
             (gains[:, 448:512], dram["odd_dk_norm"][0].partition_broadcast(P))])
    wide = lambda a, g, w: a.unsqueeze(1).unsqueeze(1).to_broadcast([P, TILES, g, w])
    group_norm_rows(c, low[:, :, 0:256].unsqueeze(2), wide(gains[:, 0:256], 1, 256), TILES, 1, 256, 40)
    group_norm_rows(c, low[:, :, 256:384].unsqueeze(2), wide(gains[:, 256:384], 1, 128), TILES, 1, 128, 40)
    heads = dqk[:].rearrange("p t (h e) -> p t h e", e=HD)
    group_norm_rows(c, heads[:, :, 0:8], wide(gains[:, 384:448], 8, 64), TILES, 8, 64, 40)
    group_norm_rows(c, heads[:, :, 8:10], wide(gains[:, 448:512], 2, 64), TILES, 2, 64, 40)
    tmp = [c.at("rope_tmp", 40 + 5 * i, [P, TILES, 10, 16]) for i in range(4)]
    table = lambda t, a, b, g: t[:, :, a:b].unsqueeze(2).to_broadcast([P, TILES, g, b - a])
    with stage(c.nc, "dve_step") as (block, dve_step):
        @block.vector
        def _(dve):
            step = Step(dve, dve_step)
            for off, a in ((0, 24), (32, 40)):
                rope(step, dve, heads[:, :, 0:10, off:off + 16], heads[:, :, 0:10, off + 16:off + 32],
                     table(c.rope_cos, a, a + 16, 10), table(c.rope_sin, a, a + 16, 10), [t[:] for t in tmp])
            kr = low[:, :, 384:416].unsqueeze(2)
            rope(step, dve, kr[:, :, :, 0:16], kr[:, :, :, 16:32], table(c.rope_cos, 8, 24, 1),
                 table(c.rope_sin, 8, 24, 1), [t[:, :, 0:1] for t in tmp])
            step(dve.tensor_copy(dqk[:, :, 640:704], dqk[:, :, 576:640]),
                 dve.tensor_copy(dqk[:, :, 704:768], dqk[:, :, 512:576]))

    mix = c.at("mix_rows", 175, [P, TILES, D])
    dT = c.at("d_parts", 38, [P, 2, 6, S], F32R)
    cols_in_parts(c, dqk, dT, TILES, 6)
    works = []
    for h in range(8):
        r, kv = slice(64 * (h % 2), 64 * (h % 2) + 64), h // 4
        kc = 4 if h % 2 == kv else 5
        for t in range(TILES):
            works.append(([dT[r, i, h // 2, t * P:(t + 1) * P] for i in (0, 1)],
                          [(a, [dT[r, i, kc, a:a + 512] for i in (0, 1)]) for a in (0, 512)],
                          [dv[:, j, kv * 64:(kv + 1) * 64] for j in range(TILES)], None,
                          mix[:, t, 512 + h * 64:512 + (h + 1) * 64], None))
    attention(c, works, HD ** -0.5, 86, lambda i: 1024)

    lowT = c.at("latent_cols", 38, [P, 3, S])
    rows_to_cols(c, low, lowT, TILES, 3)
    wq = c.at("w_cq_up", 50, [P, 2, 768])
    wkv = c.at("w_ckv_up", 56, [P, 1024])
    q = c.at("c_q_rows", 60, [P, TILES, 768])
    load(c, [(wq[:], dram["odd_w_cq_up"][0].rearrange("(k p) n -> p k n", p=P)), (wkv[:], dram["odd_w_ckv_up"][0])])
    linear(c, 2, [(0, lambda slot, k, t=t, h=h: (lowT[:, k, t * P:(t + 1) * P], wq[:, k, h * 384:(h + 1) * 384]), (P, 384))
                  for h in range(2) for t in range(TILES)], [], [None],
           (lambda u: True,
            lambda u, act, p: act.activation(q[:, u % 8, (u // 8) * 384:(u // 8 + 1) * 384], p, ACT.Copy), None))
    qr = q[:].rearrange("p t (h e) -> p t h e", e=96)
    tmp = [c.at("rope_tmp", 84 + 4 * i, [P, TILES, 8, 16]) for i in range(4)]
    with stage(c.nc, "dve_step") as (block, dve_step):
        @block.vector
        def _(dve):
            step = Step(dve, dve_step)
            rope(step, dve, qr[:, :, :, 64:80], qr[:, :, :, 80:96], table(c.rope_cos, 8, 24, 8),
                 table(c.rope_sin, 8, 24, 8), [t[:] for t in tmp])
    qT = c.at("c_q_cols", 143, [96, 8, S])
    transposes(c, [([q[:, t, h * 96:(h + 1) * 96] for t in range(a, a + 4)], qT[:, h, a * P:(a + 4) * P], None, None)
                   for a in (0, 4) for h in range(8)])
    vc = c.at("c_v_rows", 60, [P, TILES, 512])
    kc = c.at("c_k_rows", 76, [P, TILES, 768])
    kcr = kc[:].rearrange("p t (h e) -> p t h e", e=96)
    vcr = vc[:].rearrange("p t (h e) -> p t h e", e=64)

    def split_kv(u, dve, p):
        t, h = u % 8, u // 8
        p4 = p.rearrange("p (h e) -> p h e", e=128)
        dve.tensor_copy(kcr[:, t, 4 * h:4 * h + 4, 0:64], p4[:, :, 0:64])
        dve.tensor_copy(kcr[:, t, 4 * h:4 * h + 4, 64:96], low[:, t, 384:416].unsqueeze(1).to_broadcast([P, 4, 32]))
        return dve.tensor_copy(vcr[:, t, 4 * h:4 * h + 4, :], p4[:, :, 64:128])

    linear(c, 1, [(0, lambda slot, k, t=t, h=h: (lowT[:, 2, t * P:(t + 1) * P], wkv[:, h * 512:(h + 1) * 512]), (P, 512))
                  for h in range(2) for t in range(TILES)], [], [None], (lambda u: False, None, split_kv))
    kT = c.at("c_k_cols", 101, [96, 8, S])
    transposes(c, [([kc[:, t, h * 96:(h + 1) * 96] for t in range(a, a + 4)], kT[:, h, a * P:(a + 4) * P], None, None)
                   for a in (0, 4) for h in range(8)])
    works = [([qT[:, h, t * P:(t + 1) * P]], [(0, [kT[:, h, 0:512]]), (512, [kT[:, h, 512:1024]])],
              [vc[:, j, h * 64:(h + 1) * 64] for j in range(TILES)], None, mix[:, t, h * 64:(h + 1) * 64], None)
             for h in range(8) for t in range(TILES)]
    attention(c, works, 96.0 ** -0.5, 76, lambda i: 1024)
    out_and_residual(c, x, mix, dram["odd_w_out"][0])



def condition(c):
    nc, dram, ps = c.nc, c.dram, c.psum
    va, vb = c.at("vector_rows", 38, [P, P]), c.at("conv_rows", 38.5, [P, P])
    vT = c.at("vector_cols", 4.75, [P, 92])
    conv = c.at("conv_cols", 5.25, [P, 42])
    mod = c.at("modulation", 5.5, [P, 96])
    flat = lambda a: a.rearrange("(r p) -> r p", p=P)
    rows = [(0, flat(dram["b_ada_2"][0])), (48, flat(dram["c_2"][0])), (56, flat(dram["c_ctx_2"])),
            (64, dram["decay_w0_2"][0].rearrange("a (r p) -> (a r) p", p=P)),
            (72, dram["iclr_a0_2"][0].rearrange("a (r p) -> (a r) p", p=P)),
            (80, flat(dram["k_k_2"][0])), (84, flat(dram["k_a_2"][0])),
            (88, dram["r_k_2"][0].rearrange("(r a) e -> r (a e)", a=2))]
    with stage(nc, "cleared", "loaded", "turned", "copied") as (block, cleared, loaded, turned, copied):
        @block.gpsimd
        def _(pool):
            pool.memset(va[:], 0.0).then_inc(cleared, 1)
            pool.memset(vb[:], 0.0).then_inc(cleared, 1)

        @block.sync
        def _(sp):
            sp.wait_ge(cleared, 2)
            for r, src in rows:
                sp.dma_start(va[r:r + src.shape[0], :], src).then_inc(loaded, 16)
            for tap in range(3):
                cw = dram["conv_w_2"][0, tap]
                sp.dma_start(vb[14 * tap:14 * tap + 12, :], flat(cw[0:1536])).then_inc(loaded, 16)
                sp.dma_start(vb[14 * tap + 12:14 * tap + 13, 0:64], cw[1536:1600].unsqueeze(0)).then_inc(loaded, 16)
                sp.dma_start(vb[14 * tap + 13:14 * tap + 14, 0:96], cw[1600:1696].unsqueeze(0)).then_inc(loaded, 16)

        @block.tensor
        def _(pe):
            pe.wait_ge(loaded, 16 * (len(rows) + 9))
            pe.transpose(ps[:, 0, 0:P], va[:], c.ident[:])
            pe.transpose(ps[:, 1, 0:P], vb[:], c.ident[:]).then_inc(turned, 1)

        @block.vector
        def _(dve):
            dve.wait_ge(turned, 1)
            dve.tensor_copy(conv[:], ps[:, 1, 0:42])
            dve.tensor_copy(vT[:, 0:48], ps[:, 0, 0:48])
            dve.tensor_copy(vT[:, 64:92], ps[:, 0, 64:92]).then_inc(copied, 1)
            dve.wait_ge(copied, 1)

        @block.scalar
        def _(act):
            act.wait_ge(copied, 1)
            act.activation(vT[:, 48:64], ps[:, 0, 48:64], ACT.Silu).then_inc(copied, 1)
            act.wait_ge(copied, 2)
    c.vT, c.conv, c.mod = vT, conv, mod


def second_block(c, x):
    nc, dram, ps = c.nc, c.dram, c.psum
    vT, conv, mod = c.vT, c.conv, c.mod
    mod3 = mod[:].rearrange("p (i k a) -> p i k a", i=6, k=KT)
    mods = c.at("modulation_scales", 5.875, [P, 3, KT])
    with stage(nc, "dve_step") as (block, dve_step):
        @block.vector
        def _(dve):
            step = Step(dve, dve_step)
            step(dve.tensor_scalar(mods[:, 0], mod3[:, 1, :, 0], 1.0, None, ALU.add),
                 dve.tensor_scalar(mods[:, 1], mod3[:, 1, :, 1], 1.0, None, ALU.add),
                 dve.tensor_scalar(mods[:, 2], mod3[:, 4, :, 0], 1.0, None, ALU.add))

    hn = c.at("h_rows", 134, [P, TILES, D])
    rows_of = lambda name: dram[name].rearrange("(t p) d -> p t d", p=P)
    norm_rows(c, x, hn, TILES, dram["norm1_g_2"][0], 180, keep=rows_of("x_scratch"))
    hP = c.at("h_parts", 6, [P, 2, KT, S], F32R)
    hc = c.at("h_ctx_parts", 70, [P, 2, KT, CTX], F32R)
    turned = c.at("turned", 102, [P, 2, BANK])
    xc, hcn = c.at("ctx_rows", 110, [P, 2, D]), c.at("h_ctx_rows", 118, [P, 2, D])
    cols_in_parts(c, hn, hP, TILES, KT, turned, mods[:, 0], mod3[:, 0, :, 0],
                  [(xc[:], dram["ctx_2"][0].rearrange("(t p) d -> p t d", p=P))])
    norm_rows(c, xc, hcn, 2, dram["norm1_g_2"][0], 180)
    w_in = dram["w_in_2"][0]
    qk_spans = [(0, 256), (256, 512), (512, 768)]
    first = first_weights(c, w_in, qk_spans, 189)
    cols_in_parts(c, hcn, hc, 2, KT, turned, mods[:, 1], mod3[:, 0, :, 1], first[1])

    w_in = dram["w_in_2"][0]
    v = c.at("v_rows", 86, [P, 2 + TILES, 128])
    kx = c.at("ctx_k_rows", 91, [P, 2, 256])
    qk = c.at("qk_rows", 93, [P, TILES, 768])

    def copy_out(a, b, t, act, p):
        if b <= 512:
            return act.activation(qk[:, t, a:b], p, ACT.Copy)
        act.activation(qk[:, t, 512:640], p[:, 0:128], ACT.Copy)
        return act.activation(v[:, 2 + t], p[:, 128:256], ACT.Copy)

    def copy_ctx(a, b, t, act, p):
        act.activation(kx[:, t, 0:128], p[:, 0:128], ACT.Copy)
        act.activation(kx[:, t, 128:192], p[:, 64:128], ACT.Copy)
        act.activation(kx[:, t, 192:256], p[:, 0:64], ACT.Copy)
        return act.activation(v[:, t], p[:, 128:256], ACT.Copy)

    linear_in_parts(c, hP, w_in, qk_spans, 189, 157, TILES, lambda a: True, copy_out, first=first)
    linear_in_parts(c, hc, w_in, [(512, 768)], 189, 157, 2, lambda a: True, copy_ctx)
    heads = qk[:].rearrange("p t (h e) -> p t h e", e=HD)
    tmp = [c.at("rope_tmp", 147 + 10 * i, [P, TILES, 10, 32]) for i in range(4)]
    table = lambda t: t[:, :, 24:56].unsqueeze(2).to_broadcast([P, TILES, 10, 32])
    with stage(nc, "dve_step") as (block, dve_step):
        @block.vector
        def _(dve):
            step = Step(dve, dve_step)
            rope(step, dve, heads[:, :, 0:10, 0:32], heads[:, :, 0:10, 32:64], table(c.rope_cos),
                 table(c.rope_sin), [t[:] for t in tmp])
            step(dve.tensor_copy(qk[:, :, 640:704], qk[:, :, 576:640]),
                 dve.tensor_copy(qk[:, :, 704:768], qk[:, :, 512:576]))
    qkT = c.at("qk_parts", 147, [P, 2, 6, T_ALL], F32R)
    cols_in_parts(c, qk, qkT[:, :, :, CTX:], TILES, 6)
    cols_in_parts(c, kx, qkT[:, :, 4:6, 0:CTX], 2, 2)
    bias = c.at("window_bias", 93, [P, 2, 640])
    sinks = c.at("sinks", 98, [P, 2, 8])
    ya = c.at("ya_rows", 124, [P, TILES, 512])
    load(c, [(bias[:], dram["const_window_bias"]), (sinks[:, 1], dram["sink_2"][0].partition_broadcast(P))])
    with stage(nc, "dve_step") as (block, dve_step):
        @block.vector
        def _(dve):
            Step(dve, dve_step)(dve.tensor_scalar(sinks[:, 0], sinks[:, 1], float(HD) ** 0.5, None, ALU.mult))
    works = []
    for h in range(8):
        r, kv = slice(64 * (h % 2), 64 * (h % 2) + 64), h // 4
        kc = 4 if h % 2 == kv else 5
        for t in range(TILES):
            a, b = max(t - 1, 0), min(t + 2, TILES)
            n = (b - a) * P
            first = min(n, 256)
            keys = lambda a, b: [qkT[r, i, kc, a:b] for i in (0, 1)]
            pieces = [(0, keys(0, CTX)), (CTX, keys(CTX + a * P, CTX + a * P + first))]
            if n > first:
                pieces.append((512, keys(CTX + a * P + first, CTX + b * P)))
            works.append(([qkT[r, i, h // 2, CTX + t * P:CTX + (t + 1) * P] for i in (0, 1)], pieces,
                          [v[:, j, kv * 64:(kv + 1) * 64] for j in [0, 1] + list(range(2 + a, 2 + b))],
                          bias[:, 0 if t else 1, 0:CTX + n], ya[:, t, h * 64:(h + 1) * 64], h))
    attention(c, works, HD ** -0.5, 99, lambda i: works[i][3].shape[1], (sinks[:, 0], sinks[:, 1]), fillers=4)

    spans = [(a, a + 256) for a in range(0, D, 256)]
    gate_spans = lambda start: [(start + a, start + b) for a, b in spans]
    y_parts = c.at("branch_parts", 175, [P, 2, 4, S], F32R)
    first = first_weights(c, w_in, gate_spans(3488), 86)
    cols_in_parts(c, ya, y_parts, TILES, 4, loads=first[1])
    gate = c.at("gate_rows", 134, [P, TILES, D])

    def sigmoid_of(start):
        return lambda a, b, t, act, p: act.activation(gate[:, t, a - start:b - start], p, ACT.Sigmoid)

    linear_in_parts(c, hP, w_in, gate_spans(3488), 86, 102, TILES, lambda a: True, sigmoid_of(3488),
                    store=(rows_of("g_scratch"), gate), first=first)
    linear_in_parts(c, hP, w_in, gate_spans(2464), 86, 102, TILES, lambda a: True, sigmoid_of(2464))
    linear_in_parts(c, y_parts, dram["w_branch_attn_2"][0], spans, 86, 102, TILES, lambda a: False,
                    lambda a, b, t, dve, p: dve.tensor_tensor(gate[:, t, a:b], p, gate[:, t, a:b], ALU.mult), kt=4,
                    store=(rows_of("h_scratch"), gate))

    yr = rwkv(c, hP, hc, w_in, conv, vT)
    m = c.at("merged_rows", 118, [P, TILES, D])
    gate = c.at("gate_rows", 86, [P, TILES, D])
    first = first_weights(c, dram["w_branch_rwkv_2"][0], spans, 74, 4)
    cols_in_parts(c, yr, y_parts, TILES, 4,
                  loads=[(m[:], rows_of("h_scratch")), (gate[:], rows_of("g_scratch"))] + first[1])
    gt = c.at("gated", 166, [P, 2, 256])
    counter = c.nc.alloc_semaphore("second_term_ready")

    def add_second(a, b, t, dve, p):
        u = a // 256 * TILES + t
        dve.tensor_tensor(gt[:, u % 2], p, gate[:, t, a:b], ALU.mult).then_inc(counter, 1)
        dve.wait_ge(counter, u + 1)
        return dve.tensor_tensor(m[:, t, a:b], m[:, t, a:b], gt[:, u % 2], ALU.add)

    linear_in_parts(c, y_parts, dram["w_branch_rwkv_2"][0], spans, 74, 150, TILES, lambda a: False, add_second, kt=4,
                    first=first)
    c.nc.clear_and_free_semaphores([counter])
    c.nc.all_engine_barrier()
    mT = c.at("merged_parts", 38, [P, 2, KT, S], F32R)
    cols_in_parts(c, m, mT, TILES, KT, loads=[(x[:], rows_of("x_scratch"))])
    g1, g2 = c.at("gate1_rows", 102, [P, D]), c.at("gate2_rows", 106, [P, D])
    spread = c.at("gate_spread", 110, [P, 2, KT, P])
    first = first_weights(c, dram["w_out_2"][0], spans, 118)
    for j, (g, i) in enumerate(((g1, 2), (g2, 5))):
        with stage(nc, "spread_out") as (block, spread_out):
            @block.vector
            def _(dve):
                dve.tensor_copy(spread[:, j], mod3[:, i, :, 0].unsqueeze(2).to_broadcast([P, KT, P]))\
                   .then_inc(spread_out, 1)
                dve.wait_ge(spread_out, 1)
        transposes(c, [([spread[:, j, k] for k in range(a, a + 4)], g[:, a * P:(a + 4) * P], None, None)
                       for a in (0, 4)], first[1] if j else ())
    gt = c.at("gated_out", 166, [P, 2, 256])
    counter = c.nc.alloc_semaphore("gated_out_ready")

    def add_gated(a, b, t, dve, p):
        u = a // 256 * TILES + t
        dve.tensor_tensor(gt[:, u % 2], p, g1[:, a:b], ALU.mult).then_inc(counter, 1)
        dve.wait_ge(counter, u + 1)
        return dve.tensor_tensor(x[:, t, a:b], x[:, t, a:b], gt[:, u % 2], ALU.add)

    linear_in_parts(c, mT, dram["w_out_2"][0], spans, 118, 134, TILES,
                    lambda a: False, add_gated, first=first)
    c.nc.clear_and_free_semaphores([counter])
    c.nc.all_engine_barrier()

    g2k = c.at("gate2_rows_kept", 200, [P, D])
    with stage(nc, "moved") as (block, moved):
        @block.vector
        def _(dve):
            dve.tensor_copy(g2k[:], g2[:]).then_inc(moved, 1)
            dve.wait_ge(moved, 1)
    norm_rows(c, x, hn, TILES, dram["norm2_g_2"][0], 180)
    h = c.at("h_parts", 38, [P, 2, KT, S], F32R)
    up_raw, down_raw = c.at("up_raw", 102, [P, 2, KT, 256]), c.at("down_raw", 118, [P, 2, 2, D])
    w_up = dram["w_mlp_up_2"][0].rearrange("(k p) n -> p k n", p=P)
    w_down = dram["w_mlp_down_2"][0].rearrange("(s k p) n -> s p k n", p=P, k=2)
    cols_in_parts(c, hn, h, TILES, KT, c.at("turned", 166, [P, 2, BANK]), mods[:, 2], mod3[:, 3, :, 0],
                  [(up_raw[:, 0], w_up[:, :, 0:256]), (up_raw[:, 1], w_up[:, :, 256:512]),
                   (down_raw[:, 0], w_down[0]), (down_raw[:, 1], w_down[1])])
    mlp(c, x, h, up_raw, down_raw, w_up, w_down,
        c.at("up_parts", 134, [P, 2, KT, 256], F32R), c.at("down_parts", 150, [P, 2, 2, D], F32R),
        c.at("hidden_parts", 166, [P, 2, 2, S], F32R), c.at("relu_and_square", 182, [P, 2, 2, BANK]),
        c.at("gated_rows", 190, [P, 4, BANK]), g2k)


def mlp(c, x, h, up_raw, down_raw, w_up, w_down, up, down, hidden, act_tmp, gated, gate):
    nc, dram, ps = c.nc, c.dram, c.psum
    steps = 4 * D // 256
    with stage(nc, "up_loaded_0", "up_loaded_1", "down_loaded_0", "down_loaded_1", "up_high", "up_split",
               "down_high", "down_split", "up_done", "relu_done", "squared", "hidden_high", "hidden_split",
               "down_done", "gated_ready", "added") as (
            block, u0, u1, d0, d1, up_high, up_split, down_high, down_split, up_done, relu_done, squared,
            hidden_high, hidden_split, down_done, gated_ready, added):
        up_loaded, down_loaded = (u0, u1), (d0, d1)

        @block.sync
        def _(sp):
            for s in range(2, steps):
                sp.wait_ge(up_split, s - 1)
                sp.dma_start(up_raw[:, s % 2], w_up[:, :, s * 256:(s + 1) * 256]).then_inc(up_loaded[s % 2], 16)
                sp.wait_ge(down_split, s - 1)
                sp.dma_start(down_raw[:, s % 2], w_down[s]).then_inc(down_loaded[s % 2], 16)

        @block.tensor
        def _(pe):
            def do_up(s):
                pe.wait_ge(up_split, s + 1)
                for i in range(4):
                    half, f = i // 2, i % 2
                    if s >= 1:
                        pe.wait_ge(relu_done, 4 * (s - 1) + i + 1)
                    for n, (a, b) in enumerate(PARTS):
                        for k in range(KT):
                            last = pe.matmul(ps[:, i, :], up[:, a, k, f * P:(f + 1) * P],
                                             h[:, b, k, half * 512:(half + 1) * 512],
                                             start=(n == 0 and k == 0), stop=(n == 2 and k == KT - 1))
                    last.then_inc(up_done, 1)

            def do_down(s):
                pe.wait_ge(down_split, s + 1)
                for i in range(16):
                    u = 16 * s + i
                    t, half = i // 2, i % 2
                    if t % 4 == 0:
                        pe.wait_ge(hidden_split, 4 * s + 2 + 2 * (t // 4))
                    if u >= 4:
                        pe.wait_ge(gated_ready, u - 3)
                    for n, (a, b) in enumerate(PARTS):
                        for k in range(2):
                            last = pe.matmul(ps[:, 4 + i % 4, :], hidden[:, a, k, t * P:(t + 1) * P],
                                             down[:, b, k, half * 512:(half + 1) * 512],
                                             start=(n == 0 and k == 0), stop=(n == 2 and k == 1))
                    last.then_inc(down_done, 1)

            do_up(0)
            for s in range(steps):
                if s + 1 < steps:
                    do_up(s + 1)
                do_down(s)

        @block.scalar
        def _(act):
            def up_hi(s):
                if s >= 2:
                    act.wait_ge(up_loaded[s % 2], 16 * (s // 2))
                if s >= 1:
                    act.wait_ge(up_done, 4 * s)
                act.activation(up[:, 0], up_raw[:, s % 2], ACT.Copy).then_inc(up_high, 1)

            def down_hi(s):
                if s >= 2:
                    act.wait_ge(down_loaded[s % 2], 16 * (s // 2))
                if s >= 1:
                    act.wait_ge(down_done, 16 * s)
                act.activation(down[:, 0], down_raw[:, s % 2], ACT.Copy).then_inc(down_high, 1)

            def square(s, half):
                for i in (2 * half, 2 * half + 1):
                    u = 4 * s + i
                    act.wait_ge(up_done, u + 1)
                    act.activation(act_tmp[:, 0, i % 2], ps[:, i, :], ACT.Relu).then_inc(relu_done, 1)
                    act.wait_ge(relu_done, u + 1)
                    if u >= 2:
                        act.wait_ge(hidden_split, u - 1)
                    act.activation(act_tmp[:, 1, i % 2], act_tmp[:, 0, i % 2], ACT.Square).then_inc(squared, 1)
                    act.wait_ge(squared, u + 1)
                    if s >= 1:
                        act.wait_ge(down_done, 16 * (s - 1) + 8 * (half + 1))
                    act.activation(hidden[:, 0, i % 2, half * 512:(half + 1) * 512], act_tmp[:, 1, i % 2],
                                   ACT.Copy).then_inc(hidden_high, 1)

            up_hi(0)
            down_hi(0)
            up_hi(1)
            square(0, 0)
            for s in range(steps):
                square(s, 1)
                if s >= 1:
                    down_hi(s)
                if s + 2 < steps:
                    up_hi(s + 2)
                if s + 1 < steps:
                    square(s + 1, 0)

        @block.vector
        def _(dve):
            def up_lo(s):
                dve.wait_ge(up_high, s + 1)
                dve.tensor_tensor(up[:, 1], up_raw[:, s % 2], up[:, 0].bitcast(F32), ALU.subtract)\
                   .then_inc(up_split, 1)

            def down_lo(s):
                dve.wait_ge(down_high, s + 1)
                dve.tensor_tensor(down[:, 1], down_raw[:, s % 2], down[:, 0].bitcast(F32), ALU.subtract)\
                   .then_inc(down_split, 1)

            def hidden_lo(s, half):
                for i in (2 * half, 2 * half + 1):
                    dve.wait_ge(hidden_high, 4 * s + i + 1)
                    cols = slice(half * 512, (half + 1) * 512)
                    dve.tensor_tensor(hidden[:, 1, i % 2, cols], act_tmp[:, 1, i % 2],
                                      hidden[:, 0, i % 2, cols].bitcast(F32), ALU.subtract)\
                       .then_inc(hidden_split, 1)

            def add(s, tiles):
                for i in range(2 * tiles[0], 2 * tiles[-1] + 2):
                    u = 16 * s + i
                    t, cols = i // 2, slice((i % 2) * 512, (i % 2 + 1) * 512)
                    dve.wait_ge(down_done, u + 1)
                    dve.tensor_tensor(gated[:, u % 4], ps[:, 4 + i % 4, :], gate[:, cols], ALU.mult)\
                       .then_inc(gated_ready, 1)
                    if u >= 1:
                        add_up(u - 1)

            def add_up(u):
                t, cols = u % 16 // 2, slice((u % 2) * 512, (u % 2 + 1) * 512)
                dve.wait_ge(gated_ready, u + 1)
                if u >= 16:
                    dve.wait_ge(added, u - 15)
                dve.tensor_tensor(x[:, t, cols], x[:, t, cols], gated[:, u % 4], ALU.add).then_inc(added, 1)

            up_lo(0)
            down_lo(0)
            up_lo(1)
            hidden_lo(0, 0)
            for s in range(steps):
                hidden_lo(s, 1)
                if s >= 1:
                    down_lo(s)
                if s + 2 < steps:
                    up_lo(s + 2)
                add(s, range(0, 4))
                if s + 1 < steps:
                    hidden_lo(s + 1, 0)
                add(s, range(4, 8))
            add_up(16 * steps - 1)
            dve.wait_ge(added, 16 * steps)



def rwkv(c, h, hc, w_in, conv, vT):
    nc, dram, ps = c.nc, c.dram, c.psum
    widths = [P] * 12 + [64, 96]
    starts = [768 + P * j for j in range(12)] + [768 + 1536, 768 + 1600]
    U0, U1 = 1, CTX + 2
    ub = c.at("conv_in", 110, [P, 2, T_ALL + 3])
    rw = c.at("rwkv_cols", 120.5, [P, 14, T_ALL])
    raw = c.at("weights_raw", 86, [P, 2, KT, P])
    part = c.at("weight_parts", 94, [P, 2, 2, KT, P], F32R)
    w_rows = w_in.rearrange("(k p) n -> p k n", p=P)
    parts = [(0, CTX, U0), (0, 512, U1), (512, 1024, U1 + 512)]
    with stage(nc, "weights_loaded_0", "weights_loaded_1", "high_ready", "low_ready", "edges_cleared", "summed",
               "copied", "convolved", "dve_step") as (
            block, l0, l1, high, low, edges, summed, copied, convolved, dve_step):
        loaded = (l0, l1)

        @block.sync
        def _(sp):
            for j in range(14):
                if j >= 2:
                    sp.wait_ge(low, j - 1)
                sp.dma_start(raw[:, j % 2, :, 0:widths[j]], w_rows[:, :, starts[j]:starts[j] + widths[j]])\
                  .then_inc(loaded[j % 2], 16)

        @block.gpsimd
        def _(pool):
            for col in (0, CTX + 1, T_ALL + 2):
                pool.memset(ub[:, :, col:col + 1], 0.0).then_inc(edges, 1)

        @block.tensor
        def _(pe):
            for j in range(14):
                pe.wait_ge(low, j + 1)
                for i, (a, b, _) in enumerate(parts):
                    u = 3 * j + i
                    if u >= 6:
                        pe.wait_ge(copied, u - 5)
                    for m, (v, w) in enumerate(PARTS):
                        for k in range(KT):
                            rhs = hc[:, w, k, a:b] if i == 0 else h[:, w, k, a:b]
                            last = pe.matmul(ps[0:widths[j], u % 6, 0:b - a], part[:, j % 2, v, k, 0:widths[j]], rhs,
                                             start=(m == 0 and k == 0), stop=(m == 2 and k == KT - 1))
                    last.then_inc(summed, 1)

        @block.scalar
        def _(act):
            def split(j):
                act.wait_ge(loaded[j % 2], 16 * (j // 2 + 1))
                if j >= 2:
                    act.wait_ge(summed, 3 * (j - 1))
                act.activation(part[:, j % 2, 0, :, 0:widths[j]], raw[:, j % 2, :, 0:widths[j]], ACT.Copy)\
                   .then_inc(high, 1)

            split(0)
            for j in range(14):
                if j + 1 < 14:
                    split(j + 1)
                if j >= 2:
                    act.wait_ge(convolved, j - 1)
                for i, (a, b, o) in enumerate(parts):
                    u = 3 * j + i
                    act.wait_ge(summed, u + 1)
                    act.activation(ub[0:widths[j], j % 2, o:o + b - a], ps[0:widths[j], u % 6, 0:b - a], ACT.Copy)\
                       .then_inc(copied, 1)

        @block.vector
        def _(dve):
            step = Step(dve, dve_step)

            def split(j):
                dve.wait_ge(high, j + 1)
                dve.tensor_tensor(part[:, j % 2, 1, :, 0:widths[j]], raw[:, j % 2, :, 0:widths[j]],
                                  part[:, j % 2, 0, :, 0:widths[j]].bitcast(F32), ALU.subtract).then_inc(low, 1)

            split(0)
            dve.wait_ge(edges, 3)
            for j in range(14):
                if j + 1 < 14:
                    split(j + 1)
                dve.wait_ge(copied, 3 * j + 3)
                n = widths[j]
                tap = lambda i: conv[0:n, 14 * i + j:14 * i + j + 1]
                for s, (o, n_tok, d) in enumerate(((U0, CTX, 0), (U1, S, CTX))):
                    u, out = ub[0:n, j % 2], rw[0:n, j, d:d + n_tok]
                    step(dve.tensor_scalar(out, u[:, o - 1:o - 1 + n_tok], tap(0), None, ALU.mult))
                    step(dve.scalar_tensor_tensor(out, u[:, o:o + n_tok], tap(1), out, ALU.mult, ALU.add))
                    step(dve.scalar_tensor_tensor(out, u[:, o + 1:o + 1 + n_tok], tap(2), out, ALU.mult, ALU.add))
                dve.nop().then_inc(convolved, 1)

    NT = T_ALL // P
    vrow = c.at("v_rows", 38, [P, NT, 512])
    rows = []
    for a in range(0, NT, 4):
        n = min(4, NT - a)
        for j in range(4):
            for t in range(a, a + n):
                rows.append(([rw[:, 8 + j, t * P:(t + 1) * P]], vrow[:, t, j * P:(j + 1) * P], None, None))
    transposes(c, rows)

    kk = rw[:, 8:12, :]
    r_, k_ = rw[:, 0:4, :], rw[:, 4:8, :]
    sq = c.at("kk_squares", 58, [P, 4, T_ALL])
    blocks = c.at("head_blocks", 98, [P, P])
    load(c, [(blocks[:], dram["const_head_blocks"])])
    with stage(nc, "squared", "summed", "rooted", "dve_step", "normalised") as (
            block, squared, summed, rooted, dve_step, normalised):
        pieces = [(j, a, min(a + 512, T_ALL)) for j in range(4) for a in range(0, T_ALL, 512)]

        @block.vector
        def _(dve):
            step = Step(dve, dve_step)
            for i, (j, a, b) in enumerate(pieces):
                dve.wait_ge(summed, i + 1)
                dve.tensor_scalar(sq[:, j, a:b], ps[:, i % 8, 0:b - a], 1e-24, None, ALU.max).then_inc(normalised, 1)
            dve.wait_ge(rooted, 1)
            step(dve.reciprocal(sq[:], sq[:]))
            step(dve.tensor_tensor(kk, kk, sq[:], ALU.mult))

        @block.tensor
        def _(pe):
            for i, (j, a, b) in enumerate(pieces):
                pe.wait_ge(squared, 2 * j + 2)
                if i >= 8:
                    pe.wait_ge(normalised, i - 7)
                pe.matmul(ps[:, i % 8, 0:b - a], blocks[:], sq[:, j, a:b], start=True, stop=True).then_inc(summed, 1)

        @block.scalar
        def _(act):
            for j in range(4):
                act.activation(sq[:, j], k_[:, j], ACT.Square, scale=vT[:, 80 + j:81 + j]).then_inc(squared, 1)
                act.activation(kk[:, j], k_[:, j], ACT.Copy, scale=vT[:, 80 + j:81 + j]).then_inc(squared, 1)
            act.wait_ge(normalised, len(pieces))
            act.activation(sq[:], sq[:], ACT.Sqrt).then_inc(rooted, 1)

    lora = rw[:, 12, :]
    y = c.at("y_rows", 58, [P, TILES, 512])
    sc = c.at("bonus_rows", 34, [P, TILES, 8])
    ka = c.at("k_a_vectors", 36.5, [P, 2, 4])
    half = c.at("half_biases", 36.625, [P, 16])
    rks = c.at("r_k_heads", 36.75, [P, 4, 8])
    mk = c.at("order_masks", 37, [P, 2, 64])
    keep = c.at("chunk_starts", 0.75, [P, 512])
    m1 = c.at("neighbour_mask", 2.75, [P, 64])
    m1T = c.at("neighbour_mask_turned", 3, [P, 64])
    eye = c.at("chunk_identity", 3.25, [P, 64])
    lm = c.at("level_masks", 3.5, [P, 5, 32])
    w2 = c.at("lora_weights", 114, [64, 2, 512])
    streams = []
    for g in (0, 1):
        b = Stream()
        (b.lw, b.F, b.e1, b.e2, b.e3, b.rate, b.kd, b.bt, b.kt, b.bb, b.kb, b.rk) = (
            c.at(name, 6 + 14 * g + n, [P, 2, P]) for n, name in enumerate((
                "log_decay", "running_log", "exp_after", "exp_before", "exp_inverse", "rate", "key", "b_scaled",
                "k_scaled", "b_to_end", "k_to_end", "r_times_key")))
        b.ar = c.at("a_and_r", 18 + 14 * g, [P, 2, 2, P])
        H = 74 + 14.625 * g
        b.LL = c.at("pairs", H, [P, 2, 2, 2, 2, 64])
        b.M = c.at("inverse", H + 4, [P, 4, 64])
        b.MT = c.at("inverse_turned", H + 5, [P, 4, 64])
        b.X = c.at("below_diagonal", H + 6, [P, 4, 32])
        b.tm = c.at("abk_rows", H + 6.5, [P, 3, 256])
        b.W1 = c.at("a_inverse", H + 9.5, [P, 2, 2, 64])
        b.LKV = c.at("L_k_v", H + 10.5, [P, 4, 64])
        b.P1 = c.at("from_values", H + 11.5, [P, 4, 64])
        b.U = c.at("U", H + 12.5, [P, 4, 64])
        b.S = c.at("state", H + 13.5, [P, 2, 64])
        b.SG = c.at("state_decayed", H + 14, [P, 2, 64])
        b.ge = c.at("decay_to_end", H + 14.5, [P, 4])
        streams.append(b)
    DEC = float(np.exp(-0.5))
    load(c, [(keep[:], dram["const_chunk_starts"]), (eye[:], dram["const_chunk_identity"])])
    with stage(nc, "dve_step", "tanh_done") as (block, dve_step, tanh_done):
        @block.scalar
        def _(act):
            act.activation(rw[0:32, 12, :], rw[0:32, 12, :], ACT.Tanh).then_inc(tanh_done, 1)
            act.wait_ge(tanh_done, 1)

        @block.vector
        def _(dve):
            step = Step(dve, dve_step)
            step(dve.tensor_copy(ka[:, 0], vT[:, 84:88]),
                 dve.tensor_scalar(ka[:, 1], vT[:, 84:88], -1.0, 1.0, ALU.mult, ALU.add),
                 dve.tensor_scalar(half[:], vT[:, 64:80], 0.5, None, ALU.mult),
                 dve.memset(rks[:], 0.0), dve.memset(sc[:], 0.0), dve.memset(w2[:], 0.0))
            for h in range(8):
                r = slice(64 * (h % 2), 64 * (h % 2) + 64)
                step(dve.tensor_copy(rks[r, h // 2, h:h + 1], vT[r, 88 + h // 2:89 + h // 2]))
    for d in range(2):
        cm = dram["const_scan_masks"][d]
        load(c, [(mk[:], cm[:, 0:128].rearrange("p (a t) -> p a t", a=2)), (m1[:], cm[:, 128:192]),
                 (m1T[:], cm[:, 192:256]), (lm[:], cm[:, 256:416].rearrange("p (a t) -> p a t", a=5)),
                 (w2[0:32, 0], dram["decay_w2_2"][0, d]), (w2[32:64, 1], dram["iclr_a2_2"][0, d])])
        scan(c, d, list(range(NT)) if d == 0 else [1, 0] + list(range(NT - 1, 1, -1)), locals())

    hg = rw[0:96, 13, CTX:]
    sq = c.at("squares", 74, [P, TILES, 8, 64])
    lnw, lnb = c.at("lnx_w_rows", 90, [P, 512]), c.at("lnx_b_rows", 92, [P, 512])
    g2 = c.at("gate_g2", 94, [96, 512])
    st = c.at("stats", 96, [P, 3, TILES, 8])
    lneps = c.at("lnx_eps", 98, [P, 1])
    y4 = y[:].rearrange("p t (h e) -> p t h e", e=64)
    wide = lambda a: a.unsqueeze(3).to_broadcast([P, TILES, 8, 64])
    along = lambda a: a[:].unsqueeze(1).to_broadcast([P, TILES, 512])
    load(c, [(lnw[:], dram["lnx_w_2"][0].partition_broadcast(P)), (lnb[:], dram["lnx_b_2"][0].partition_broadcast(P)),
             (g2[:], dram["gate_g2_2"][0])])
    with stage(nc, "variance_ready", "root_ready", "gate_open", "gates_ready", "gated", "dve_step") as (
            block, variance, root, gate_open, gates_ready, gated, dve_step):
        @block.scalar
        def _(act):
            act.activation(hg, hg, ACT.Sigmoid).then_inc(gate_open, 1)
            act.wait_ge(variance, 1)
            act.activation(st[:, 1], st[:, 0], ACT.Sqrt, scale=1.0 / 64, bias=lneps[:, 0:1]).then_inc(root, 1)

        @block.tensor
        def _(pe):
            pe.wait_ge(gate_open, 1)
            for t in range(TILES):
                pe.matmul(ps[:, t, :], rw[0:96, 13, CTX + t * P:CTX + (t + 1) * P], g2[:], start=True, stop=True)\
                  .then_inc(gates_ready, 1)

        @block.vector
        def _(dve):
            step = Step(dve, dve_step)
            step(dve.memset(lneps[:], LNX_EPS))
            step(dve.tensor_reduce(st[:, 2], y4, AX.X, ALU.add))
            step(dve.tensor_scalar(st[:, 2], st[:, 2], 1.0 / 64, None, ALU.mult))
            step(dve.tensor_tensor(y4, y4, wide(st[:, 2]), ALU.subtract))
            step(dve.tensor_tensor(sq[:], y4, y4, ALU.mult))
            dve.tensor_reduce(st[:, 0], sq[:], AX.X, ALU.add).then_inc(variance, 1)
            dve.wait_ge(root, 1)
            step(dve.reciprocal(st[:, 2], st[:, 1]))
            step(dve.tensor_tensor(y4, y4, wide(st[:, 2]), ALU.mult),
                 dve.tensor_tensor(sq[:], vrow[:, 2:NT].rearrange("p t (h e) -> p t h e", e=64), wide(sc[:]), ALU.mult))
            step(dve.tensor_tensor(y[:], y[:], along(lnw), ALU.mult))
            step(dve.tensor_tensor(y[:], y[:], along(lnb), ALU.add))
            step(dve.tensor_tensor(y4, y4, sq[:], ALU.add))
            for t in range(TILES):
                dve.wait_ge(gates_ready, t + 1)
                dve.tensor_tensor(y[:, t], y[:, t], ps[:, t, :], ALU.mult).then_inc(gated, 1)
            dve.wait_ge(gated, TILES)
    return y


def take_turns(first, second, lag):
    live = [first, second]
    for _ in range(lag):
        next(first)
    while live:
        for s in list(live):
            if next(s, "end") == "end":
                live.remove(s)


def scan(c, d, tiles, m):
    nc, ps = c.nc, c.psum
    (rw, vrow, y, sc, ka, half, rks, mk, keep, m1, m1T, w2, lm, eye, kk, r_, k_, DEC) = (m[n] for n in (
        "rw vrow y sc ka half rks mk keep m1 m1T w2 lm eye kk r_ k_ DEC").split())
    streams = m["streams"]
    tok = lambda t: slice(t * P, (t + 1) * P)
    half_of = lambda par: slice(64 * par, 64 * par + 64)
    order = (0, 1) if d == 0 else (1, 0)
    flat = lambda a: a[:].rearrange("p a b -> p (a b)")
    halves = lambda a: a[:].rearrange("p j (q n) -> p (j q) n", q=2)
    end = lambda a: a.unsqueeze(2).to_broadcast([P, 4, 64])
    HEADS = [(par, jj) for par in (0, 1) for jj in (0, 1)]
    slot = lambda par, jj: 2 * par + jj
    CH = [(cc, half_of(cc)) for cc in (0, 1)]

    def first_blocks(a, level):
        v = a.rearrange("p (g two n) -> p g two n", two=2, n=2 << level) if len(a.shape) == 2 else \
            a.rearrange("p h (g two n) -> p h g two n", two=2, n=2 << level)
        return v[:, :, d, :] if len(a.shape) == 2 else v[:, :, :, d, :]

    names = ("lora_done", "tanh_done", "logs_ready", "exps_ready", "scaled", "ends_scaled", "pairs_done",
             "pairs_masked", "abk_turned", "abk_copied", "l_turned", "m_ready", "mt_started", "x_done", "x_masked",
             "m_done", "mt_turned", "mt_copied", "w1_done", "w1_copied", "lkv_done", "lkv_copied", "p1_done",
             "p1_copied", "u_done", "u_ready", "s_done", "state_ready", "y_done", "tile_done", "state_cleared")
    both = [f"{n}_{g}" for g in (0, 1) for n in names]
    with stage(nc, "dve_step", *both) as (block, dve_step, *sems):
        sem = [dict(zip(names, sems[g * len(names):(g + 1) * len(names)])) for g in (0, 1)]

        @block.tensor
        def _(pe):
            def stream(g):
                b, s = streams[g], sem[g]
                B = 4 * g
                for i, t in enumerate(tiles):
                    emit = t >= 2
                    if i >= 1:
                        pe.wait_ge(s["tile_done"], i)
                    for kind in (0, 1):
                        for jj in (0, 1):
                            j = 2 * g + jj
                            last = pe.matmul(ps[:, B, (2 * kind + jj) * P:(2 * kind + jj + 1) * P],
                                             w2[:, kind, j * P:(j + 1) * P], rw[0:64, 12, tok(t)], start=True, stop=True)
                    last.then_inc(s["lora_done"], 1)
                    yield
                    yield
                    pe.wait_ge(s["scaled"], i + 1)
                    for kind, key in ((0, b.bt), (1, b.kt)):
                        for jj in (0, 1):
                            for cc, C in CH:
                                for par in (0, 1):
                                    o = (2 * kind + jj) * P
                                    last = pe.matmul(ps[C, B + 1 + par, o:o + P].rearrange("p (a n) -> p a n", a=2),
                                                     key[half_of(par), jj, C], b.ar[half_of(par), jj, :, C],
                                                     start=True, stop=True)
                    last.then_inc(s["pairs_done"], 1)
                    yield
                    pe.wait_ge(s["ends_scaled"], i + 1)
                    pe.wait_ge(s["tanh_done"], i + 1)
                    for n, src in enumerate((b.ar[:, :, 0, :], b.bb, b.kb)):
                        for jj in (0, 1):
                            col = n * 256 + jj * P
                            last = pe.transpose(ps[:, B + 3 if n < 2 else B, col % 512:col % 512 + P], src[:, jj],
                                                c.ident[:])
                    last.then_inc(s["abk_turned"], 1)
                    pe.wait_ge(s["pairs_masked"], i + 1)
                    for par, jj in HEADS:
                        for cc, C in CH:
                            last = pe.matmul(ps[C, B + 1, slot(par, jj) * 64:(slot(par, jj) + 1) * 64],
                                             b.LL[C, par, 0, jj, 0, :], c.ident[C, C], start=True, stop=True)
                    last.then_inc(s["l_turned"], 1)
                    for par, jj in HEADS:
                        h = 4 * g + 2 * jj + par
                        for cc, C in CH:
                            last = pe.matmul(ps[C, B + 2, slot(par, jj) * 64:(slot(par, jj) + 1) * 64],
                                             b.LL[C, par, 1, jj, 0, :], vrow[C, t, h * 64:(h + 1) * 64],
                                             start=True, stop=True)
                    last.then_inc(s["lkv_done"], 1)
                    yield
                    pe.wait_ge(s["mt_started"], i + 1)
                    pe.wait_ge(s["abk_copied"], i + 1)
                    pe.wait_ge(s["lkv_copied"], i + 1)

                    def turn_inverse():
                        for h4 in range(4):
                            for cc, C in CH:
                                last = pe.matmul(ps[C, B + 3, h4 * 64:(h4 + 1) * 64], b.M[C, h4], c.ident[C, C],
                                                 start=True, stop=True)
                        last.then_inc(s["mt_turned"], 1)

                    for level in range(5):
                        n = 5 * i + level
                        pe.wait_ge(s["m_ready"], n + i + 1)
                        if level:
                            turn_inverse()
                        for par, jj in HEADS:
                            h4 = slot(par, jj)
                            for cc, C in CH:
                                last = pe.matmul(ps[C, B + 1, h4 * 32:(h4 + 1) * 32], b.LL[C, par, 0, jj, 0, :],
                                                 first_blocks(b.M[C, h4], level), start=True, stop=True)
                        last.then_inc(s["x_done"], 1)
                        yield
                        pe.wait_ge(s["x_masked"], n + 1)
                        if level:
                            pe.wait_ge(s["mt_copied"], n)
                        for h4 in range(4):
                            for cc, C in CH:
                                last = pe.matmul(ps[C, B + 2, h4 * 32:(h4 + 1) * 32], b.MT[C, h4], b.X[C, h4],
                                                 start=True, stop=True)
                        last.then_inc(s["m_done"], 1)
                        yield
                    pe.wait_ge(s["m_ready"], 6 * i + 6)
                    turn_inverse()
                    yield
                    pe.wait_ge(s["mt_copied"], 5 * i + 5)
                    for h4 in range(4):
                        for cc, C in CH:
                            last = pe.matmul(ps[C, B + 2, h4 * 64:(h4 + 1) * 64], b.MT[C, h4], b.LKV[C, h4],
                                             start=True, stop=True)
                    last.then_inc(s["p1_done"], 1)
                    for par, jj in HEADS:
                        col = (2 * jj + par) * 64
                        for cc, C in CH:
                            last = pe.matmul(ps[half_of(par), B + cc, jj * 64:(jj + 1) * 64],
                                             b.tm[C, 0, col:col + 64], b.MT[C, slot(par, jj)], start=True, stop=True)
                    last.then_inc(s["w1_done"], 1)
                    yield
                    pe.wait_ge(s["p1_copied"], i + 1)
                    pe.wait_ge(s["w1_copied"], i + 1)
                    if i == 0:
                        pe.wait_ge(s["state_cleared"], 1)
                    for q, cc in enumerate(order):
                        C = half_of(cc)
                        if 2 * i + q:
                            pe.wait_ge(s["state_ready"], 2 * i + q)
                        for jj in (0, 1):
                            for par in (0, 1):
                                last = pe.matmul(ps[C, B + 2 + par, jj * 64:(jj + 1) * 64], b.W1[half_of(par), cc, jj],
                                                 b.S[half_of(par), jj], start=True, stop=True)
                        last.then_inc(s["u_done"], 1)
                        if emit:
                            for jj in (0, 1):
                                for par in (0, 1):
                                    pe.matmul(ps[C, B + par, jj * 64:(jj + 1) * 64], b.ar[half_of(par), jj, 1, C],
                                              b.S[half_of(par), jj], start=True, stop=True)
                        yield
                        pe.wait_ge(s["u_ready"], 2 * i + q + 1)
                        for par, jj in HEADS:
                            col, h = (2 * jj + par) * 64, 4 * g + 2 * jj + par
                            out = ps[half_of(par), B + 3, 128 + jj * 64:128 + (jj + 1) * 64]
                            pe.matmul(out, b.tm[C, 1, col:col + 64], b.U[C, slot(par, jj)], start=True, stop=False)
                            last = pe.matmul(out, b.tm[C, 2, col:col + 64], vrow[C, t, h * 64:(h + 1) * 64],
                                             start=False, stop=True)
                        last.then_inc(s["s_done"], 1)
                        yield
                    if emit:
                        for par, jj in HEADS:
                            h = 4 * g + 2 * jj + par
                            for cc, C in CH:
                                out = ps[C, B + 2, slot(par, jj) * 64:(slot(par, jj) + 1) * 64]
                                pe.matmul(out, b.LL[C, par, 0, jj, 1, :], b.U[C, slot(par, jj)], start=True, stop=False)
                                pe.matmul(out, b.LL[C, par, 1, jj, 1, :], vrow[C, t, h * 64:(h + 1) * 64],
                                          start=False, stop=True)
                        for jj in (0, 1):
                            last = pe.matmul(ps[:, B + 2, 256:260], b.rk[:, jj], rks[:, 2 * g + jj, 4 * g:4 * g + 4],
                                             start=(jj == 0), stop=(jj == 1))
                        last.then_inc(s["y_done"], 1)
                    yield

            take_turns(stream(0), stream(1), LAG)

        @block.scalar
        def _(act):
            def stream(g):
                b, s = streams[g], sem[g]
                B = 4 * g
                for i, t in enumerate(tiles):
                    act.wait_ge(s["lora_done"], i + 1)
                    for kind, dst in ((0, b.lw), (1, b.rate)):
                        for jj in (0, 1):
                            k = 8 * kind + 4 * d + 2 * g + jj
                            last = act.activation(dst[:, jj], ps[:, B, (2 * kind + jj) * P:(2 * kind + jj + 1) * P],
                                                  ACT.Tanh, scale=0.5, bias=half[:, k:k + 1])
                    last.then_inc(s["tanh_done"], 1)
                    yield
                    act.wait_ge(s["logs_ready"], i + 1)
                    after = b.F if d == 0 else b.e1
                    act.activation(b.e3[:], after[:], ACT.Exp, scale=-1.0)
                    act.activation(b.e1[:], after[:], ACT.Exp)
                    act.activation(b.e2[:], b.e2[:], ACT.Exp)
                    act.activation(b.ge[:], halves(b.F)[:, :, 63], ACT.Exp).then_inc(s["exps_ready"], 1)
                    yield
                    yield
                    act.wait_ge(s["abk_turned"], i + 1)
                    act.activation(b.tm[:, 0:2].rearrange("p a b -> p (a b)"), ps[:, B + 3, :], ACT.Copy)
                    act.activation(b.tm[:, 2], ps[:, B, 0:256], ACT.Copy).then_inc(s["abk_copied"], 1)
                    act.wait_ge(s["lkv_done"], i + 1)
                    act.activation(flat(b.LKV), ps[:, B + 2, 0:256], ACT.Copy).then_inc(s["lkv_copied"], 1)
                    yield

                    def copy_inverse(n):
                        act.wait_ge(s["mt_turned"], n)
                        act.activation(flat(b.MT), ps[:, B + 3, 0:256], ACT.Copy).then_inc(s["mt_copied"], 1)

                    for level in range(5):
                        if level:
                            copy_inverse(5 * i + level)
                        yield
                        yield
                    copy_inverse(5 * i + 5)
                    yield
                    act.wait_ge(s["p1_done"], i + 1)
                    act.activation(flat(b.P1), ps[:, B + 2, 0:256], ACT.Copy).then_inc(s["p1_copied"], 1)
                    act.wait_ge(s["w1_done"], i + 1)
                    act.activation(b.W1[:].rearrange("p a j n -> p a (j n)"), ps[:, B:B + 2, 0:128], ACT.Copy)\
                       .then_inc(s["w1_copied"], 1)
                    for _ in range(6):
                        yield

            take_turns(stream(0), stream(1), LAG)

        @block.gpsimd
        def _(pool):
            def stream(g):
                b, s = streams[g], sem[g]
                pool.memset(b.S[:], 0.0).then_inc(s["state_cleared"], 1)
                for i, t in enumerate(tiles):
                    yield
                    yield
                    pool.wait_ge(s["scaled"], i + 1)
                    pool.tensor_tensor(halves(b.bb), halves(b.bt), end(b.ge[:]), ALU.mult)
                    pool.tensor_tensor(halves(b.kb), halves(b.kt), end(b.ge[:]), ALU.mult)
                    pool.tensor_tensor(b.rk[:], r_[:, 2 * g:2 * g + 2, tok(t)], b.kd[:], ALU.mult)\
                        .then_inc(s["ends_scaled"], 1)
                    for _ in range(PHASES - 2):
                        yield

            take_turns(stream(0), stream(1), LAG)

        @block.vector
        def _(dve):
            step = Step(dve, dve_step)

            def stream(g):
                b, s = streams[g], sem[g]
                B = 4 * g
                pair = slice(2 * g, 2 * g + 2)
                wide = lambda a: a.unsqueeze(1).to_broadcast([P, 4, a.shape[-1]])
                for i, t in enumerate(tiles):
                    emit = t >= 2
                    kkt, rt, kts = kk[:, pair, tok(t)], r_[:, pair, tok(t)], k_[:, pair, tok(t)]
                    dve.wait_ge(s["tanh_done"], i + 1)
                    step(dve.tensor_scalar(b.lw[:], b.lw[:], -DEC / 2, -DEC / 2, ALU.mult, ALU.add),
                         dve.tensor_scalar(b.rate[:], b.rate[:], 0.5, 0.5, ALU.mult, ALU.add))
                    step(dve.tensor_tensor_scan(flat(b.F), keep[:, 0:256], flat(b.lw), 0.0, ALU.mult, ALU.add))
                    total = end(halves(b.F)[:, :, 63])
                    if d == 0:
                        dve.tensor_tensor(b.e2[:], b.F[:], b.lw[:], ALU.subtract).then_inc(s["logs_ready"], 1)
                    else:
                        step(dve.tensor_tensor(halves(b.e2), total, halves(b.F), ALU.subtract))
                        dve.tensor_tensor(b.e1[:], b.e2[:], b.lw[:], ALU.add).then_inc(s["logs_ready"], 1)
                    yield
                    if i >= 1:
                        dve.wait_ge(s["ends_scaled"], i)
                    step(*[dve.tensor_scalar(b.kd[:, jj], b.rate[:, jj], ka[:, 0, 2 * g + jj:2 * g + jj + 1],
                                             ka[:, 1, 2 * g + jj:2 * g + jj + 1], ALU.mult, ALU.add)
                           for jj in (0, 1)], dve.tensor_tensor(b.bt[:], kkt, b.rate[:], ALU.mult))
                    step(dve.tensor_tensor(b.kd[:], b.kd[:], kts, ALU.mult))
                    dve.wait_ge(s["exps_ready"], i + 1)
                    step(dve.scalar_tensor_tensor(b.ar[:, :, 0, :], kkt, -1.0, b.e2[:], ALU.mult, ALU.mult),
                         dve.tensor_tensor(b.ar[:, :, 1, :], rt, b.e1[:], ALU.mult),
                         dve.tensor_tensor(b.bt[:], b.bt[:], b.e3[:], ALU.mult))
                    dve.tensor_tensor(b.kt[:], b.kd[:], b.e3[:], ALU.mult).then_inc(s["scaled"], 1)
                    yield
                    dve.wait_ge(s["pairs_done"], i + 1)
                    dve.tensor_tensor(b.LL[:].rearrange("p a b j r n -> p (a b j) (r n)"),
                                      ps[:, B + 1:B + 3, :].rearrange("p a (b n) -> p (a b) n", n=P),
                                      mk[:].rearrange("p a t -> p (a t)").unsqueeze(1).to_broadcast([P, 8, P]),
                                      ALU.mult).then_inc(s["pairs_masked"], 1)
                    dve.wait_ge(s["pairs_masked"], i + 1)
                    step(*[dve.tensor_tensor(b.MT[:, 2 * par:2 * par + 2], b.LL[:, par, 0, :, 0, :],
                                             m1T[:].unsqueeze(1).to_broadcast([P, 2, 64]), ALU.mult)
                           for par in (0, 1)])
                    dve.tensor_tensor(b.MT[:], b.MT[:], wide(eye[:]), ALU.add).then_inc(s["mt_started"], 1)
                    yield
                    dve.wait_ge(s["l_turned"], i + 1)
                    step(dve.tensor_tensor(b.M[:], ps[:, B + 1, 0:256].rearrange("p (h n) -> p h n", h=4),
                                           wide(m1[:]), ALU.mult))
                    dve.tensor_tensor(b.M[:], b.M[:], wide(eye[:]), ALU.add).then_inc(s["m_ready"], 1)
                    yield
                    for level in range(5):
                        n = 5 * i + level
                        dve.wait_ge(s["x_done"], n + 1)
                        dve.tensor_tensor(b.X[:], ps[:, B + 1, 0:128].rearrange("p (h n) -> p h n", h=4),
                                          wide(lm[:, level]), ALU.mult).then_inc(s["x_masked"], 1)
                        yield
                        dve.wait_ge(s["m_done"], n + 1)
                        dve.wait_ge(s["m_ready"], n + i + 1)
                        target = first_blocks(b.M[:], level)
                        dve.tensor_tensor(target, target, ps[:, B + 2, 0:128]
                                          .rearrange("p (h g n) -> p h g n", h=4, n=2 << level), ALU.add)\
                           .then_inc(s["m_ready"], 1)
                        yield
                    yield
                    dve.wait_ge(s["p1_copied"], i + 1)
                    yield
                    for q, cc in enumerate(order):
                        C = half_of(cc)
                        ends = b.ge[:].rearrange("p (j q) -> p j q", q=2)[:, :, cc].unsqueeze(2)\
                                .to_broadcast([P, 2, 64])
                        if i == 0 and q == 0:
                            dve.wait_ge(s["state_cleared"], 1)
                        step(dve.tensor_tensor(b.SG[:], b.S[:], ends, ALU.mult))
                        dve.wait_ge(s["u_done"], 2 * i + q + 1)
                        dve.tensor_tensor(b.U[C].rearrange("p (a h) n -> p a (h n)", a=2), ps[C, B + 2:B + 4, 0:128],
                                          b.P1[C].rearrange("p (a h) n -> p a (h n)", a=2), ALU.add)\
                           .then_inc(s["u_ready"], 1)
                        yield
                        dve.wait_ge(s["s_done"], 2 * i + q + 1)
                        dve.tensor_tensor(b.S[:], ps[:, B + 3, 128:256].rearrange("p (j n) -> p j n", j=2), b.SG[:],
                                          ALU.add).then_inc(s["state_ready"], 1)
                        dve.wait_ge(s["state_ready"], 2 * i + q + 1)
                        yield
                    if emit:
                        row = t - 2
                        out = y[:, row, 256 * g:256 * g + 256].rearrange("p (j a e) -> p a j e", a=2, e=64)
                        from_state = ps[:, B:B + 2, 0:128].rearrange("p a (j e) -> p a j e", e=64)
                        inside = ps[:, B + 2, 0:256].rearrange("p (a j e) -> p a j e", a=2, e=64)
                        bonus = sc[:, row, 4 * g:4 * g + 4]
                        dve.wait_ge(s["y_done"], sum(1 for x in tiles[:i + 1] if x >= 2))
                        if d == 0:
                            step(dve.tensor_copy(out, from_state),
                                 dve.tensor_tensor(bonus, bonus, ps[:, B + 2, 256:260], ALU.add))
                        else:
                            step(dve.tensor_tensor(out, out, from_state, ALU.add),
                                 dve.tensor_tensor(bonus, bonus, ps[:, B + 2, 256:260], ALU.add))
                        dve.tensor_tensor(out, out, inside, ALU.add).then_inc(s["tile_done"], 1)
                        dve.wait_ge(s["tile_done"], i + 1)
                    else:
                        dve.nop().then_inc(s["tile_done"], 1)
                    yield

            take_turns(stream(0), stream(1), LAG)



def rope_tables():
    pos = np.arange(S, dtype=np.float32)
    inv = lambda theta, r: np.power(np.float32(theta), (-np.arange(r // 2, dtype=np.float32) * np.float32(2.0 / r)))
    angles = [pos[:, None] * inv(5e5, 16)[None], pos[:, None] * inv(5e5, 32)[None],
              (pos // 64)[:, None] * inv(1e4, 32)[None], (pos % 64)[:, None] * inv(1e4, 32)[None]]
    a = np.concatenate(angles, axis=1).astype(np.float32)
    return np.cos(a).astype(np.float32), np.sin(a).astype(np.float32)


def even_bias():
    dist = np.arange(1920)[None, :] - 896 - np.arange(P)[:, None]
    held = sum(((dist % dil == 0) & (abs(dist) <= win // 2)).astype(np.int64) for win, dil in
               ((128, 1), (512, 4), (2048, 16)))
    return np.where(held > 0, np.log(np.maximum(held, 1)) * HD ** 0.5, NEG).astype(np.float32)


def window_bias():
    q, k = np.arange(P)[:, None], np.arange(P)[None, :]
    before, after = np.where(k >= q, 0, NEG), np.where(k <= q, 0, NEG)
    opened = np.zeros((P, P))
    ctx = np.zeros((P, CTX))
    kinds = [np.concatenate([ctx, before, opened, after], 1), np.concatenate([ctx, opened, after, opened], 1)]
    return np.stack(kinds, 1).astype(np.float32)


def scan_masks():
    out = np.zeros((2, P, 416), np.float32)
    a, b = np.arange(P)[:, None] % CHUNK, np.arange(CHUNK)[None, :]
    out[0, :, 0:64], out[0, :, 64:128] = a < b, a <= b
    out[1, :, 0:64], out[1, :, 64:128] = a > b, a >= b
    out[0, :, 128:192] = (a % 2 == 1) & (b == a - 1)
    out[1, :, 128:192] = (a % 2 == 0) & (b == a + 1)
    out[0, :, 192:256] = (b % 2 == 1) & (a == b - 1)
    out[1, :, 192:256] = (b % 2 == 0) & (a == b + 1)
    col = np.arange(32)
    for level in range(5):
        n = 2 << level
        for d in range(2):
            block = 2 * (col // n) + d
            out[d, :, 256 + 32 * level:288 + 32 * level] = a // n == (block + (1 if d == 0 else -1))[None, :]
    return out


def constants():
    cos, sin = rope_tables()
    starts = np.ones((P, 512), np.float32)
    starts[:, ::CHUNK] = 0
    half = np.arange(P) // 64
    return {"const_rope_cos": cos, "const_rope_sin": sin, "const_even_bias": even_bias(),
            "const_window_bias": window_bias(), "const_scan_masks": scan_masks(), "const_chunk_starts": starts,
            "const_head_blocks": (half[:, None] == half[None, :]).astype(np.float32),
            "const_chunk_identity": np.tile(np.eye(CHUNK, dtype=np.float32), (2, 1)),
            "const_identity": np.eye(P, dtype=np.float32)}


def build(nc, dram, out):
    c = Chip(nc, dram)
    result_stored = nc.alloc_semaphore("result_stored")
    c.ident = c.at("identity", 0, [P, P])
    c.eps = c.at("eps", 0.5, [P, 1])
    c.idle = c.at("idle_operand", 0.53125, [P, 64], BF16)
    c.rope_cos = c.at("rope_cos", 0.75, [P, TILES, 56])
    c.rope_sin = c.at("rope_sin", 2.5, [P, TILES, 56])
    x = c.at("x", 6, [P, TILES, D])
    with stage(nc, "eps_set") as (block, eps_set):
        @block.gpsimd
        def _(pool):
            pool.memset(c.eps[:], EPS).then_inc(eps_set, 1)
            pool.memset(c.idle[:], 0.0).then_inc(eps_set, 1)
            pool.wait_ge(eps_set, 2)
    load(c, [(c.ident[:], dram["const_identity"]), (x[:], dram["x"][0].rearrange("(t p) d -> p t d", p=P)),
             (c.rope_cos[:], dram["const_rope_cos"].rearrange("(t p) d -> p t d", p=P)),
             (c.rope_sin[:], dram["const_rope_sin"].rearrange("(t p) d -> p t d", p=P))])
    condition(c)
    even_mixer(c, x, dram["even_w_in"][0])
    experts(c, x, 0)
    odd_mixer(c, x)
    experts(c, x, 1)
    norm_rows(c, x, x, TILES, dram["final_norm"], 102)
    second_block(c, x)
    rows = c.at("result_rows", 38, [P, TILES, D])
    norm_rows(c, x, rows, TILES, dram["norm_f_g_2"], 102,
              result=(out[0].rearrange("(t p) d -> p t d", p=P), result_stored))


def kernel(**inputs):
    import concourse.bacc as bacc
    from concourse.bass_utils import run_bass_kernel_spmd

    nc = bacc.Bacc("TRN2", target_bir_lowering=False, num_devices=1)
    arrays, dram = {}, {}
    for name, a in {**inputs, **constants()}.items():
        a = np.ascontiguousarray(a)
        arrays["in_" + name] = a
        dram[name] = nc.dram_tensor("in_" + name, a.shape, F32, kind="ExternalInput").ap()
    for name in ("h_scratch", "x_scratch", "g_scratch"):
        dram[name] = nc.dram_tensor(name, (S, D), F32).ap()
    out = nc.dram_tensor("out", (1, S, D), F32, kind="ExternalOutput").ap()
    build(nc, dram, out)
    return run_bass_kernel_spmd(nc, [arrays], core_ids=[0]).results[0]["out"]
```
